# Optimizing a Trainium2 kernel written in Bass

```python
import math
import jax, jax.numpy as jnp
from jax import lax
import numpy as np

D_MODEL = 2048
BATCH = 1
SEQ = 256
DEPTH = 1
DEC_BATCH = 8
DEC_SEQ = 1
PAST_LEN = 2048
PAGE_SIZE = 128

D_CONV = D_MODEL // 2
CONV_W = 3
N_HEADS = 8
DK = D_MODEL // 32
DV = 2 * DK
QK_W = N_HEADS * 2 * DK
V_W = N_HEADS * DV
ROT_DIM = DK // 4
ROPE_THETA = 500000.0
N_MEM = 256
MEM_HEADS = 4
MEM_HD = D_MODEL // 8
CROSS_W = MEM_HEADS * MEM_HD
N_BRANCH = 3
N_KEYS = 128
N_EXPERTS = N_KEYS * N_KEYS
PEER_HEADS = 8
PEER_TOPK = 16
D_KEY = 256
Q_BLOCK = 128
PEER_BLOCK = 128
EPS = 1e-6
NEG_INF = -1e30
IN_WIDTHS = (D_CONV, D_CONV, D_CONV, QK_W, QK_W, V_W, CROSS_W, N_BRANCH * D_MODEL)
IN_COLS = sum(IN_WIDTHS)
SPLIT_POINTS = tuple(int(s) for s in np.cumsum(IN_WIDTHS)[:-1])

kernel_name = "hybrid_conv_diffattn_mem_peer_step"

def rms_norm(x, w):
    xf = x.astype(jnp.float32)
    y = xf * lax.rsqrt(jnp.mean(xf * xf, axis=-1, keepdims=True) + EPS)
    return (y * w.astype(jnp.float32)).astype(x.dtype)

def partial_rope(x, pos):
    half = ROT_DIM // 2
    inv_freq = ROPE_THETA ** (-jnp.arange(half, dtype=jnp.float32) / half)
    ang = pos.astype(jnp.float32)[:, None] * inv_freq[None, :]
    cos = jnp.cos(ang)[None, :, None, None, :]
    sin = jnp.sin(ang)[None, :, None, None, :]
    xf = x.astype(jnp.float32)
    x1 = xf[..., :half]
    x2 = xf[..., half:ROT_DIM]
    out = jnp.concatenate([x1 * cos - x2 * sin, x2 * cos + x1 * sin, xf[..., ROT_DIM:]], axis=-1)
    return out.astype(x.dtype)

def short_conv(u, buf, conv_w):
    T = u.shape[1]
    ext = jnp.concatenate([buf, u], axis=1)
    y = conv_w[0] * ext[:, 0:T] + conv_w[1] * ext[:, 1:T + 1] + conv_w[2] * ext[:, 2:T + 2]
    return y, ext[:, -(CONV_W - 1):]

def diff_attn(q, k, v, q_pos, k_pos, lam):
    s = jnp.einsum('bqhcd,bkhcd->bhcqk', q, k).astype(jnp.float32) * (DK ** -0.5)
    mask = k_pos[None, :] <= q_pos[:, None]
    s = jnp.where(mask, s, NEG_INF)
    p = jax.nn.softmax(s, axis=-1)
    a = p[:, :, 0] - lam * p[:, :, 1]
    return jnp.einsum('bhqk,bkhd->bqhd', a.astype(v.dtype), v)

def memory_kv(mem, mem_norm_w, w_mem_kv, mk_norm_w):
    B = mem.shape[0]
    kv = rms_norm(mem, mem_norm_w) @ w_mem_kv
    mk, mv = jnp.split(kv, 2, axis=-1)
    mk = rms_norm(mk.reshape(B, N_MEM, MEM_HEADS, MEM_HD), mk_norm_w)
    mv = mv.reshape(B, N_MEM, MEM_HEADS, MEM_HD)
    return mk, mv

def mem_attn(q, mk, mv):
    s = jnp.einsum('bqhd,bmhd->bhqm', q, mk).astype(jnp.float32) * (MEM_HD ** -0.5)
    p = jax.nn.softmax(s, axis=-1)
    return jnp.einsum('bhqm,bmhd->bqhd', p.astype(mv.dtype), mv)

def token_mixer(x, pos, conv_buf, k_past, v_past, mem_k, mem_v, lam, lam_init,
                norm1_w, w_in, conv_w, q_norm_w, k_norm_w, subln_w, mq_norm_w,
                w_conv_out, w_diff_out, w_cross_out, w_o):
    B, T, _ = x.shape
    h = rms_norm(x, norm1_w)
    z = h @ w_in
    zb, zc, zx, zq, zk, zv, zmq, zg = jnp.split(z, SPLIT_POINTS, axis=-1)
    y_c, new_buf = short_conv(zc * zx, conv_buf, conv_w)
    y_conv = (zb * y_c) @ w_conv_out
    q = partial_rope(rms_norm(zq.reshape(B, T, N_HEADS, 2, DK), q_norm_w), pos)
    k = partial_rope(rms_norm(zk.reshape(B, T, N_HEADS, 2, DK), k_norm_w), pos)
    v = zv.reshape(B, T, N_HEADS, DV)
    if k_past is None:
        nb = T // Q_BLOCK
        q_blocks = jnp.moveaxis(q.reshape(B, nb, Q_BLOCK, N_HEADS, 2, DK), 1, 0)
        pos_blocks = pos.reshape(nb, Q_BLOCK)
        o = lax.map(lambda qp: diff_attn(qp[0], k, v, qp[1], pos, lam), (q_blocks, pos_blocks))
        o = jnp.moveaxis(o, 0, 1).reshape(B, T, N_HEADS, DV)
    else:
        k_all = jnp.concatenate([k_past, k], axis=1)
        v_all = jnp.concatenate([v_past, v], axis=1)
        k_pos = jnp.arange(k_all.shape[1], dtype=jnp.int32)
        o = diff_attn(q, k_all, v_all, pos, k_pos, lam)
    o = rms_norm(o, subln_w) * (1.0 - lam_init)
    y_diff = o.reshape(B, T, V_W) @ w_diff_out
    qm = rms_norm(zmq.reshape(B, T, MEM_HEADS, MEM_HD), mq_norm_w)
    y_mem = mem_attn(qm, mem_k, mem_v).reshape(B, T, CROSS_W) @ w_cross_out
    g = jax.nn.sigmoid(zg.reshape(B, T, N_BRANCH, D_MODEL))
    merged = g[:, :, 0] * y_conv + g[:, :, 1] * y_diff + g[:, :, 2] * y_mem
    x = x + merged @ w_o
    return x, k.reshape(B, T, N_HEADS, 2 * DK), v, new_buf

def peer_ffn(h, w_peer_q, sub_keys, peer_u, peer_v):
    B, T, D = h.shape
    n = B * T
    hf = h.reshape(n, D)
    q = (hf @ w_peer_q).reshape(n, PEER_HEADS, 2, D_KEY // 2)
    s1 = jnp.einsum('nhd,kd->nhk', q[:, :, 0], sub_keys[0]).astype(jnp.float32)
    s2 = jnp.einsum('nhd,kd->nhk', q[:, :, 1], sub_keys[1]).astype(jnp.float32)
    v1, i1 = lax.top_k(s1, PEER_TOPK)
    v2, i2 = lax.top_k(s2, PEER_TOPK)
    cand_s = (v1[..., :, None] + v2[..., None, :]).reshape(n, PEER_HEADS, PEER_TOPK * PEER_TOPK)
    cand_i = (i1[..., :, None] * N_KEYS + i2[..., None, :]).reshape(n, PEER_HEADS, PEER_TOPK * PEER_TOPK)
    top_s, top_pos = lax.top_k(cand_s, PEER_TOPK)
    idx = jnp.take_along_axis(cand_i, top_pos, axis=-1)
    gate = jax.nn.softmax(top_s, axis=-1).astype(h.dtype)
    blk = min(PEER_BLOCK, n)
    n_pad = -(-n // blk) * blk
    pad = n_pad - n
    hp = jnp.pad(hf, ((0, pad), (0, 0))).reshape(-1, blk, D)
    ip = jnp.pad(idx, ((0, pad), (0, 0), (0, 0))).reshape(-1, blk, PEER_HEADS, PEER_TOPK)
    gp = jnp.pad(gate, ((0, pad), (0, 0), (0, 0))).reshape(-1, blk, PEER_HEADS, PEER_TOPK)

    def expert_block(args):
        hb, ib, gb = args
        u = jnp.take(peer_u, ib, axis=0)
        a = jnp.einsum('nhkd,nd->nhk', u, hb)
        w = gb * jax.nn.gelu(a, approximate=False)
        vv = jnp.take(peer_v, ib, axis=0)
        return jnp.einsum('nhk,nhkd->nd', w, vv)

    out = lax.map(expert_block, (hp, ip, gp))
    return out.reshape(n_pad, D)[:n].reshape(B, T, D)

def setup_inputs(seed: int = 0) -> dict:
    key = jax.random.key(seed)
    ks = jax.random.split(key, 40)
    f32 = jnp.float32

    def nrm(i, shape, scale):
        return jax.random.normal(ks[i], shape, f32) * scale

    def gain(i, dim):
        return 1.0 + 0.02 * jax.random.normal(ks[i], (DEPTH, dim), f32)

    n_pages = PAST_LEN // PAGE_SIZE
    n_used = DEC_BATCH * n_pages
    n_pool = n_used + (n_used + 3) // 4
    page_table = jax.random.permutation(ks[0], n_pool)[:n_used].reshape(DEC_BATCH, n_pages).astype(jnp.int32)
    return {
        "x_prompt": nrm(1, (BATCH, SEQ, D_MODEL), 1.0),
        "x_sample": nrm(2, (DEC_BATCH, DEC_SEQ, D_MODEL), 1.0),
        "mem_prompt": nrm(3, (BATCH, N_MEM, D_MODEL), 1.0),
        "cache_k": nrm(4, (DEPTH, n_pool, PAGE_SIZE, N_HEADS, 2 * DK), 1.0),
        "cache_v": nrm(5, (DEPTH, n_pool, PAGE_SIZE, N_HEADS, DV), 1.0),
        "page_table": page_table,
        "state_conv": nrm(6, (DEPTH, DEC_BATCH, CONV_W - 1, D_CONV), 1.0),
        "cache_mem_k": nrm(7, (DEPTH, DEC_BATCH, N_MEM, MEM_HEADS, MEM_HD), 1.0),
        "cache_mem_v": nrm(8, (DEPTH, DEC_BATCH, N_MEM, MEM_HEADS, MEM_HD), 1.0),
        "norm1_w": gain(9, D_MODEL),
        "w_in": nrm(10, (DEPTH, D_MODEL, IN_COLS), D_MODEL ** -0.5),
        "conv_w": nrm(11, (DEPTH, CONV_W, D_CONV), CONV_W ** -0.5),
        "q_norm_w": gain(12, DK),
        "k_norm_w": gain(13, DK),
        "lambda_q1": nrm(14, (DEPTH, DK), 0.1),
        "lambda_k1": nrm(15, (DEPTH, DK), 0.1),
        "lambda_q2": nrm(16, (DEPTH, DK), 0.1),
        "lambda_k2": nrm(17, (DEPTH, DK), 0.1),
        "subln_w": gain(18, DV),
        "mem_norm_w": gain(19, D_MODEL),
        "w_mem_kv": nrm(20, (DEPTH, D_MODEL, 2 * CROSS_W), D_MODEL ** -0.5),
        "mq_norm_w": gain(21, MEM_HD),
        "mk_norm_w": gain(22, MEM_HD),
        "w_conv_out": nrm(23, (DEPTH, D_CONV, D_MODEL), D_CONV ** -0.5),
        "w_diff_out": nrm(24, (DEPTH, V_W, D_MODEL), V_W ** -0.5),
        "w_cross_out": nrm(25, (DEPTH, CROSS_W, D_MODEL), CROSS_W ** -0.5),
        "w_o": nrm(26, (DEPTH, D_MODEL, D_MODEL), D_MODEL ** -0.5),
        "norm2_w": gain(27, D_MODEL),
        "w_peer_q": nrm(28, (DEPTH, D_MODEL, PEER_HEADS * D_KEY), D_MODEL ** -0.5),
        "sub_keys": nrm(29, (DEPTH, 2, N_KEYS, D_KEY // 2), (D_KEY // 2) ** -0.5),
        "peer_u": nrm(30, (DEPTH, N_EXPERTS, D_MODEL), D_MODEL ** -0.5),
        "peer_v": nrm(31, (DEPTH, N_EXPERTS, D_MODEL), PEER_HEADS ** -0.5),
    }

def reference(x_prompt, x_sample, mem_prompt, cache_k, cache_v, page_table, state_conv,
              cache_mem_k, cache_mem_v, norm1_w, w_in, conv_w, q_norm_w, k_norm_w,
              lambda_q1, lambda_k1, lambda_q2, lambda_k2, subln_w, mem_norm_w, w_mem_kv,
              mq_norm_w, mk_norm_w, w_conv_out, w_diff_out, w_cross_out, w_o, norm2_w,
              w_peer_q, sub_keys, peer_u, peer_v):
    B, T = x_prompt.shape[:2]
    DB, TS = x_sample.shape[:2]
    pos_p = jnp.arange(T, dtype=jnp.int32)
    pos_s = PAST_LEN + jnp.arange(TS, dtype=jnp.int32)
    xp, xs = x_prompt, x_sample
    kp_l, vp_l, cp_l, mkp_l, mvp_l, ks_l, vs_l, cs_l = [], [], [], [], [], [], [], []
    for l in range(DEPTH):
        lam_init = 0.8 - 0.6 * math.exp(-0.3 * l)
        lam = (jnp.exp(jnp.sum(lambda_q1[l].astype(jnp.float32) * lambda_k1[l].astype(jnp.float32)))
               - jnp.exp(jnp.sum(lambda_q2[l].astype(jnp.float32) * lambda_k2[l].astype(jnp.float32)))
               + lam_init)
        layer_w = (norm1_w[l], w_in[l], conv_w[l], q_norm_w[l], k_norm_w[l], subln_w[l], mq_norm_w[l],
                   w_conv_out[l], w_diff_out[l], w_cross_out[l], w_o[l])
        mk_p, mv_p = memory_kv(mem_prompt, mem_norm_w[l], w_mem_kv[l], mk_norm_w[l])
        zero_buf = jnp.zeros((B, CONV_W - 1, D_CONV), dtype=xp.dtype)
        xp, kp, vp, cp = token_mixer(xp, pos_p, zero_buf, None, None, mk_p, mv_p, lam, lam_init, *layer_w)
        xp = xp + peer_ffn(rms_norm(xp, norm2_w[l]), w_peer_q[l], sub_keys[l], peer_u[l], peer_v[l])
        k_past = cache_k[l][page_table].reshape(DB, -1, N_HEADS, 2, DK)
        v_past = cache_v[l][page_table].reshape(DB, -1, N_HEADS, DV)
        xs, ks, vs, cs = token_mixer(xs, pos_s, state_conv[l], k_past, v_past, cache_mem_k[l], cache_mem_v[l],
                                     lam, lam_init, *layer_w)
        xs = xs + peer_ffn(rms_norm(xs, norm2_w[l]), w_peer_q[l], sub_keys[l], peer_u[l], peer_v[l])
        kp_l.append(kp); vp_l.append(vp); cp_l.append(cp); mkp_l.append(mk_p); mvp_l.append(mv_p)
        ks_l.append(ks); vs_l.append(vs); cs_l.append(cs)
    return (xp, xs, jnp.stack(kp_l), jnp.stack(vp_l), jnp.stack(cp_l), jnp.stack(mkp_l), jnp.stack(mvp_l),
            jnp.stack(ks_l), jnp.stack(vs_l), jnp.stack(cs_l))


_drawn_inputs = setup_inputs


def setup_inputs(seed=0):
    import zlib

    import numpy as np

    out = dict(_drawn_inputs(seed))
    spreads = {}
    factors = {'q_norm_w': 3.857,
     'k_norm_w': 2.817,
     'lambda_q1': 5.522,
     'subln_w': 12.157,
     'mem_norm_w': 2.904,
     'mq_norm_w': 8.0,
     'mk_norm_w': 3.157,
     'norm2_w': 4.961}
    for name, (base, spread) in spreads.items():
        noise = np.random.default_rng([zlib.crc32(name.encode()), seed]).standard_normal(out[name].shape)
        drawn = base * np.exp(spread * noise) if base else spread * noise
        out[name] = __import__('jax').numpy.asarray(drawn.astype(out[name].dtype))
    for name, factor in factors.items():
        out[name] = (out[name] * factor).astype(out[name].dtype)
    return out
```

```python
from contextlib import ExitStack, contextmanager

import numpy as np

import concourse.bass as bass
from concourse import mybir

F32 = mybir.dt.float32
I32 = mybir.dt.int32
U32 = mybir.dt.uint32
ALU = mybir.AluOpType
ACT = mybir.ActivationFunctionType
X = mybir.AxisListType.X
ds = bass.ds

P = 128
D = 2048
KC = D // P
TP, TS = 256, 8
NT = TP + TS
DC = D // 2
BC = DC // P
HEADS, DK, DV = 8, 64, 128
MH, MD, NM = 4, 256, 256
PAGES, PAGE = 16, 128
POOL_PAGES = 160
NKEY, PH, TOPK = 128, 8, 16
EPS = 1e-6
NEG = -1e30
LAM_INIT = 0.2
BLK = 256
NR = 2
TILES = [(0, P), (P, P), (TP, TS)]


class Steps:

    def __init__(self, eng, sem):
        self.eng, self.sem, self.base, self.k = eng, sem, 0, 0

    def run(self, ins):
        ins.then_inc(self.sem, 1)
        self.k += 1

    def settle(self):
        self.eng.wait_ge(self.sem, self.base + self.k)

    def __call__(self, ins):
        self.run(ins)
        self.settle()

    @contextmanager
    def loop(self, n, per):
        base, k = self.base, self.k
        with self.eng.Fori(0, n) as i:
            self.base, self.k = base + (i * per + k), 0
            yield i
            assert self.k == per, f"the body has {self.k} steps, not {per}"
        self.base, self.k = base, k + n * per


def build(nc, A, O):
    rope_tab = A["rope_tab"]
    w_in = A["w_in"][0].rearrange("(k p) n -> p k n", p=P)
    w_mem = A["w_mem_kv"][0].rearrange("(k p) n -> p k n", p=P)
    w_o = A["w_o"][0].rearrange("(k p) n -> p k n", p=P)
    w_pq = A["w_peer_q"][0].rearrange("(k p) n -> p k n", p=P)
    w_br = [A[n][0].rearrange("(k p) n -> p k n", p=P) for n in ("w_conv_out", "w_cross_out", "w_diff_out")]
    gate_col = [7 * 1024, 7 * 1024 + 2 * D, 7 * 1024 + D]
    cache_k = A["cache_k"][0].rearrange("n t h d -> (n t) (h d)")
    cache_v = A["cache_v"][0].rearrange("n t h d -> (n t) (h d)")
    cmem_k = A["cache_mem_k"][0].rearrange("b m h d -> (b m) (h d)")
    cmem_v = A["cache_mem_v"][0].rearrange("b m h d -> (b m) (h d)")
    peer_u, peer_v = A["peer_u"][0], A["peer_v"][0]
    q_dram = nc.dram_tensor("q_rows_scratch", [TS, DC], F32, kind="Internal").ap()
    mq_dram = nc.dram_tensor("mq_rows_scratch", [TS, DC], F32, kind="Internal").ap()
    h2_dram = nc.dram_tensor("h2_rows_scratch", [TS, D], F32, kind="Internal").ap()

    ctx = ExitStack()
    with ctx:
        def sb(name, shape, dt=F32):
            return ctx.enter_context(nc.sbuf_tensor("sb_" + name, shape, dt))

        def sem(name):
            return ctx.enter_context(nc.semaphore(name))

        ps = ctx.enter_context(nc.psum_tensor("ps", [P, 8, 512], F32))

        wring = sb("wring", [P, NR, KC, BLK])
        bregion = sb("bregion", [P, 4096])
        ring4 = sb("ring4", [P, 4, DC])
        hT = sb("hT", [P, KC, NT])
        conv = sb("conv", [P, 3 * BC, NT])
        rows = sb("rows", [P, 3, 4 * DC])
        mkv = sb("mkv", [P, 2, 2 * DC])
        S = sb("S", [P, TS, PAGES, 2 * HEADS])
        Ad = sb("Ad", [P, TS, PAGES, HEADS])
        oreg = sb("oreg", [P, 2 * BC, NT])
        memT = bregion[:, :].rearrange("p (k m) -> p k m", k=KC)
        bwring = bregion[:, :].rearrange("p (s k n) -> p s k n", s=NR, k=BC)
        merged = conv[:, BC:3 * BC, :]
        oT_mem, oT_diff = oreg[:, 0:BC, :], oreg[:, BC:2 * BC, :]
        oflat = oreg[:, :, :].rearrange("p a b -> p (a b)")
        qb = oflat[:, 0:2 * DC].rearrange("p (s n) -> p s n", s=2)
        prod = oflat[:, 2 * DC:3 * DC]
        cflat = conv[:, :, :].rearrange("p a b -> p (a b)")
        temp = [ring4[:, :, :].rearrange("p a b -> p (a b)"), cflat[:, BC * NT:3 * BC * NT]]
        x_rows, h2_rows = rows[:, :, 0:D], rows[:, :, D:2 * D]
        cs_rows = Ad[:, :, :, :].rearrange("p a b c -> p (a b c)")
        n2_w, sk_rows = mkv[:, 0, :], mkv[:, 1, 0:2 * P].rearrange("p (c d) -> p c d", c=2)
        skT = mkv[:, 1, 2 * P:4 * P].rearrange("p (c d) -> p c d", c=2)
        sq_mkv = mkv[:, :, :].rearrange("p a b -> p (a b)")
        scores = cflat[:, 0:3 * 2 * PH * NKEY].rearrange("p (t n) -> p t n", t=3)
        work = S[:, :, :, :].rearrange("p a b c -> p (a b c)")
        colrows, lam4 = work[0:56, 0:P], work[:, P:P + 4 * DK].rearrange("p (a n) -> p a n", a=4)
        mask = work[:, 0:2 * TP].rearrange("p (t n) -> p t n", t=2)
        sg = work[:, 1024:1024 + 2 * NT].rearrange("p (s n) -> p s n", s=2)
        rt = ring4[:, :, :].rearrange("p a b -> p (a b)")
        top_v, top_i = rt[:, 0:256], rt[:, 256:512].bitcast(U32)
        top_f = rt[:, 512:768]
        win_v, win_p = rt[:, 768:896], rt[:, 896:1024].bitcast(U32)
        part_i, part_f = rt[:, 1024:1152].bitcast(U32), rt[:, 1152:1408]
        pick = rt[:, 1408:1664]
        iota_i, iota_f = rt[:, 1664:1680].bitcast(I32), rt[:, 1680:1696]
        idx_f = rt[:, 1696:1824]
        idx_all = rt[:, 1824:2208].bitcast(I32).rearrange("p (t n) -> p t n", t=3)
        gates = rt[:, 2208:2592].rearrange("p (t n) -> p t n", t=3)
        uidx = rt[:, 2592:2624].bitcast(I32).rearrange("p (s n) -> p s n", s=2)
        sidx, sgate = rt[:, 2624:2632].bitcast(I32), rt[:, 2632:2640]
        act_a = rt[:, 2640:2672].rearrange("p (s n) -> p s n", s=2)
        act_g = rt[:, 2672:2704].rearrange("p (s n) -> p s n", s=2)
        wexp = rt[:, 2704:2736].rearrange("p (s n) -> p s n", s=2)
        wz = rt[:, 2736:2800].rearrange("p (b c) -> p b c", b=TS)
        denom = rt[:, 2800:2816]
        diag = rt[:, 3072:3584].rearrange("p (s n) -> p s n", s=4)
        zero512 = rt[:, 3584:4096]
        cand, hot = oflat[:, 0:2048], oflat[:, 2048:4096]
        u_slots = [wring[:, r].rearrange("p k n -> p (k n)")[:, h * D:(h + 1) * D] for r in range(NR) for h in range(2)]
        hflat = hT[:, :, :].rearrange("p k n -> p (k n)")
        e_slots = [bregion[:, 0:D], bregion[:, D:2 * D], hflat[:, 0:D], hflat[:, D:2 * D]]
        hb = [oflat[:, 0:D], oflat[:, D:2 * D]]
        v_slots = [rows[:, t, c * DC:(c + 1) * DC] for t in range(2) for c in range(2)]

        ident = sb("ident", [P, P])
        ones = sb("ones", [P, P])
        cols = sb("cols", [P, 56])
        stT = sb("stT", [P, BC, 2 * TS])
        qn_w, kn_w, sub_w = sb("qn_w", [P, DK]), sb("kn_w", [P, DK]), sb("sub_w", [P, 1])
        mq_w, mk_w = sb("mq_w", [P, MD]), sb("mk_w", [P, MD])
        rope = sb("rope", [P, 3, 16])
        lam = sb("lam", [P, 4])
        zst = sb("zst", [P, 2, NT])
        stat = sb("stat", [P, 64])
        pt = sb("pt", [1, TS * PAGES], I32)
        Sm = sb("Sm", [P, TS, 2, MH])
        small = sb("small", [P, 5, P])
        mask0 = zst[:, :, :].rearrange("p a b -> p (a b)")[:, 0:P]
        Ad_f, Sm_f = cs_rows, Sm[:, :, :, :].rearrange("p a b c -> p (a b c)")
        tmpm = small[:, 0:3, :].rearrange("p a b -> p (a b)")[:, 0:NT]

        names = """consts const_w x_in x_clear mem_in cols_in st_in small_in lam_in rope_in pt_in x_ss x_var x_sd x_scaled
            xT_full xT_taken cols_full cols_ready st_full chunk_full chunk_taken tr_full rows_taken
            q_ready qk_stored q_scratch kpage_used token_done kd_done conv_ready cs_full cs_rows conv_stored
            sqrt_in sqrt_out mk_ready mkv_stored self_full self_in max_full max_diag mb_full exp_in exp_out sum_in
            sum_full a_ready attn_staged tt_full qk_T s_full sm_ready exp_ready p_ready at_full at_ready o_full
            attn_done vpage_used vo_full vo_ready sub_in sub_full sub_scaled gate_full gate_done y_full y_taken
            merge_ready x_again x1_ready h2T_in h2_ready h2T_full h2T_taken h2_scratch sk_in sk_full sk_ready
            s_cleared gate_in gate_out idx_ready sT_full sT_in u_used a_in a_out w_ready diag_ready v_used yo_full
            y_ready y_stored hb_used zero_ready dve_done act_done pool_done mem_taken n2_in lam_pre lam_exp sqrt_pad x1_rows n2_ss h2T_x st_ready
            merge_zero sub_taken gather_turn loop_turn""".split()
        s = {n: sem(n) for n in names}
        w_landed = [sem(f"w_landed{i}") for i in range(NR)]
        bw_landed = [sem(f"bw_landed{i}") for i in range(NR)]
        k_landed = [sem(f"k_landed{i}") for i in range(4)]
        v_landed = [sem(f"v_landed{i}") for i in range(4)]
        qb_landed = [sem(f"qb_landed{i}") for i in range(2)]
        u_landed = [sem(f"u_landed{i}") for i in range(4)]
        e_landed = [sem(f"e_landed{i}") for i in range(4)]
        hb_landed = [sem(f"hb_landed{i}") for i in range(2)]

        G_QKV, G_CONV, G_MEM, G_GATE, G_O, G_PQ = 0, 16, 28, 36, 60, 68
        C_QKV, C_CONV, C_MEM, C_O, C_PQ = 0, 32, 56, 72, 88
        R_QKV, R_O, R_PQ = 0, 32, 48

        selfA = small[:, 4, 64:128].rearrange("p (h b) -> p h b", h=HEADS)

        block = ctx.enter_context(nc.Block())

        @block.sync
        def _(sp):
            sp.dma_start(colrows[0:16, :], A["norm1_w"][0].rearrange("(k p) -> k p", p=P)).then_inc(s["cols_in"], 16)
            sp.dma_start(colrows[16:32, :], A["mem_norm_w"][0].rearrange("(k p) -> k p", p=P)).then_inc(s["cols_in"], 16)
            sp.dma_start(colrows[32:56, :], A["conv_w"][0].rearrange("w (k p) -> (w k) p", p=P)).then_inc(s["cols_in"], 16)
            sp.dma_start(x_rows[:, 0:2, :], A["x_prompt"][0].rearrange("(t p) d -> p t d", p=P)).then_inc(s["x_in"], 16)
            sp.dma_start(x_rows[0:TS, 2, :], A["x_sample"].rearrange("b t d -> (b t) d")).then_inc(s["x_in"], 16)
            sp.dma_start(h2_rows[:, 0:2, :], A["mem_prompt"][0].rearrange("(t p) d -> p t d", p=P)).then_inc(s["mem_in"], 16)

            def fetch(r, src, col):
                sp.dma_start(wring[:, r], src[:, :, ds(col, BLK)]).then_inc(w_landed[r], 16)

            def stream(n, src, col, c0, before):
                for r in range(NR):
                    if before:
                        sp.wait_ge(s[before[0]], before[1] - 2 * (NR - 1 - r))
                    fetch(r, src, col + r * BLK)
                with sp.Fori(0, n // NR - 1) as i:
                    for r in range(NR):
                        sp.wait_ge(s["chunk_full"], i * (2 * NR) + (c0 + 2 * r + 2))
                        fetch(r, src, i * (NR * BLK) + (col + (NR + r) * BLK))

            stream(16, w_in, 3 * DC, C_QKV, None)
            stream(12, w_in, 0, C_CONV, ("chunk_full", C_CONV))
            stream(8, w_mem, 0, C_MEM, ("chunk_full", C_MEM))
            for b in range(3):
                for r in range(NR):
                    if b == 0:
                        sp.wait_ge(s["chunk_full"], C_O - 2 * (NR - 1 - r))
                    else:
                        sp.wait_ge(s["y_full"], 16 * b - 2 * (NR - 1 - r))
                    fetch(r, w_in, gate_col[b] + r * BLK)
                for r in range(NR):
                    if b == 0:
                        sp.wait_ge(s["chunk_full"], C_O)
                    sp.dma_start(bwring[:, r], w_br[b][:, :, ds(r * BLK, BLK)]).then_inc(bw_landed[r], 16)
                with sp.Fori(0, 8 // NR - 1) as i:
                    for r in range(NR):
                        sp.wait_ge(s["y_full"], i * (2 * NR) + (16 * b + 2 * r + 2))
                        fetch(r, w_in, i * (NR * BLK) + (gate_col[b] + (NR + r) * BLK))
                        sp.dma_start(bwring[:, r], w_br[b][:, :, ds(i * (NR * BLK) + (NR + r) * BLK, BLK)]).then_inc(bw_landed[r], 16)
            stream(8, w_o, 0, C_O, ("y_full", 48))
            stream(8, w_pq, 0, C_PQ, ("chunk_full", C_PQ))
            for t in range(2):
                sp.wait_ge(s["y_ready"], t + 1)
                sp.dma_start(O["y_prompt"][0, t * P:(t + 1) * P, :], x_rows[:, t, :]).then_inc(s["y_stored"], 16)
            sp.wait_ge(s["y_ready"], 3)
            sp.dma_start(O["y_sample"].rearrange("b t d -> (b t) d"), x_rows[0:TS, 2, :]).then_inc(s["y_stored"], 16)
            sp.wait_ge(s["y_stored"], 48)

        @block.gpsimd
        def _(pool):
            st = Steps(pool, s["pool_done"])
            pool.sem_inc(s["kpage_used"], 4)
            pool.sem_inc(s["vpage_used"], 4)
            pool.sem_inc(s["u_used"], 4)
            pool.sem_inc(s["v_used"], 4)
            pool.sem_inc(s["hb_used"], 2)
            pool.sem_inc(s["token_done"], 2)
            pool.dma_start(pt[:, :], A["page_table"].rearrange("(a b) n -> a (b n)", a=1)).then_inc(s["pt_in"], 16)
            st_rows = ring4[0:2 * TS, 0, :]
            pool.dma_start(st_rows, A["state_conv"][0].rearrange("b t c -> (b t) c")).then_inc(s["st_in"], 16)
            for dst, name in ((qn_w, "q_norm_w"), (kn_w, "k_norm_w"), (mq_w, "mq_norm_w"), (mk_w, "mk_norm_w")):
                pool.dma_start(dst[:, :], A[name][0:1, :].to_broadcast([P, dst.shape[1]])).then_inc(s["small_in"], 16)
            pool.dma_start(sub_w[:, :], A["subln_w"].rearrange("a p -> p a")).then_inc(s["small_in"], 16)
            for j, name in enumerate(("lambda_q1", "lambda_k1", "lambda_q2", "lambda_k2")):
                pool.dma_start(lam4[:, j, :], A[name][0:1, :].to_broadcast([P, DK])).then_inc(s["lam_in"], 16)
            pool.dma_start(rope[:, :, :], rope_tab).then_inc(s["rope_in"], 16)
            st(nc.gpsimd.memset(ident[:, :], 0.0))
            st(nc.gpsimd.affine_select(out=ident[:, :], in_=ident[:, :], compare_op=ALU.not_equal, fill=1.0, base=0,
                                       pattern=[[-1, P]], channel_multiplier=1))
            st(nc.gpsimd.memset(ones[:, :], 1.0))
            pool.sem_inc(s["consts"], 1)

            pool.wait_ge(s["q_ready"], 1)
            pool.dma_start(q_dram, rows[0:TS, 2, 0:DC]).then_inc(s["q_scratch"], 16)
            pool.dma_start(mq_dram, rows[0:TS, 2, 3 * DC:4 * DC]).then_inc(s["q_scratch"], 16)
            for c, (po, so) in ((1, ("k_prompt", "k_sample")), (2, ("v_prompt", "v_sample"))):
                pool.dma_start(O[po][0, 0].rearrange("(t p) h d -> p t (h d)", p=P),
                               rows[:, 0:2, c * DC:(c + 1) * DC]).then_inc(s["qk_stored"], 16)
                pool.dma_start(O[so][0].rearrange("b t h d -> (b t) (h d)"),
                               rows[0:TS, 2, c * DC:(c + 1) * DC]).then_inc(s["qk_stored"], 16)
            pool.wait_ge(s["q_scratch"], 32)
            pool.wait_ge(s["pt_in"], 16)
            pool.wait_ge(s["st_full"], 1)
            pool.wait_ge(s["small_in"], 80)
            with pool.Fori(0, TS // 2) as i:
                for par in range(2):
                    b = i * 2 + par
                    pool.wait_ge(s["token_done"], i * 2 + (par + 1))
                    pool.dma_start(qb[:, par, :], q_dram[ds(b, 1), :].to_broadcast([P, DC])).then_inc(qb_landed[par], 16)
                    with pool.Fori(0, PAGES // 4) as j:
                        for r in range(4):
                            n = i * 32 + j * 4 + (par * 16 + r)
                            pool.wait_ge(s["kpage_used"], n + 1)
                            page = pool.value_load(pt[0:1, ds(n, 1)], min_val=0, max_val=POOL_PAGES - 1)
                            pool.dma_start(ring4[:, r, :], cache_k[ds(page * PAGE, PAGE), :]).then_inc(k_landed[r], 16)
            with pool.Fori(0, TS // 2) as i:
                for par in range(2):
                    b = i * 2 + par
                    pool.wait_ge(s["token_done"], i * 2 + (TS + par + 1))
                    pool.dma_start(qb[:, par, :], mq_dram[ds(b, 1), :].to_broadcast([P, DC])).then_inc(qb_landed[par], 16)
                    for t in range(2):
                        pool.wait_ge(s["kpage_used"], i * 4 + (TS * PAGES + 2 * par + t + 1))
                        pool.dma_start(ring4[:, 2 * par + t, :], cmem_k[ds(b * NM + t * P, P), :]).then_inc(k_landed[2 * par + t], 16)

            pool.wait_ge(s["cs_rows"], 1)
            cs = cs_rows
            pool.dma_start(O["conv_prompt"][0, 0], cs[0:2, :]).then_inc(s["conv_stored"], 16)
            pool.dma_start(O["conv_sample"][0, :, 1, :], cs[2:2 + TS, :]).then_inc(s["conv_stored"], 16)
            pool.dma_start(O["conv_sample"][0, :, 0, :], A["state_conv"][0, :, 1, :]).then_inc(s["conv_stored"], 16)
            pool.wait_ge(s["a_ready"], 1)
            st(nc.gpsimd.memset(mask[:, :, :], 0.0))
            for t in range(2):
                st(nc.gpsimd.affine_select(out=mask[:, t, :], in_=mask[:, t, :], compare_op=ALU.is_ge, fill=NEG,
                                           base=t * P, pattern=[[-1, TP]], channel_multiplier=1))
            pool.sem_inc(s["consts"], 1)
            pool.wait_ge(s["mk_ready"], 1)
            for c, name in ((0, "mem_k_prompt"), (1, "mem_v_prompt")):
                pool.dma_start(O[name][0, 0].rearrange("(t p) h d -> p t (h d)", p=P),
                               mkv[:, :, c * DC:(c + 1) * DC]).then_inc(s["mkv_stored"], 16)

            pool.wait_ge(s["attn_done"], 2)
            pool.wait_ge(s["qk_stored"], 64)
            with pool.Fori(0, TS // 2) as i:
                for par in range(2):
                    with pool.Fori(0, PAGES // 4) as j:
                        for k in range(4):
                            r = (2 * par + k) % 4
                            pool.wait_ge(s["vpage_used"], i * 36 + j * 4 + (18 * par + k + 1))
                            page = pool.value_load(pt[0:1, ds(i * 32 + j * 4 + (16 * par + k), 1)], min_val=0, max_val=POOL_PAGES - 1)
                            pool.dma_start(v_slots[r], cache_v[ds(page * PAGE, PAGE), :]).then_inc(v_landed[r], 16)
                    for t in range(2):
                        r = (2 * par + t) % 4
                        pool.wait_ge(s["vpage_used"], i * 36 + (18 * par + 16 + t + 1))
                        pool.dma_start(v_slots[r], cmem_v[ds(i * (2 * NM) + (par * NM + t * P), P), :]).then_inc(v_landed[r], 16)

            pool.wait_ge(s["vpage_used"], TS * PAGES + 2 * TS + 4)
            pool.dma_start(x_rows[:, 0:2, :], A["x_prompt"][0].rearrange("(t p) d -> p t d", p=P)).then_inc(s["x_again"], 16)
            pool.dma_start(x_rows[0:TS, 2, :], A["x_sample"].rearrange("b t d -> (b t) d")).then_inc(s["x_again"], 16)
            st(nc.gpsimd.iota(iota_i, pattern=[[1, TOPK]], base=0, channel_multiplier=0))
            pool.sem_inc(s["consts"], 1)
            pool.wait_ge(s["mkv_stored"], 32)
            pool.wait_ge(s["conv_stored"], 48)
            pool.wait_ge(s["sub_scaled"], 1)
            pool.dma_start(n2_w, A["norm2_w"][0:1, :].to_broadcast([P, D])).then_inc(s["n2_in"], 16)
            pool.dma_start(sk_rows, A["sub_keys"][0].rearrange("c k d -> k c d")).then_inc(s["sk_in"], 16)
            pool.wait_ge(s["h2_ready"], 1)
            pool.dma_start(h2_dram, h2_rows[0:TS, 2, :]).then_inc(s["h2_scratch"], 16)

            def gather(table, dst, idx, landed):
                pool.sem_inc(s["gather_turn"], 1)
                nc.gpsimd.indirect_dma_start(dst, None, table, bass.IndirectOffsetOnAxis(ap=idx, axis=0)).then_inc(landed, 16)

            for t in range(2):
                pool.wait_ge(s["idx_ready"], t + 1)

                def stage(par, g):
                    st(nc.gpsimd.tensor_copy(uidx[:, par, :], idx_all[:, t, ds(g * TOPK, TOPK)]))

                def gather_u(par, n):
                    for j in range(TOPK):
                        gather_u1(par, n, j)

                def gather_u1(par, n, j):
                    pool.wait_ge(s["u_used"], n + (t * P + j + 1))
                    gather(peer_u, u_slots[j % 4], uidx[:, par, j:j + 1], u_landed[j % 4])

                def gather_v1(par, n, j):
                    pool.wait_ge(s["v_used"], n + (t * P + j + 1))
                    gather(peer_v, e_slots[j % 4], uidx[:, par, j:j + 1], e_landed[j % 4])

                if t:
                    pool.wait_ge(s["v_used"], P + 4)
                stage(0, 0)
                gather_u(0, 0)
                with st.loop(3, 2) as i:
                    for par in range(2):
                        g = i * 2 + par
                        pool.wait_ge(s["v_used"], i * 32 + (t * P + par * 16 + 4))
                        st(nc.gpsimd.tensor_copy(uidx[:, 1 - par, :], idx_all[:, t, ds(g * TOPK + TOPK, TOPK)]))
                        for j in range(TOPK):
                            gather_u1(1 - par, i * 32 + (par * 16 + 16), j)
                            gather_v1(par, i * 32 + par * 16, j)
                pool.wait_ge(s["v_used"], t * P + 96 + 4)
                stage(1, 7)
                for j in range(TOPK):
                    gather_u1(1, 112, j)
                    gather_v1(0, 96, j)
                for j in range(TOPK):
                    gather_v1(1, 112, j)

            pool.wait_ge(s["idx_ready"], 4)
            pool.wait_ge(s["h2_scratch"], 16)
            for b in range(TS):
                r = b % 2
                pool.wait_ge(s["hb_used"], b + 1)
                pool.dma_start(hb[r], h2_dram[b:b + 1, :].to_broadcast([P, D])).then_inc(hb_landed[r], 16)
                pool.wait_ge(s["u_used"], 2 * P + b + 1)
                gather(peer_u, u_slots[b % 4], sidx[:, b:b + 1], u_landed[b % 4])
                if b >= 4:
                    sample_v = b - 4
                    pool.wait_ge(s["v_used"], 2 * P + sample_v + 1)
                    gather(peer_v, e_slots[sample_v % 4], sidx[:, sample_v:sample_v + 1], e_landed[sample_v % 4])
            for b in range(4, TS):
                pool.wait_ge(s["v_used"], 2 * P + b + 1)
                gather(peer_v, e_slots[b % 4], sidx[:, b:b + 1], e_landed[b % 4])
            pool.wait_ge(s["qk_stored"], 64)

        @block.tensor
        def _(pe):
            mm = nc.tensor.matmul

            pe.wait_ge(s["consts"], 1)
            pe.wait_ge(s["cols_in"], 48)
            nc.tensor.transpose(ps[:, 0, 0:56], colrows, ident[0:56, 0:56]).then_inc(s["cols_full"], 1)
            pe.wait_ge(s["st_in"], 16)
            for j in range(BC):
                last = nc.tensor.transpose(ps[:, 1, j * 16:(j + 1) * 16], ring4[0:16, 0, j * P:(j + 1) * P], ident[0:16, 0:16])
            last.then_inc(s["st_full"], 1)

            def transpose_rows(src, k, bank, tiles):
                for t, (first, n) in enumerate(tiles):
                    last = nc.tensor.transpose(ps[:, bank, first:first + n], src[0:n, t, k * P:(k + 1) * P], ident[0:n, 0:n])
                return last

            pe.wait_ge(s["x_scaled"], 1)
            for k in range(KC):
                if k >= 4:
                    pe.wait_ge(s["xT_taken"], k - 3)
                transpose_rows(x_rows, k, 4 + k % 4, TILES).then_inc(s["xT_full"], 1)
            pe.wait_ge(s["x_scaled"], 2)
            for k in range(KC):
                pe.wait_ge(s["xT_taken"], KC + k - 3)
                transpose_rows(h2_rows, k, 4 + k % 4, TILES[0:2]).then_inc(s["xT_full"], 1)
            pe.wait_ge(s["xT_taken"], 2 * KC)

            def chunk(r, c, n, rhs):
                pe.wait_ge(s["chunk_taken"], n + 1)
                for k in range(KC):
                    last = mm(ps[:, (2 * r + c) % 4, 0:NT], wring[:, r, k, c * P:(c + 1) * P], rhs[:, k, :], start=(k == 0), stop=(k == KC - 1))
                last.then_inc(s["chunk_full"], 1)

            def linear(g0, n_blocks, c0, rhs, turn=None):
                with pe.Fori(0, n_blocks // NR) as i:
                    for r in range(NR):
                        pe.wait_ge(w_landed[r], i * 16 + 16 * (g0 // NR + 1))
                        for c in range(2):
                            q = 2 * r + c
                            chunk(r, c, i * (2 * NR) + (c0 + q), rhs)
                            if turn and q:
                                turn(q - 1, i * (2 * NR) + (q - 1))
                    if turn:
                        turn(2 * NR - 1, i * (2 * NR) + (2 * NR - 1))

            def turner(c0, m0):
                def turn(q, m):
                    pe.wait_ge(s["chunk_taken"], m + (c0 + 4 + 1))
                    pe.wait_ge(s["rows_taken"], m + (m0 + 1))
                    for t, (first, n) in enumerate(TILES):
                        last = nc.tensor.transpose(ps[0:n, 4 + q % 2, t * P:(t + 1) * P], zst[:, q % 2, first:first + n], ident[:, :])
                    last.then_inc(s["tr_full"], 1)
                return turn

            linear(G_QKV, 16, C_QKV, hT, turner(C_QKV, R_QKV))
            linear(G_CONV, 12, C_CONV, hT)
            with pe.Fori(0, 8 // NR) as i:
                for r in range(NR):
                    pe.wait_ge(w_landed[r], i * 16 + 16 * (G_MEM // NR + 1))
                    for t in range(2):
                        pe.wait_ge(s["chunk_taken"], i * (2 * NR) + (C_MEM + 2 * r + t + 1))
                        for k in range(KC):
                            last = mm(ps[:, (2 * r + t) % 4, 0:BLK], memT[:, k, t * P:(t + 1) * P], wring[:, r, k, :], start=(k == 0), stop=(k == KC - 1))
                        last.then_inc(s["chunk_full"], 1)
            pe.wait_ge(s["chunk_taken"], C_O + 4)
            pe.wait_ge(s["rows_taken"], 32 + 2)

            pe.wait_ge(s["conv_ready"], 1)
            for j in range(BC):
                last = nc.tensor.transpose(ps[0:2 + TS, j // 4, (j % 4) * P:(j % 4 + 1) * P], conv[:, BC + j, TP - 2:NT], ident[:, :])
            last.then_inc(s["cs_full"], 1)

            pe.wait_ge(s["self_in"], 1)
            mm(ps[:, 4, 0:P], ones[0:TS, :], small[0:TS, 0, :], start=True, stop=True).then_inc(s["self_full"], 1)
            for m in range(2):
                n = (P, TS * MH)[m]
                pe.wait_ge(s["max_full"], m + 1)
                nc.tensor.transpose(ps[0:n, 5, 0:P], small[:, 1, 0:n], ident[:, :]).then_inc(s["max_diag"], 1)
                pe.wait_ge(s["mb_full"], m + 1)
                mm(ps[:, 6, 0:n], ones[0:n, :], small[0:n, 2, 0:n], start=True, stop=True).then_inc(s["max_diag"], 1)
                pe.wait_ge(s["sum_in"], m + 1)
                mm(ps[:, 7, 0:n], ones[:, :], small[:, 1, 0:n], start=True, stop=True).then_inc(s["sum_full"], 1)
            pe.wait_ge(s["a_ready"], 1)

            def flat(u):
                b = 4 - 4 * u
                return ps[:, b:b + 4, :].rearrange("p a b -> p (a b)")

            def attention(n_heads, base, w):
                halves = w // P
                a0 = 1536
                s0 = 512 * halves
                with pe.Fori(0, n_heads // 2) as i:
                    for u in range(2):
                        pe.wait_ge(s["attn_staged"], i * 2 + (base + u + 1))
                        for o in range(2):
                            for f in range(halves):
                                for t in range(2):
                                    last = nc.tensor.transpose(
                                        flat(u)[:, (o * halves + f) * 256 + t * P:(o * halves + f) * 256 + (t + 1) * P],
                                        temp[u][:, (2 * o + t) * w + f * P:(2 * o + t) * w + (f + 1) * P], ident[:, :])
                        last.then_inc(s["tt_full"], 1)
                    for u in range(2):
                        pe.wait_ge(s["qk_T"], i * 2 + (base + u + 1))
                        T = temp[u][:, 6 * w:6 * w + 1024]
                        for t in range(2):
                            if halves == 1:
                                for c in range(2):
                                    last = mm(flat(u)[:, s0 + (2 * c + t) * 256:s0 + (2 * c + t + 1) * 256],
                                              T[c * DK:(c + 1) * DK, t * P:(t + 1) * P], T[c * DK:(c + 1) * DK, 256:512], start=True, stop=True)
                            else:
                                for f in range(2):
                                    last = mm(flat(u)[:, s0 + t * 256:s0 + (t + 1) * 256], T[:, f * 256 + t * P:f * 256 + (t + 1) * P],
                                              T[:, 512 + f * 256:512 + (f + 1) * 256], start=(f == 0), stop=(f == 1))
                        last.then_inc(s["s_full"], 1)
                    for u in range(2):
                        pe.wait_ge(s["p_ready"], i * 2 + (base + u + 1))
                        p0, step = (6 * w + 512, 512) if halves == 1 else (6 * w + 1024, 256)
                        for k in range(2):
                            for t in range(2):
                                last = nc.tensor.transpose(flat(u)[:, a0 + k * 256 + t * P:a0 + k * 256 + (t + 1) * P],
                                                           temp[u][:, p0 + t * step + k * P:p0 + t * step + (k + 1) * P], ident[:, :])
                        last.then_inc(s["at_full"], 1)
                    for u in range(2):
                        pe.wait_ge(s["at_ready"], i * 2 + (base + u + 1))
                        t0 = 6 * w + 512 + 1024 if halves == 1 else 6 * w + 1024 + 512
                        for f in range(halves):
                            for k in range(2):
                                last = mm(flat(u)[:, a0 + f * 256:a0 + (f + 1) * 256], temp[u][:, 4 * w + k * w + f * P:4 * w + k * w + (f + 1) * P],
                                          temp[u][:, t0 + k * 256:t0 + (k + 1) * 256], start=(k == 0), stop=(k == 1))
                        last.then_inc(s["o_full"], 1)

            attention(HEADS, 0, DV)
            attention(MH, HEADS, MD)
            pe.wait_ge(s["attn_done"], 2)

            pe.wait_ge(s["merge_zero"], 1)
            mm(ps[:, 4, 0:P], mask0, mask0, start=True, stop=False, skip_group_check=True)

            def own_value():
                for h in range(HEADS):
                    mm(ps[:, 4, h:TS * HEADS:HEADS], rows[0:TS, 2, 2 * DC + h * DV:2 * DC + (h + 1) * DV],
                       selfA[0:TS, h, :], start=False, stop=False, skip_group_check=True)
            own_value()

            def value_page(i, par, j, k):
                r = (2 * par + k) % 4
                b = i * 2 + par
                pe.wait_ge(v_landed[r], i * (9 * 16) + j * 16 + 16 * ((18 * par + k) // 4 + 1))
                for h in range(HEADS):
                    last = mm(ps[:, 4, ds(b * HEADS + h, 1)], v_slots[r][:, h * DV:(h + 1) * DV],
                              Ad_f[:, ds(b * (PAGES * HEADS) + j * (4 * HEADS) + (k * HEADS + h), 1)], start=False, stop=False, skip_group_check=True)
                last.then_inc(s["vpage_used"], 1)

            def value_mem(i, par, t):
                r = (2 * par + t) % 4
                b = i * 2 + par
                pe.wait_ge(v_landed[r], i * (9 * 16) + 16 * ((18 * par + 16 + t) // 4 + 1))
                for h in range(MH):
                    for f in range(2):
                        last = mm(ps[:, 4, ds(b * BC + (64 + 2 * h + f), 1)], v_slots[r][:, h * MD + f * P:h * MD + (f + 1) * P],
                                  Sm_f[:, ds(b * (2 * MH) + (t * MH + h), 1)], start=False, stop=False, skip_group_check=True)
                last.then_inc(s["vpage_used"], 1)

            for b, operand in enumerate((conv[:, 0:BC, :], oT_mem, oT_diff)):
                if b:
                    pe.wait_ge(s["vo_ready" if b == 1 else "sub_scaled"], 1)
                with pe.Fori(0, 8 // NR) as i:
                    for r in range(NR):
                        g = G_GATE // NR + b * (8 // NR)
                        pe.wait_ge(w_landed[r], i * 16 + 16 * (g + 1))
                        pe.wait_ge(bw_landed[r], i * 16 + 16 * (b * (8 // NR) + 1))
                        for c in range(2):
                            q = i * (2 * NR) + (16 * b + 2 * r + c)
                            pe.wait_ge(s["gate_done"], q + 1)
                            for k in range(KC):
                                last = mm(ps[:, c, 0:NT], wring[:, r, k, c * P:(c + 1) * P], hT[:, k, :], start=(k == 0), stop=(k == KC - 1))
                            last.then_inc(s["gate_full"], 1)
                            pe.wait_ge(s["y_taken"], q + 1)
                            for k in range(BC):
                                last = mm(ps[:, 2 + c, 0:NT], bwring[:, r, k, c * P:(c + 1) * P], operand[:, k, :], start=(k == 0), stop=(k == BC - 1))
                            last.then_inc(s["y_full"], 1)
                            if b == 0:
                                with pe.Fori(2 * c, 2 * c + 2) as j:
                                    for k in range(4):
                                        value_page(i, r, j, k)
                                if c:
                                    value_mem(i, r, 0)
                                    value_mem(i, r, 1)
                if b == 0:
                    mm(ps[:, 4, 0:P], mask0, mask0, start=False, stop=True, skip_group_check=True).then_inc(s["vo_full"], 1)
                if b == 1:
                    pe.wait_ge(s["sub_in"], 1)
                    for h in range(HEADS):
                        if h >= 4:
                            pe.wait_ge(s["sub_taken"], h - 3)
                        mm(ps[:, 4 + h % 4, 0:NT], ones[:, :], sq_mkv[:, h * NT:(h + 1) * NT], start=True, stop=True).then_inc(s["sub_full"], 1)

            pe.wait_ge(s["merge_ready"], 1)
            linear(G_O, 8, C_O, merged, turner(C_O, R_O))
            pe.wait_ge(s["x1_ready"], 1)
            for k in range(KC):
                if k >= 4:
                    pe.wait_ge(s["h2T_taken"], k - 3)
                transpose_rows(h2_rows, k, 4 + k % 4, TILES).then_inc(s["h2T_full"], 1)
            pe.wait_ge(s["h2T_taken"], KC)
            pe.wait_ge(s["sk_in"], 16)
            for c in range(2):
                last = nc.tensor.transpose(ps[:, 6, c * P:(c + 1) * P], sk_rows[:, c, :], ident[:, :])
            last.then_inc(s["sk_full"], 1)
            pe.wait_ge(s["sk_ready"], 1)

            def score(q, m):
                pe.wait_ge(s["chunk_taken"], m + (C_PQ + 4 + 1))
                pe.wait_ge(s["rows_taken"], m + (R_PQ + 1))
                for t, (first, n) in enumerate(TILES):
                    last = mm(ps[0:n, 4 + q % 2, t * P:(t + 1) * P], zst[:, q % 2, first:first + n], skT[:, q % 2, :], start=True, stop=True)
                last.then_inc(s["tr_full"], 1)

            linear(G_PQ, 8, C_PQ, hT, score)
            pe.wait_ge(s["rows_taken"], 64 + 2)
            pe.wait_ge(s["chunk_taken"], 104 + 4)

            pe.wait_ge(s["sT_in"], 1)
            nc.tensor.transpose(ps[:, 4, 0:TS], idx_f[0:TS, :], ident[0:TS, 0:TS])
            nc.tensor.transpose(ps[:, 4, TS:2 * TS], gates[0:TS, 2, :], ident[0:TS, 0:TS]).then_inc(s["sT_full"], 1)

            pe.wait_ge(s["zero_ready"], 1)
            for t in range(3):
                if t:
                    pe.wait_ge(s["y_ready"], t)
                n = TILES[t][1]

                def add_zero(start, stop):
                    for q in range(4):
                        last = mm(ps[0:n, q, :], zero512[:, 0:n], zero512, start=start, stop=stop, skip_group_check=True)
                    return last

                add_zero(True, False)

                def add_head(g):
                    for j in range(TOPK):
                        pe.wait_ge(s["diag_ready"], g * TOPK + (t * P + j + 1))
                        pe.wait_ge(e_landed[j % 4], g * 64 + 16 * (t * 32 + j // 4 + 1))
                        for q in range(4):
                            last = mm(ps[:, q, :], diag[:, j % 4, :], e_slots[j % 4][:, q * 512:(q + 1) * 512], start=False, stop=False, skip_group_check=True)
                        last.then_inc(s["v_used"], 1)

                if t < 2:
                    with pe.Fori(0, PH) as g:
                        add_head(g)
                else:
                    pe.wait_ge(s["w_ready"], 17)
                    for b in range(TS):
                        pe.wait_ge(e_landed[b % 4], 16 * (64 + b // 4 + 1))
                        for q in range(4):
                            last = mm(ps[0:TS, q, :], wz[:, b, :], e_slots[b % 4][:, q * 512:(q + 1) * 512], start=False, stop=False, skip_group_check=True)
                        last.then_inc(s["v_used"], 1)
                add_zero(False, True).then_inc(s["yo_full"], 1)

        @block.scalar
        def _(act):
            st = Steps(act, s["act_done"])
            A_ = nc.scalar.activation
            act.sem_inc(s["chunk_taken"], 4)
            act.sem_inc(s["gate_done"], 2)
            junk = cflat[:, 0:D]

            def square_sums(tiles):
                for col, src, n in tiles:
                    st(A_(junk[0:n], src, ACT.Square, accum_out=stat[0:n, col:col + 1]))

            def root(n, ap):
                act.wait_ge(s["sqrt_in"], n)
                st(A_(ap, ap, ACT.Sqrt))
                act.sem_inc(s["sqrt_out"], 1)

            act.wait_ge(s["x_clear"], 1)
            act.wait_ge(s["x_in"], 32)
            square_sums([(t, x_rows[0:n, t, :], n) for t, (_, n) in enumerate(TILES)])
            act.wait_ge(s["mem_in"], 16)
            square_sums([(3 + t, h2_rows[:, t, :], P) for t in range(2)])
            act.sem_inc(s["x_ss"], 1)
            root(1, stat[:, 0:5])
            act.wait_ge(s["lam_pre"], 1)
            st(A_(lam[:, 0:2], lam[:, 0:2], ACT.Exp))
            act.sem_inc(s["lam_exp"], 1)
            act.wait_ge(s["cols_ready"], 1)
            for k in range(2 * KC):
                act.wait_ge(s["xT_full"], k + 1)
                if k < KC:
                    st(A_(hT[:, k, :], ps[:, 4 + k % 4, 0:NT], ACT.Copy, scale=cols[:, k:k + 1]))
                else:
                    st(A_(memT[:, k - KC, :], ps[:, 4 + k % 4, 0:NM], ACT.Copy, scale=cols[:, k:k + 1]))
                act.sem_inc(s["xT_taken"], 1)

            def to_stage(n_chunks, c0, m0):
                with st.loop(n_chunks // 4, 4) as i:
                    for q in range(4):
                        act.wait_ge(s["chunk_full"], i * 4 + (c0 + q + 1))
                        act.wait_ge(s["rows_taken"], i * 4 + (m0 + q + 1))
                        st(A_(zst[:, q % 2, :], ps[:, q, 0:NT], ACT.Copy))
                        act.sem_inc(s["chunk_taken"], 1)

            to_stage(32, C_QKV, R_QKV)
            with st.loop(6, 4) as i:
                for q in range(4):
                    act.wait_ge(s["chunk_full"], i * 4 + (C_CONV + q + 1))
                    st(A_(cflat[:, ds(i * (4 * NT) + q * NT, NT)], ps[:, q, 0:NT], ACT.Copy))
                    act.sem_inc(s["chunk_taken"], 1)
            root(2, small[:, 3, 0:108])
            act.wait_ge(s["q_ready"], 1)
            with st.loop(4, 4) as i:
                for q in range(4):
                    act.wait_ge(s["chunk_full"], i * 4 + (C_MEM + q + 1))
                    st(A_(mkv[:, q % 2, ds(i * (2 * BLK) + (q // 2) * BLK, BLK)], ps[:, q, 0:BLK], ACT.Copy))
                    act.sem_inc(s["chunk_taken"], 1)

            act.wait_ge(s["exp_in"], 1)
            st.run(A_(work, work, ACT.Exp, scale=DK ** -0.5))
            st(A_(small[:, 0, :], small[:, 0, :], ACT.Exp, scale=DK ** -0.5))
            act.sem_inc(s["exp_out"], 1)
            act.wait_ge(s["exp_in"], 2)
            st(A_(Sm_f, Sm_f, ACT.Exp, scale=MD ** -0.5))
            act.sem_inc(s["exp_out"], 1)
            root(3, small[:, 3, 0:8])

            def flat(u):
                b = 4 - 4 * u
                return ps[:, b:b + 4, :].rearrange("p a b -> p (a b)")

            def attention(n_heads, base, w, srcs, out, n_rows, scale):
                T0 = 6 * w
                tt = 512 * (w // P)
                with st.loop(n_heads // 2, 2 * (3 + 1 + n_rows + 1 + 1)) as i:
                    for u in range(2):
                        for o, (src, col) in enumerate(srcs):
                            st.run(A_(temp[u][:, 2 * o * w:(2 * o + 2) * w].rearrange("p (t n) -> p t n", t=2),
                                      src[:, 0:2, ds(i * (2 * w) + (col + u * w), w)], ACT.Copy))
                        st.settle()
                        act.sem_inc(s["attn_staged"], 1)
                    for u in range(2):
                        act.wait_ge(s["tt_full"], i * 2 + (base + u + 1))
                        st(A_(temp[u][:, T0:T0 + tt], flat(u)[:, 0:tt], ACT.Copy))
                        act.sem_inc(s["qk_T"], 1)
                    for u in range(2):
                        act.wait_ge(s["sm_ready"], i * 2 + (base + u + 1))
                        for n in range(n_rows):
                            dst = temp[u][:, T0 + tt + n * 256:T0 + tt + (n + 1) * 256]
                            src = dst if n_rows == 4 else flat(u)[:, tt + n * 256:tt + (n + 1) * 256]
                            st.run(A_(dst, src, ACT.Exp, scale=scale, bias=stat[:, 16 * u + 4 + n:16 * u + 5 + n],
                                      accum_out=stat[:, 16 * u + 8 + n:16 * u + 9 + n]))
                        st.settle()
                        act.sem_inc(s["exp_ready"], 1)
                    for u in range(2):
                        act.wait_ge(s["at_full"], i * 2 + (base + u + 1))
                        st(A_(temp[u][:, T0 + 1536:T0 + 2048], flat(u)[:, 1536:2048], ACT.Copy))
                        act.sem_inc(s["at_ready"], 1)
                    for u in range(2):
                        act.wait_ge(s["o_full"], i * 2 + (base + u + 1))
                        c = w // P
                        st(A_(out[:, ds(i * (2 * c) + u * c, c), 0:TP], flat(u)[:, 1536:1536 + 256 * c].rearrange("p (a b) -> p a b", a=c), ACT.Copy))
                act.sem_inc(s["attn_done"], 1)

            qkv = [(rows, 0), (rows, DC), (rows, 2 * DC)]
            act.wait_ge(s["mk_ready"], 1)
            attention(HEADS, 0, DV, qkv, oT_diff, 4, DK ** -0.5)
            attention(MH, HEADS, MD, [(rows, 3 * DC), (mkv, 0), (mkv, DC)], oT_mem, 2, MD ** -0.5)

            for b in range(3):
                with st.loop(4, 4) as i:
                    for q in range(4):
                        act.wait_ge(s["gate_full"], i * 4 + (16 * b + q + 1))
                        act.wait_ge(s["y_taken"], i * 4 + (16 * b + q + 1))
                        st(A_(sg[:, q % 2, :], ps[:, q % 2, 0:NT], ACT.Sigmoid))
                        act.sem_inc(s["gate_done"], 1)
                if b == 1:
                    root(4, sq_mkv[:, 0:BC * NT])

            to_stage(16, C_O, R_O)
            act.wait_ge(s["x1_rows"], 1)
            square_sums([(t, x_rows[0:n, t, :], n) for t, (_, n) in enumerate(TILES)])
            act.sem_inc(s["n2_ss"], 1)
            root(5, stat[:, 0:3])
            for k in range(KC):
                act.wait_ge(s["h2T_full"], k + 1)
                st(A_(hT[:, k, :], ps[:, 4 + k % 4, 0:NT], ACT.Copy))
                act.sem_inc(s["h2T_taken"], 1)
            to_stage(16, C_PQ, R_PQ)
            for t in range(3):
                act.wait_ge(s["gate_in"], t + 1)
                st(A_(win_v, win_v, ACT.Exp))
                act.sem_inc(s["gate_out"], 1)

            for t in range(2):
                with st.loop(PH, 1 + TOPK) as g:
                    act.wait_ge(s["a_in"], g + (t * PH + 1))
                    st(A_(act_g[:, 0, :], act_a[:, 0, :], ACT.Gelu))
                    act.sem_inc(s["a_out"], 1)
                    act.wait_ge(s["w_ready"], g + (t * PH + 1))
                    for j in range(TOPK):
                        act.wait_ge(s["v_used"], g * TOPK + (t * P + j + 1))
                        st(A_(diag[:, j % 4, :], ident[:, :], ACT.Copy, scale=wexp[:, 0, j:j + 1]))
                        act.sem_inc(s["diag_ready"], 1)
            act.wait_ge(s["a_in"], 2 * PH + 1)
            st(A_(act_g[:, 0, 0:TS], act_a[:, 0, 0:TS], ACT.Gelu))
            act.sem_inc(s["a_out"], 1)

        @block.vector
        def _(dve):
            st = Steps(dve, s["dve_done"])
            V = nc.vector
            TT, TSC, STT, CP, RED, REC = V.tensor_tensor, V.tensor_scalar, V.scalar_tensor_tensor, V.tensor_copy, V.tensor_reduce, V.reciprocal

            def signal(name, n=1):
                dve.sem_inc(s[name], n)

            def root(n):
                signal("sqrt_in")
                dve.wait_ge(s["sqrt_out"], n)

            signal("rows_taken", 2)
            signal("y_taken", 2)
            st(V.memset(stat[:, :], 1.0))
            signal("x_clear")
            dve.wait_ge(s["lam_in"], 64)
            st(TT(lam4[:, 0, :], lam4[:, 0, :], lam4[:, 1, :], ALU.mult))
            st(TT(lam4[:, 2, :], lam4[:, 2, :], lam4[:, 3, :], ALU.mult))
            st(RED(lam[:, 0:1], lam4[:, 0, :], X, ALU.add))
            st(RED(lam[:, 1:2], lam4[:, 2, :], X, ALU.add))
            signal("lam_pre")
            dve.wait_ge(s["cols_full"], 1)
            st.run(CP(cols[:, :], ps[:, 0, 0:56]))
            dve.wait_ge(s["st_full"], 1)
            st(CP(stT[:, :, :], ps[:, 1, 0:P].rearrange("p (a b) -> p a b", a=BC)))
            signal("cols_ready")

            dve.wait_ge(s["x_ss"], 1)
            st(TSC(stat[:, 0:5], stat[:, 0:5], 1.0 / D, EPS, ALU.mult, ALU.add))
            root(1)
            st(REC(stat[:, 0:5], stat[:, 0:5]))
            for t, (_, n) in enumerate(TILES):
                st.run(TSC(x_rows[0:n, t, :], x_rows[0:n, t, :], stat[0:n, t:t + 1], None, ALU.mult))
            st.settle()
            signal("x_scaled")
            for t in range(2):
                st.run(TSC(h2_rows[:, t, :], h2_rows[:, t, :], stat[:, 3 + t:4 + t], None, ALU.mult))
            st.settle()
            signal("x_scaled")
            dve.wait_ge(s["lam_exp"], 1)
            st(TT(lam[:, 2:3], lam[:, 1:2], lam[:, 0:1], ALU.subtract))
            st(TSC(lam[:, 3:4], lam[:, 2:3], LAM_INIT, None, ALU.subtract))

            dve.wait_ge(s["xT_full"], 2 * KC)
            st(V.memset(rows[:, 2, :], 0.0))

            def rows_from(n_chunks, m0, out, add=False):
                with st.loop(n_chunks // 4, 8) as i:
                    for q in range(4):
                        dve.wait_ge(s["tr_full"], i * 4 + (m0 + q + 1))
                        at = ds(i * (4 * P) + q * P, P)
                        src = ps[:, 4 + q % 2, 0:2 * P].rearrange("p (t n) -> p t n", t=2)
                        own = ps[0:TS, 4 + q % 2, 2 * P:3 * P]
                        if add:
                            st.run(TT(out[:, 0:2, at], src, out[:, 0:2, at], ALU.add))
                            st(TT(out[0:TS, 2, at], own, out[0:TS, 2, at], ALU.add))
                        else:
                            st.run(CP(out[:, 0:2, at], src))
                            st(CP(out[0:TS, 2, at], own))
                        signal("rows_taken")

            rows_from(32, R_QKV, rows)

            dve.wait_ge(s["small_in"], 80)
            dve.wait_ge(s["rope_in"], 16)
            r_ = small[:, 3, :]
            sq3 = sq_mkv[:, 0:3 * DC].rearrange("p (t n) -> p t n", t=3)
            groups = [(0, 16, DK, qn_w, 0), (DC, 16, DK, kn_w, 48), (3 * DC, 4, MD, mq_w, 96)]
            for c, g, w, _, at in groups:
                part = rows[:, :, c:c + DC]
                st(TT(sq3, part, part, ALU.mult))
                st(RED(r_[:, at:at + 3 * g], sq_mkv[:, 0:3 * DC].rearrange("p (g w) -> p g w", w=w), X, ALU.add))
                st(TSC(r_[:, at:at + 3 * g], r_[:, at:at + 3 * g], 1.0 / w, EPS, ALU.mult, ALU.add))
            root(2)
            st(REC(r_[:, 0:108], r_[:, 0:108]))
            for c, g, w, wt, at in groups:
                part = rows[:, :, c:c + DC].rearrange("p t (g w) -> p t g w", w=w)
                rr = r_[:, at:at + 3 * g].rearrange("p (t g) -> p t g", t=3).unsqueeze(3).broadcast_to([P, 3, g, w])
                st(TT(part, part, rr, ALU.mult))
                for t in range(3):
                    st.run(TT(part[:, t], part[:, t], wt[:, :].unsqueeze(1).broadcast_to([P, g, w]), ALU.mult))
                st.settle()
                if w == DK:
                    cos, sin = [rope[:, :, 8 * h:8 * h + 8].unsqueeze(2).broadcast_to([P, 3, g, 8]) for h in range(2)]
                    x1, x2 = part[:, :, :, 0:8], part[:, :, :, 8:16]
                    t4 = [sq_mkv[:, 384 * n:384 * (n + 1)].rearrange("p (t g w) -> p t g w", t=3, g=g) for n in range(4)]
                    for n, (a, b) in enumerate(((x1, cos), (x2, sin), (x2, cos), (x1, sin))):
                        st.run(TT(t4[n], a, b, ALU.mult))
                    st.settle()
                    st.run(TT(x1, t4[0], t4[1], ALU.subtract))
                    st(TT(x2, t4[2], t4[3], ALU.add))
            signal("q_ready")

            def page_scores(slot, par, out, w):
                st(TT(prod, ring4[:, slot, :], qb[:, par, :], ALU.mult))
                signal("kpage_used")
                st(RED(out, prod.rearrange("p (g w) -> p g w", w=w), X, ALU.add))

            with st.loop(TS // 2, 2 * PAGES * 2) as i:
                for par in range(2):
                    dve.wait_ge(qb_landed[par], i * 16 + 16)
                    signal("loop_turn")
                    with st.loop(PAGES // 4, 8) as j:
                        for r in range(4):
                            dve.wait_ge(k_landed[r], i * (16 * 8) + j * 16 + (16 * 4 * par + 16))
                            page_scores(r, par, work[:, ds(i * 512 + j * 64 + (par * 256 + r * 16), 16)], DK)
                    signal("token_done")
            with st.loop(TS // 2, 8) as i:
                for par in range(2):
                    dve.wait_ge(qb_landed[par], i * 16 + (64 + 16))
                    for t in range(2):
                        dve.wait_ge(k_landed[2 * par + t], i * 16 + (32 * 16 + 16))
                        page_scores(2 * par + t, par, Sm_f[:, ds(i * 16 + (par * 8 + t * 4), 4)], MD)
                    signal("token_done")

            dve.wait_ge(s["chunk_taken"], C_MEM + 4)
            st(TT(conv[:, BC:2 * BC, :], conv[:, BC:2 * BC, :], conv[:, 2 * BC:3 * BC, :], ALU.mult))
            for j in range(BC):
                u, y = conv[:, BC + j, :], conv[:, 2 * BC + j, :]
                w0, w1, w2 = [cols[:, 32 + 8 * n + j:33 + 8 * n + j] for n in range(3)]
                st(TSC(y, u, w2, None, ALU.mult))
                st(STT(y[:, 1:TP], u[:, 0:TP - 1], w1, y[:, 1:TP], ALU.mult, ALU.add))
                st(STT(y[:, 2:TP], u[:, 0:TP - 2], w0, y[:, 2:TP], ALU.mult, ALU.add))
                st(STT(y[:, TP:NT], stT[:, j, 1:2 * TS:2], w1, y[:, TP:NT], ALU.mult, ALU.add))
                st(STT(y[:, TP:NT], stT[:, j, 0:2 * TS:2], w0, y[:, TP:NT], ALU.mult, ALU.add))
            st(TT(conv[:, 0:BC, :], conv[:, 0:BC, :], conv[:, 2 * BC:3 * BC, :], ALU.mult))
            signal("conv_ready")

            b0, b1, b2, b3, b4 = [small[:, n, :] for n in range(5)]
            st(TT(prod[0:TS], rows[0:TS, 2, 0:DC], rows[0:TS, 2, DC:2 * DC], ALU.mult))
            st(RED(b4[0:TS, 0:16], prod[0:TS].rearrange("p (g w) -> p g w", w=DK), X, ALU.add))
            st(TT(b0[0:TS].rearrange("p (b c) -> p b c", b=TS), b4[0:TS, 0:16].unsqueeze(1).broadcast_to([TS, TS, 16]),
                  ident[0:TS, 0:TS].unsqueeze(2).broadcast_to([TS, TS, 16]), ALU.mult))
            signal("self_in")
            by_page = S[:, :, :, :].rearrange("p b g c -> p b c g")
            c3 = lambda ap: ap.rearrange("p (b c) -> p b c", b=TS)
            st(RED(c3(b1), by_page, X, ALU.max))
            dve.wait_ge(s["self_full"], 1)
            st(CP(b0, ps[:, 4, 0:P]))
            st(TT(b1, b1, b0, ALU.max))

            def all_max(m, n):
                signal("max_full")
                dve.wait_ge(s["max_diag"], 2 * m + 1)
                st(RED(stat[0:n, 40:41], ps[0:n, 5, 0:P], X, ALU.max))
                st(TSC(b2[0:n, 0:n], ident[0:n, 0:n], stat[0:n, 40:41], None, ALU.mult))
                signal("mb_full")
                dve.wait_ge(s["max_diag"], 2 * m + 2)
                st(CP(b3[:, 0:n], ps[:, 6, 0:n]))

            all_max(0, P)
            over_pages = lambda ap: c3(ap).unsqueeze(2).broadcast_to([P, TS, PAGES, 16])
            st.run(TT(S[:, :, :, :], S[:, :, :, :], over_pages(b3), ALU.subtract))
            st(TT(b0, b0, b3, ALU.subtract))
            signal("exp_in")
            dve.wait_ge(s["exp_out"], 1)
            st(RED(c3(b1), by_page, X, ALU.add))
            signal("sum_in")
            dve.wait_ge(s["sum_full"], 1)
            st(TT(b1, ps[:, 7, 0:P], b0, ALU.add))
            st(REC(b1, b1))
            odd = b1.rearrange("p (a c) -> p a c", c=2)[:, :, 1:2]
            st(TSC(odd, odd, lam[:, 3:4], None, ALU.mult))
            st.run(TT(S[:, :, :, :], S[:, :, :, :], over_pages(b1), ALU.mult))
            st(TT(b0, b0, b1, ALU.mult))
            dve.wait_ge(s["cs_full"], 1)
            st(CP(cs_rows[0:2 + TS, :].rearrange("p (a b) -> p a b", a=2), ps[0:2 + TS, 0:2, :]))
            signal("cs_rows")
            pairs = work.rearrange("p (a c) -> p a c", c=2)
            ob = b0.rearrange("p (a c) -> p a c", c=2)
            st(TT(b4[:, 0:64].unsqueeze(2), ob[:, :, 0:1], ob[:, :, 1:2], ALU.add))
            st(TT(selfA[0:TS], b4[0:TS, 0:64].rearrange("p (b h) -> p h b", b=TS),
                  ident[0:TS, 0:TS].unsqueeze(1).broadcast_to([TS, HEADS, TS]), ALU.mult))

            mem3 = Sm[:, :, :, :]
            n = TS * MH
            m3 = b1[:, 0:n].rearrange("p (b h) -> p b h", b=TS)
            st(TT(m3, mem3[:, :, 0, :], mem3[:, :, 1, :], ALU.max))
            all_max(1, n)
            over_m = lambda ap: ap[:, 0:n].rearrange("p (b h) -> p b h", b=TS).unsqueeze(2).broadcast_to([P, TS, 2, MH])
            st(TT(mem3, mem3, over_m(b3), ALU.subtract))
            signal("exp_in")
            dve.wait_ge(s["exp_out"], 2)
            st(TT(m3, mem3[:, :, 0, :], mem3[:, :, 1, :], ALU.add))
            signal("sum_in")
            dve.wait_ge(s["sum_full"], 2)
            st(REC(b1[:, 0:n], ps[:, 7, 0:n]))
            st(TT(mem3, mem3, over_m(b1), ALU.mult))
            dve.wait_ge(s["conv_stored"], 48)
            st(TT(cs_rows.unsqueeze(2), pairs[:, :, 0:1], pairs[:, :, 1:2], ALU.add))
            signal("a_ready")

            dve.wait_ge(s["chunk_taken"], C_O + 4)
            sqm = oflat[:, 0:D].rearrange("p (t n) -> p t n", t=2)
            mk = mkv[:, :, 0:DC]
            st(TT(sqm, mk, mk, ALU.mult))
            st(RED(b3[:, 0:8], oflat[:, 0:D].rearrange("p (g w) -> p g w", w=MD), X, ALU.add))
            st(TSC(b3[:, 0:8], b3[:, 0:8], 1.0 / MD, EPS, ALU.mult, ALU.add))
            root(3)
            st(REC(b3[:, 0:8], b3[:, 0:8]))
            mk4 = mk.rearrange("p t (g w) -> p t g w", w=MD)
            st(TT(mk4, mk4, b3[:, 0:8].rearrange("p (t g) -> p t g", t=2).unsqueeze(3).broadcast_to([P, 2, 4, MD]), ALU.mult))
            for t in range(2):
                st.run(TT(mk4[:, t], mk4[:, t], mk_w[:, :].unsqueeze(1).broadcast_to([P, 4, MD]), ALU.mult))
            st.settle()
            signal("mk_ready")

            dve.wait_ge(s["consts"], 2)

            def flat(u):
                b = 4 - 4 * u
                return ps[:, b:b + 4, :].rearrange("p a b -> p (a b)")

            with st.loop(HEADS // 2, 2 * 3 + 2 * 6) as i:
                for u in range(2):
                    sm = temp[u][:, 6 * DV + 512:6 * DV + 1536]
                    v4 = lambda ap: ap.rearrange("p (t c n) -> p t c n", t=2, c=2)
                    dve.wait_ge(s["s_full"], i * 2 + (u + 1))
                    st(TT(v4(sm), flat(u)[:, 512:1536].rearrange("p (c t n) -> p t c n", t=2, c=2), mask[:, :, :].unsqueeze(2).broadcast_to([P, 2, 2, TP]), ALU.add))
                    st(RED(stat[:, 16 * u:16 * u + 4], sm.rearrange("p (a n) -> p a n", a=4), X, ALU.max))
                    st(TSC(stat[:, 16 * u + 4:16 * u + 8], stat[:, 16 * u:16 * u + 4], -DK ** -0.5, None, ALU.mult))
                    signal("sm_ready")
                for u in range(2):
                    sm = temp[u][:, 6 * DV + 512:6 * DV + 1536]
                    r4 = stat[:, 16 * u + 12:16 * u + 16]
                    dve.wait_ge(s["exp_ready"], i * 2 + (u + 1))
                    st(REC(r4, stat[:, 16 * u + 8:16 * u + 12]))
                    st(TSC(r4[:, 1:4:2], r4[:, 1:4:2], lam[:, 3:4], None, ALU.mult))
                    for t in range(2):
                        a, b = sm[:, t * 512:t * 512 + 256], sm[:, t * 512 + 256:t * 512 + 512]
                        st(TSC(a, a, r4[:, 2 * t:2 * t + 1], None, ALU.mult))
                        st(STT(a, b, r4[:, 2 * t + 1:2 * t + 2], a, ALU.mult, ALU.add))
                    signal("p_ready")
            with st.loop(MH // 2, 2 * 2 + 2 * 3) as i:
                for u in range(2):
                    dve.wait_ge(s["s_full"], i * 2 + (HEADS + u + 1))
                    st(RED(stat[:, 16 * u:16 * u + 2], flat(u)[:, 1024:1536].rearrange("p (a n) -> p a n", a=2), X, ALU.max))
                    st(TSC(stat[:, 16 * u + 4:16 * u + 6], stat[:, 16 * u:16 * u + 2], -MD ** -0.5, None, ALU.mult))
                    signal("sm_ready")
                for u in range(2):
                    sm = temp[u][:, 6 * MD + 1024:6 * MD + 1536]
                    dve.wait_ge(s["exp_ready"], i * 2 + (HEADS + u + 1))
                    st(REC(stat[:, 16 * u + 12:16 * u + 14], stat[:, 16 * u + 8:16 * u + 10]))
                    for t in range(2):
                        st.run(TSC(sm[:, t * 256:(t + 1) * 256], sm[:, t * 256:(t + 1) * 256], stat[:, 16 * u + 12 + t:16 * u + 13 + t], None, ALU.mult))
                    st.settle()
                    signal("p_ready")
            dve.wait_ge(s["attn_done"], 2)
            st.run(V.memset(merged, 0.0))
            st(V.memset(zst[:, :, :], 0.0))
            signal("merge_zero")

            for b in range(3):
                with st.loop(4, 8) as i:
                    for q in range(4):
                        dve.wait_ge(s["gate_done"], i * 4 + (16 * b + q + 3))
                        dve.wait_ge(s["y_full"], i * 4 + (16 * b + q + 1))
                        st(TT(tmpm, sg[:, q % 2, :], ps[:, 2 + q % 2, 0:NT], ALU.mult))
                        signal("y_taken")
                        at = ds(i * (4 * NT) + (BC * NT + q * NT), NT)
                        st(TT(cflat[:, at], cflat[:, at], tmpm, ALU.add))
                if b == 0:
                    dve.wait_ge(s["vo_full"], 1)
                    st.run(CP(oT_diff[:, :, TP:NT], ps[:, 4, 0:64].rearrange("p (b h) -> p h b", b=TS)))
                    st(CP(oT_mem[:, :, TP:NT], ps[:, 4, 64:128].rearrange("p (b h) -> p h b", b=TS)))
                    signal("vo_ready")
                    dve.wait_ge(s["mkv_stored"], 32)
                    of = oflat[:, BC * NT:2 * BC * NT]
                    st(TT(sq_mkv[:, 0:BC * NT], of, of, ALU.mult))
                    signal("sub_in")
                if b == 1:
                    for h in range(HEADS):
                        dve.wait_ge(s["sub_full"], h + 1)
                        st(TSC(sq_mkv[:, h * NT:(h + 1) * NT], ps[:, 4 + h % 4, 0:NT], 1.0 / DV, EPS, ALU.mult, ALU.add))
                        signal("sub_taken")
                    root(4)
                    st(REC(sq_mkv[:, 0:BC * NT], sq_mkv[:, 0:BC * NT]))
                    st(TT(of, of, sq_mkv[:, 0:BC * NT], ALU.mult))
                    st(TSC(of, of, sub_w[:, 0:1], 1.0 - LAM_INIT, ALU.mult, ALU.mult))
                    signal("sub_scaled")
            signal("merge_ready")

            dve.wait_ge(s["x_again"], 32)
            rows_from(16, R_O, rows, add=True)
            st(V.memset(stat[:, 0:8], 1.0))
            signal("x1_rows")
            dve.wait_ge(s["n2_ss"], 1)
            st(TSC(stat[:, 0:3], stat[:, 0:3], 1.0 / D, EPS, ALU.mult, ALU.add))
            root(5)
            st(REC(stat[:, 0:3], stat[:, 0:3]))
            dve.wait_ge(s["n2_in"], 16)
            for t, (_, n) in enumerate(TILES):
                st.run(STT(h2_rows[0:n, t, :], x_rows[0:n, t, :], stat[0:n, t:t + 1], n2_w[0:n, :], ALU.mult, ALU.mult))
            st.settle()
            signal("x1_ready")
            signal("h2_ready")
            dve.wait_ge(s["sk_full"], 1)
            st(CP(skT, ps[:, 6, 0:2 * P].rearrange("p (c d) -> p c d", c=2)))
            signal("sk_ready")
            st(V.memset(scores[:, 2, :], 0.0))
            rows_from(16, R_PQ, scores)

            st.run(V.memset(zero512, 0.0))
            st.run(V.memset(wz, 0.0))
            dve.wait_ge(s["consts"], 3)
            st(CP(iota_f, iota_i))
            signal("zero_ready")
            for t in range(3):
                st(CP(work, scores[:, t, :]))
                for c in range(2 * PH):
                    sc, a, b = work[:, c * NKEY:(c + 1) * NKEY], c * TOPK, c * TOPK + 8
                    st(V.max(top_v[:, a:a + 8], sc))
                    st(V.max_index(top_i[:, a:a + 8], top_v[:, a:a + 8], sc))
                    st(V.match_replace(sc, top_v[:, a:a + 8], sc, -3e38))
                    st(V.max(top_v[:, b:b + 8], sc))
                    st(V.max_index(top_i[:, b:b + 8], top_v[:, b:b + 8], sc))
                st(CP(top_f, top_i))
                four = [P, PH, TOPK, TOPK]
                hv = top_v.rearrange("p (h c n) -> p h c n", h=PH, c=2)
                hf = top_f.rearrange("p (h c n) -> p h c n", h=PH, c=2)
                f4 = lambda ap: ap.rearrange("p (h a b) -> p h a b", h=PH, a=TOPK)
                st(TT(f4(cand), hv[:, :, 0, :].unsqueeze(3).broadcast_to(four), hv[:, :, 1, :].unsqueeze(2).broadcast_to(four), ALU.add))
                for h in range(PH):
                    sc, a, b = cand[:, h * 256:(h + 1) * 256], h * TOPK, h * TOPK + 8
                    st(V.max(win_v[:, a:a + 8], sc))
                    st(V.max_index(win_p[:, a:a + 8], win_v[:, a:a + 8], sc))
                    st(V.match_replace(sc, win_v[:, a:a + 8], sc, -3e38))
                    st(V.max(win_v[:, b:b + 8], sc))
                    st(V.max_index(win_p[:, b:b + 8], win_v[:, b:b + 8], sc))
                wv = win_v.rearrange("p (h n) -> p h n", h=PH)
                st(TT(hot[:, 0:P].rearrange("p (h n) -> p h n", h=PH), wv, wv[:, :, 0:1].broadcast_to([P, PH, TOPK]), ALU.subtract))
                st(CP(win_v, hot[:, 0:P]))
                signal("gate_in")
                for half, (op, arg) in enumerate(((ALU.logical_shift_right, 4), (ALU.bitwise_and, 15))):
                    st(V.tensor_single_scalar(part_i, win_p, arg, op))
                    st(CP(part_f[:, half * P:(half + 1) * P], part_i))
                    pf = part_f[:, half * P:(half + 1) * P].rearrange("p (h n) -> p h n", h=PH).unsqueeze(3).broadcast_to(four)
                    st(TT(f4(hot), pf, iota_f.unsqueeze(1).unsqueeze(1).broadcast_to(four), ALU.is_equal))
                    st(TT(f4(hot), f4(hot), hf[:, :, half, :].unsqueeze(2).broadcast_to(four), ALU.mult))
                    st(RED(pick[:, half * P:(half + 1) * P], hot.rearrange("p (a b) -> p a b", b=TOPK), X, ALU.add))
                st(STT(idx_f, pick[:, 0:P], float(NKEY), pick[:, P:2 * P], ALU.mult, ALU.add))
                st(CP(idx_all[:, t, :], idx_f))
                dve.wait_ge(s["gate_out"], t + 1)
                st(RED(denom[:, 0:PH], wv, X, ALU.add))
                st(REC(denom[:, 0:PH], denom[:, 0:PH]))
                st(TT(gates[:, t, :].rearrange("p (h n) -> p h n", h=PH), wv, denom[:, 0:PH].unsqueeze(2).broadcast_to([P, PH, TOPK]), ALU.mult))
                signal("idx_ready")
            signal("sT_in")
            dve.wait_ge(s["sT_full"], 1)
            st.run(CP(sidx, ps[:, 4, 0:TS]))
            st(CP(sgate, ps[:, 4, TS:2 * TS]))
            signal("idx_ready")

            def dots(count, h2, slot, out):
                st(V.tensor_tensor_reduce(out=work, in0=u_slots[slot], in1=h2, scale=1.0, scalar=0.0, op0=ALU.mult, op1=ALU.add, accum_out=out))
                signal("u_used")

            for t in range(2):
                with st.loop(PH, TOPK + 1) as g:
                    for j in range(TOPK):
                        dve.wait_ge(u_landed[j % 4], g * 64 + 16 * (t * 32 + j // 4 + 1))
                        dots(None, h2_rows[:, t, :], j % 4, act_a[:, 0, j:j + 1])
                    signal("a_in")
                    dve.wait_ge(s["a_out"], g + (t * PH + 1))
                    dve.wait_ge(s["v_used"], g * TOPK + (t * P + 4))
                    st(TT(wexp[:, 0, :], act_g[:, 0, :], gates[:, t, ds(g * TOPK, TOPK)], ALU.mult))
                    signal("w_ready")
                dve.wait_ge(s["yo_full"], t + 1)
                st(TT(x_rows[:, t, :].rearrange("p (a b) -> p a b", a=4), ps[:, 0:4, :], x_rows[:, t, :].rearrange("p (a b) -> p a b", a=4), ALU.add))
                signal("y_ready")
            for b in range(TS):
                dve.wait_ge(hb_landed[b % 2], 16 * (b // 2 + 1))
                dve.wait_ge(u_landed[b % 4], 16 * (64 + b // 4 + 1))
                dots(None, hb[b % 2], b % 4, act_a[:, 0, b:b + 1])
                signal("hb_used")
            signal("a_in")
            dve.wait_ge(s["a_out"], 2 * PH + 1)
            st(TT(wz.rearrange("p b c -> p (b c)")[:, 0:TS * TS:TS + 1], act_g[:, 0, 0:TS], sgate, ALU.mult))
            signal("w_ready")
            dve.wait_ge(s["yo_full"], 3)
            st(TT(x_rows[0:TS, 2, :].rearrange("p (a b) -> p a b", a=4), ps[0:TS, 0:4, :], x_rows[0:TS, 2, :].rearrange("p (a b) -> p a b", a=4), ALU.add))
            signal("y_ready")


_OUTS = [("y_prompt", (1, 256, 2048)), ("y_sample", (8, 1, 2048)), ("k_prompt", (1, 1, 256, 8, 128)),
         ("v_prompt", (1, 1, 256, 8, 128)), ("conv_prompt", (1, 1, 2, 1024)), ("mem_k_prompt", (1, 1, 256, 4, 256)),
         ("mem_v_prompt", (1, 1, 256, 4, 256)), ("k_sample", (1, 8, 1, 8, 128)), ("v_sample", (1, 8, 1, 8, 128)),
         ("conv_sample", (1, 8, 2, 1024))]


def rope_table():
    half = DK // 8
    freq = np.float32(500000.0) ** (-np.arange(half, dtype=np.float32) / np.float32(half))
    pos = np.concatenate([np.arange(TP), np.full(P, PAGES * PAGE)]).astype(np.float32)
    ang = pos[:, None] * freq[None, :]
    tab = np.concatenate([np.cos(ang), np.sin(ang)], axis=1).astype(np.float32)
    return np.ascontiguousarray(tab.reshape(3, P, 2 * half).transpose(1, 0, 2))


def kernel(**inputs):
    import concourse.bacc as bacc
    from concourse.bass_utils import run_bass_kernel_spmd

    nc = bacc.Bacc("TRN2", target_bir_lowering=False, num_devices=1)
    arrays, A, O = {}, {}, {}
    for name, a in list(inputs.items()) + [("rope_tab", rope_table())]:
        a = np.ascontiguousarray(a)
        arrays[f"in_{name}_dram"] = a
        A[name] = nc.dram_tensor(f"in_{name}_dram", a.shape, mybir.dt.from_np(a.dtype), kind="ExternalInput").ap()
    for name, shape in _OUTS:
        O[name] = nc.dram_tensor(f"out_{name}_dram", shape, F32, kind="ExternalOutput").ap()
    build(nc, A, O)
    r = run_bass_kernel_spmd(nc, [arrays], core_ids=[0])
    return tuple(r.results[0][f"out_{name}_dram"] for name, _ in _OUTS)
```

```python
from contextlib import ExitStack, contextmanager

import numpy as np

import concourse.bass as bass
from concourse import mybir

F32 = mybir.dt.float32
I32 = mybir.dt.int32
U32 = mybir.dt.uint32
ALU = mybir.AluOpType
ACT = mybir.ActivationFunctionType
X = mybir.AxisListType.X
ds = bass.ds

P = 128
D = 2048
KC = D // P
TP, TS = 256, 8
NT = TP + TS
DC = D // 2
BC = DC // P
HEADS, DK, DV = 8, 64, 128
MH, MD, NM = 4, 256, 256
PAGES, PAGE = 16, 128
POOL_PAGES = 160
NKEY, PH, TOPK = 128, 8, 16
EPS = 1e-6
NEG = -1e30
LAM_INIT = 0.2
BLK = 256
NR = 2
TILES = [(0, P), (P, P), (TP, TS)]


class Steps:

    def __init__(self, eng, sem):
        self.eng, self.sem, self.base, self.k = eng, sem, 0, 0

    def run(self, ins):
        ins.then_inc(self.sem, 1)
        self.k += 1

    def settle(self):
        self.eng.wait_ge(self.sem, self.base + self.k)

    def reach(self, k):
        self.eng.wait_ge(self.sem, self.base + k)

    def __call__(self, ins):
        self.run(ins)
        self.settle()

    @contextmanager
    def loop(self, n, per):
        base, k = self.base, self.k
        with self.eng.Fori(0, n) as i:
            self.base, self.k = base + (i * per + k), 0
            yield i
            assert self.k == per, f"the body has {self.k} steps, not {per}"
        self.base, self.k = base, k + n * per


def build(nc, A, O):
    rope_tab = A["rope_tab"]
    w_in = A["w_in"][0].rearrange("(k p) n -> p k n", p=P)
    w_mem = A["w_mem_kv"][0].rearrange("(k p) n -> p k n", p=P)
    w_o = A["w_o"][0].rearrange("(k p) n -> p k n", p=P)
    w_pq = A["w_peer_q"][0].rearrange("(k p) n -> p k n", p=P)
    w_br = [A[n][0].rearrange("(k p) n -> p k n", p=P) for n in ("w_conv_out", "w_cross_out", "w_diff_out")]
    gate_col = [7 * 1024, 7 * 1024 + 2 * D, 7 * 1024 + D]
    cache_k = A["cache_k"][0].rearrange("n t h d -> (n t) (h d)")
    cache_v = A["cache_v"][0].rearrange("n t h d -> (n t) (h d)")
    cmem_k = A["cache_mem_k"][0].rearrange("b m h d -> (b m) (h d)")
    cmem_v = A["cache_mem_v"][0].rearrange("b m h d -> (b m) (h d)")
    peer_u, peer_v = A["peer_u"][0], A["peer_v"][0]
    q_dram = nc.dram_tensor("q_rows_scratch", [TS, DC], F32, kind="Internal").ap()
    mq_dram = nc.dram_tensor("mq_rows_scratch", [TS, DC], F32, kind="Internal").ap()
    h2_dram = nc.dram_tensor("h2_rows_scratch", [TS, D], F32, kind="Internal").ap()

    ctx = ExitStack()
    with ctx:
        def sb(name, shape, dt=F32):
            return ctx.enter_context(nc.sbuf_tensor("sb_" + name, shape, dt))

        def sem(name):
            return ctx.enter_context(nc.semaphore(name))

        ps = ctx.enter_context(nc.psum_tensor("ps", [P, 8, 512], F32))

        wring = sb("wring", [P, NR, KC, BLK])
        bregion = sb("bregion", [P, 4096])
        ring4 = sb("ring4", [P, 4, DC])
        hT = sb("hT", [P, KC, NT])
        conv = sb("conv", [P, 3 * BC, NT])
        rows = sb("rows", [P, 3, 4 * DC])
        mkv = sb("mkv", [P, 2, 2 * DC])
        S = sb("S", [P, TS, PAGES, 2 * HEADS])
        Ad = sb("Ad", [P, TS, PAGES, HEADS])
        oreg = sb("oreg", [P, 2 * BC, NT])
        memT = bregion[:, :].rearrange("p (k m) -> p k m", k=KC)
        bwring = bregion[:, :].rearrange("p (s k n) -> p s k n", s=NR, k=BC)
        merged = conv[:, BC:3 * BC, :]
        oT_mem, oT_diff = oreg[:, 0:BC, :], oreg[:, BC:2 * BC, :]
        oflat = oreg[:, :, :].rearrange("p a b -> p (a b)")
        qb = oflat[:, 0:2 * DC].rearrange("p (s n) -> p s n", s=2)
        prods = [oflat[:, n * DC:(n + 1) * DC] for n in (2, 3)]
        prod = prods[0]
        cflat = conv[:, :, :].rearrange("p a b -> p (a b)")
        temp = [ring4[:, :, :].rearrange("p a b -> p (a b)"), cflat[:, BC * NT:3 * BC * NT]]
        x_rows, h2_rows = rows[:, :, 0:D], rows[:, :, D:2 * D]
        cs_rows = Ad[:, :, :, :].rearrange("p a b c -> p (a b c)")
        n2_w, sk_rows = mkv[:, 0, :], mkv[:, 1, 0:2 * P].rearrange("p (c d) -> p c d", c=2)
        skT = mkv[:, 1, 2 * P:4 * P].rearrange("p (c d) -> p c d", c=2)
        sq_mkv = mkv[:, :, :].rearrange("p a b -> p (a b)")
        kpages = [ring4[:, n, :] for n in range(4)] + [sq_mkv[:, n * DC:(n + 1) * DC] for n in range(4)]
        ring_flat = ring4[:, :, :].rearrange("p a b -> p (a b)")
        scores = cflat[:, 0:3 * 2 * PH * NKEY].rearrange("p (t n) -> p t n", t=3)
        work = S[:, :, :, :].rearrange("p a b c -> p (a b c)")
        colrows, lam4 = work[0:56, 0:P], work[:, P:P + 4 * DK].rearrange("p (a n) -> p a n", a=4)
        mask = work[:, 0:2 * TP].rearrange("p (t n) -> p t n", t=2)
        sg = work[:, 1024:1024 + 2 * NT].rearrange("p (s n) -> p s n", s=2)
        rt = ring4[:, :, :].rearrange("p a b -> p (a b)")
        top_v, top_i = [mkv[:, 1, n:n + 3 * 256].rearrange("p (t n) -> p t n", t=3) for n in (4 * P, 4 * P + 3 * 256)]
        top_i = top_i.bitcast(U32)
        top_f = rt[:, 0:256]
        win_v, win_p = [rt[:, n:n + 3 * P].rearrange("p (t n) -> p t n", t=3) for n in (256, 640)]
        win_p = win_p.bitcast(U32)
        part_i, part_f = rt[:, 1024:1152].bitcast(U32), rt[:, 1152:1408]
        pick = rt[:, 1408:1664]
        iota_i, iota_f = rt[:, 1664:1680].bitcast(I32), rt[:, 1680:1696]
        idx_f = rt[:, 1696:1824]
        idx_all = rt[:, 1824:2208].bitcast(I32).rearrange("p (t n) -> p t n", t=3)
        idx_flat = rt[:, 1824:2208].bitcast(I32)
        gates = rt[:, 2208:2592].rearrange("p (t n) -> p t n", t=3)
        uidx = rt[:, 2592:2624].bitcast(I32).rearrange("p (s n) -> p s n", s=2)
        sidx, sgate = rt[:, 2624:2632].bitcast(I32), rt[:, 2632:2640]
        act_a = rt[:, 2640:2672].rearrange("p (s n) -> p s n", s=2)
        act_g = rt[:, 2672:2704].rearrange("p (s n) -> p s n", s=2)
        wexp = rt[:, 2704:2736].rearrange("p (s n) -> p s n", s=2)
        wz = rt[:, 2736:2800].rearrange("p (b c) -> p b c", b=TS)
        denom = rt[:, 2800:2824]
        diag = rt[:, 3072:3584].rearrange("p (s n) -> p s n", s=4)
        zero512 = rt[:, 3584:4096]
        hot = oflat[:, 2048:4096]
        cand, cand_rest = [oflat[:, n:n + 3 * 256].rearrange("p (t n) -> p t n", t=3) for n in (0, 768)]
        score_rest = work[:, 0:3 * NKEY].rearrange("p (t n) -> p t n", t=3)
        shifted = work[:, 1024:1024 + 3 * P]
        u_slots = [wring[:, r].rearrange("p k n -> p (k n)")[:, h * D:(h + 1) * D] for r in range(NR) for h in range(2)]
        hflat = hT[:, :, :].rearrange("p k n -> p (k n)")
        e_slots = [bregion[:, 0:D], bregion[:, D:2 * D], hflat[:, 0:D], hflat[:, D:2 * D]]
        hb = [oflat[:, 0:D], oflat[:, D:2 * D]]
        v_slots = [rows[:, t, c * DC:(c + 1) * DC] for t in range(2) for c in range(2)]

        ident = sb("ident", [P, P])
        ones = sb("ones", [P, P])
        cols = sb("cols", [P, 56])
        stT = sb("stT", [P, BC, 2 * TS])
        qn_w, kn_w, sub_w = sb("qn_w", [P, DK]), sb("kn_w", [P, DK]), sb("sub_w", [P, 1])
        mq_w, mk_w = sb("mq_w", [P, MD]), sb("mk_w", [P, MD])
        rope = sb("rope", [P, 3, 16])
        lam = sb("lam", [P, 4])
        zst = sb("zst", [P, 2, NT])
        stat = sb("stat", [P, 64])
        pt = sb("pt", [1, TS * PAGES], I32)
        Sm = sb("Sm", [P, TS, 2, MH])
        small = sb("small", [P, 5, P])
        mask0 = zst[:, :, :].rearrange("p a b -> p (a b)")[:, 0:P]
        Ad_f, Sm_f = cs_rows, Sm[:, :, :, :].rearrange("p a b c -> p (a b c)")
        tmpm = small[:, 0:3, :].rearrange("p a b -> p (a b)")[:, 0:NT]

        names = """consts const_w x_in x_clear mem_in cols_in st_in small_in lam_in rope_in pt_in x_ss x_var x_sd x_scaled
            xT_full xT_taken cols_full cols_ready st_full chunk_full chunk_taken tr_full rows_taken kprod_ready
            q_ready qk_stored q_scratch kpage_used token_done kd_done conv_ready cs_full cs_rows conv_stored
            sqrt_in sqrt_out mk_ready mkv_stored self_full self_in max_full max_diag mb_full exp_in exp_out sum_in
            sum_full a_ready attn_staged tt_full qk_T s_full sm_ready exp_ready p_ready at_full at_ready o_full
            attn_done vpage_used vo_full vo_ready sub_in sub_full sub_scaled gate_full gate_done y_full y_taken
            merge_ready x_again x1_ready h2T_in h2_ready h2T_full h2T_taken h2_scratch sk_in sk_full sk_ready
            s_cleared gate_in gate_out idx_ready sT_full sT_in u_used a_in a_out w_ready diag_ready v_used yo_full
            y_ready y_stored hb_used zero_ready dve_done act_done pool_done mem_taken n2_in lam_pre lam_exp sqrt_pad x1_rows n2_ss h2T_x st_ready
            merge_zero sub_taken gather_turn loop_turn""".split()
        s = {n: sem(n) for n in names}
        w_landed = [sem(f"w_landed{i}") for i in range(NR)]
        bw_landed = [sem(f"bw_landed{i}") for i in range(NR)]
        k_landed = [sem(f"k_landed{i}") for i in range(8)]
        v_landed = [sem(f"v_landed{i}") for i in range(4)]
        qb_landed = [sem(f"qb_landed{i}") for i in range(2)]
        u_landed = [sem(f"u_landed{i}") for i in range(4)]
        e_landed = [sem(f"e_landed{i}") for i in range(4)]
        hb_landed = [sem(f"hb_landed{i}") for i in range(2)]

        G_QKV, G_CONV, G_MEM, G_GATE, G_O, G_PQ = 0, 16, 28, 36, 60, 68
        C_QKV, C_CONV, C_MEM, C_O, C_PQ = 0, 32, 56, 72, 88
        R_QKV, R_O, R_PQ = 0, 32, 48

        selfA = small[:, 4, 64:128].rearrange("p (h b) -> p h b", h=HEADS)

        block = ctx.enter_context(nc.Block())

        @block.sync
        def _(sp):
            sp.dma_start(colrows[0:16, :], A["norm1_w"][0].rearrange("(k p) -> k p", p=P)).then_inc(s["cols_in"], 16)
            sp.dma_start(colrows[16:32, :], A["mem_norm_w"][0].rearrange("(k p) -> k p", p=P)).then_inc(s["cols_in"], 16)
            sp.dma_start(colrows[32:56, :], A["conv_w"][0].rearrange("w (k p) -> (w k) p", p=P)).then_inc(s["cols_in"], 16)
            sp.dma_start(x_rows[:, 0:2, :], A["x_prompt"][0].rearrange("(t p) d -> p t d", p=P)).then_inc(s["x_in"], 16)
            sp.dma_start(x_rows[0:TS, 2, :], A["x_sample"].rearrange("b t d -> (b t) d")).then_inc(s["x_in"], 16)
            sp.dma_start(h2_rows[:, 0:2, :], A["mem_prompt"][0].rearrange("(t p) d -> p t d", p=P)).then_inc(s["mem_in"], 16)

            def fetch(r, src, col):
                sp.dma_start(wring[:, r], src[:, :, ds(col, BLK)]).then_inc(w_landed[r], 16)

            def stream(n, src, col, c0, before):
                for r in range(NR):
                    if before:
                        sp.wait_ge(s[before[0]], before[1] - 2 * (NR - 1 - r))
                    fetch(r, src, col + r * BLK)
                with sp.Fori(0, n // NR - 1) as i:
                    for r in range(NR):
                        sp.wait_ge(s["chunk_full"], i * (2 * NR) + (c0 + 2 * r + 2))
                        fetch(r, src, i * (NR * BLK) + (col + (NR + r) * BLK))

            stream(16, w_in, 3 * DC, C_QKV, None)
            stream(12, w_in, 0, C_CONV, ("chunk_full", C_CONV))
            stream(8, w_mem, 0, C_MEM, ("chunk_full", C_MEM))
            for b in range(3):
                for r in range(NR):
                    if b == 0:
                        sp.wait_ge(s["chunk_full"], C_O - 2 * (NR - 1 - r))
                    else:
                        sp.wait_ge(s["y_full"], 16 * b - 2 * (NR - 1 - r))
                    fetch(r, w_in, gate_col[b] + r * BLK)
                for r in range(NR):
                    if b == 0:
                        sp.wait_ge(s["chunk_full"], C_O)
                    sp.dma_start(bwring[:, r], w_br[b][:, :, ds(r * BLK, BLK)]).then_inc(bw_landed[r], 16)
                with sp.Fori(0, 8 // NR - 1) as i:
                    for r in range(NR):
                        sp.wait_ge(s["y_full"], i * (2 * NR) + (16 * b + 2 * r + 2))
                        fetch(r, w_in, i * (NR * BLK) + (gate_col[b] + (NR + r) * BLK))
                        sp.dma_start(bwring[:, r], w_br[b][:, :, ds(i * (NR * BLK) + (NR + r) * BLK, BLK)]).then_inc(bw_landed[r], 16)
            stream(8, w_o, 0, C_O, ("y_full", 48))
            stream(8, w_pq, 0, C_PQ, ("chunk_full", C_PQ))
            for t in range(2):
                sp.wait_ge(s["y_ready"], t + 1)
                sp.dma_start(O["y_prompt"][0, t * P:(t + 1) * P, :], x_rows[:, t, :]).then_inc(s["y_stored"], 16)
            sp.wait_ge(s["y_ready"], 3)
            sp.dma_start(O["y_sample"].rearrange("b t d -> (b t) d"), x_rows[0:TS, 2, :]).then_inc(s["y_stored"], 16)
            sp.wait_ge(s["y_stored"], 48)

        @block.gpsimd
        def _(pool):
            st = Steps(pool, s["pool_done"])
            pool.sem_inc(s["kpage_used"], 8)
            pool.sem_inc(s["vpage_used"], 4)
            pool.sem_inc(s["u_used"], 4)
            pool.sem_inc(s["v_used"], 4)
            pool.sem_inc(s["hb_used"], 2)
            pool.sem_inc(s["token_done"], 2)
            pool.dma_start(pt[:, :], A["page_table"].rearrange("(a b) n -> a (b n)", a=1)).then_inc(s["pt_in"], 16)
            st_rows = ring4[0:2 * TS, 0, :]
            pool.dma_start(st_rows, A["state_conv"][0].rearrange("b t c -> (b t) c")).then_inc(s["st_in"], 16)
            for dst, name in ((qn_w, "q_norm_w"), (kn_w, "k_norm_w"), (mq_w, "mq_norm_w"), (mk_w, "mk_norm_w")):
                pool.dma_start(dst[:, :], A[name][0:1, :].to_broadcast([P, dst.shape[1]])).then_inc(s["small_in"], 16)
            pool.dma_start(sub_w[:, :], A["subln_w"].rearrange("a p -> p a")).then_inc(s["small_in"], 16)
            for j, name in enumerate(("lambda_q1", "lambda_k1", "lambda_q2", "lambda_k2")):
                pool.dma_start(lam4[:, j, :], A[name][0:1, :].to_broadcast([P, DK])).then_inc(s["lam_in"], 16)
            pool.dma_start(rope[:, :, :], rope_tab).then_inc(s["rope_in"], 16)
            st(nc.gpsimd.memset(ident[:, :], 0.0))
            st(nc.gpsimd.affine_select(out=ident[:, :], in_=ident[:, :], compare_op=ALU.not_equal, fill=1.0, base=0,
                                       pattern=[[-1, P]], channel_multiplier=1))
            st(nc.gpsimd.memset(ones[:, :], 1.0))
            pool.sem_inc(s["consts"], 1)

            pool.wait_ge(s["q_ready"], 1)
            pool.dma_start(q_dram, rows[0:TS, 2, 0:DC]).then_inc(s["q_scratch"], 16)
            pool.wait_ge(s["q_scratch"], 16)
            pool.wait_ge(s["pt_in"], 16)
            pool.wait_ge(s["st_full"], 1)
            pool.wait_ge(s["small_in"], 80)

            def load_pages(i, g):
                par, half = g // 4 % 2, g % 2
                if g % 4 == 0:
                    b = i * 2 + g // 4
                    pool.wait_ge(s["token_done"], i * 2 + (g // 4 + 1))
                    pool.dma_start(qb[:, par, :], q_dram[ds(b, 1), :].to_broadcast([P, DC])).then_inc(qb_landed[par], 16)
                for r in range(4):
                    n = i * 32 + (g * 4 + r)
                    pool.wait_ge(s["kpage_used"], n + 1)
                    page = pool.value_load(pt[0:1, ds(n, 1)], min_val=0, max_val=POOL_PAGES - 1)
                    pool.dma_start(kpages[4 * half + r], cache_k[ds(page * PAGE, PAGE), :]).then_inc(k_landed[4 * half + r], 16)

            def multiply_pages(i, g):
                par, half = g // 4, g % 2
                pool.wait_ge(qb_landed[par], i * 16 + 16)
                for r in (1, 3):
                    pool.wait_ge(k_landed[4 * half + r], i * 64 + 16 * (g // 2 + 1))
                    st(nc.gpsimd.tensor_tensor(kpages[4 * half + r], kpages[4 * half + r], qb[:, par, :], ALU.mult))
                    pool.sem_inc(s["kprod_ready"], 1)

            load_pages(0, 0)
            with st.loop(TS // 2 - 1, 16) as i:
                for g in range(8):
                    load_pages(i, g + 1)
                    multiply_pages(i, g)
            for g in range(8):
                if g < 7:
                    load_pages(TS // 2 - 1, g + 1)
                multiply_pages(TS // 2 - 1, g)

            pool.wait_ge(s["q_ready"], 2)
            pool.dma_start(mq_dram, rows[0:TS, 2, 3 * DC:4 * DC]).then_inc(s["q_scratch"], 16)
            for c, (po, so) in ((1, ("k_prompt", "k_sample")), (2, ("v_prompt", "v_sample"))):
                pool.dma_start(O[po][0, 0].rearrange("(t p) h d -> p t (h d)", p=P),
                               rows[:, 0:2, c * DC:(c + 1) * DC]).then_inc(s["qk_stored"], 16)
                pool.dma_start(O[so][0].rearrange("b t h d -> (b t) (h d)"),
                               rows[0:TS, 2, c * DC:(c + 1) * DC]).then_inc(s["qk_stored"], 16)
            pool.wait_ge(s["q_scratch"], 32)
            with pool.Fori(0, TS // 2) as i:
                for par in range(2):
                    b = i * 2 + par
                    pool.wait_ge(s["token_done"], i * 2 + (TS + par + 1))
                    pool.dma_start(qb[:, par, :], mq_dram[ds(b, 1), :].to_broadcast([P, DC])).then_inc(qb_landed[par], 16)
                    for t in range(2):
                        pool.wait_ge(s["kpage_used"], i * 4 + (TS * PAGES + 4 + 2 * par + t + 1))
                        pool.dma_start(ring4[:, 2 * par + t, :], cmem_k[ds(b * NM + t * P, P), :]).then_inc(k_landed[2 * par + t], 16)

            pool.wait_ge(s["cs_rows"], 1)
            cs = cs_rows
            pool.dma_start(O["conv_prompt"][0, 0], cs[0:2, :]).then_inc(s["conv_stored"], 16)
            pool.dma_start(O["conv_sample"][0, :, 1, :], cs[2:2 + TS, :]).then_inc(s["conv_stored"], 16)
            pool.dma_start(O["conv_sample"][0, :, 0, :], A["state_conv"][0, :, 1, :]).then_inc(s["conv_stored"], 16)
            pool.wait_ge(s["a_ready"], 1)
            st(nc.gpsimd.memset(mask[:, :, :], 0.0))
            for t in range(2):
                st(nc.gpsimd.affine_select(out=mask[:, t, :], in_=mask[:, t, :], compare_op=ALU.is_ge, fill=NEG,
                                           base=t * P, pattern=[[-1, TP]], channel_multiplier=1))
            pool.sem_inc(s["consts"], 1)
            pool.wait_ge(s["mk_ready"], 1)
            for c, name in ((0, "mem_k_prompt"), (1, "mem_v_prompt")):
                pool.dma_start(O[name][0, 0].rearrange("(t p) h d -> p t (h d)", p=P),
                               mkv[:, :, c * DC:(c + 1) * DC]).then_inc(s["mkv_stored"], 16)

            pool.wait_ge(s["attn_done"], 2)
            pool.wait_ge(s["qk_stored"], 64)
            with pool.Fori(0, TS // 2) as i:
                for par in range(2):
                    with pool.Fori(0, PAGES // 4) as j:
                        for k in range(4):
                            r = (2 * par + k) % 4
                            pool.wait_ge(s["vpage_used"], i * 36 + j * 4 + (18 * par + k + 1))
                            page = pool.value_load(pt[0:1, ds(i * 32 + j * 4 + (16 * par + k), 1)], min_val=0, max_val=POOL_PAGES - 1)
                            pool.dma_start(v_slots[r], cache_v[ds(page * PAGE, PAGE), :]).then_inc(v_landed[r], 16)
                    for t in range(2):
                        r = (2 * par + t) % 4
                        pool.wait_ge(s["vpage_used"], i * 36 + (18 * par + 16 + t + 1))
                        pool.dma_start(v_slots[r], cmem_v[ds(i * (2 * NM) + (par * NM + t * P), P), :]).then_inc(v_landed[r], 16)

            pool.wait_ge(s["vpage_used"], TS * PAGES + 2 * TS + 4)
            pool.dma_start(x_rows[:, 0:2, :], A["x_prompt"][0].rearrange("(t p) d -> p t d", p=P)).then_inc(s["x_again"], 16)
            pool.dma_start(x_rows[0:TS, 2, :], A["x_sample"].rearrange("b t d -> (b t) d")).then_inc(s["x_again"], 16)
            st(nc.gpsimd.iota(iota_i, pattern=[[1, TOPK]], base=0, channel_multiplier=0))
            pool.sem_inc(s["consts"], 1)
            pool.wait_ge(s["mkv_stored"], 32)
            pool.wait_ge(s["conv_stored"], 48)
            pool.wait_ge(s["sub_scaled"], 1)
            pool.dma_start(n2_w, A["norm2_w"][0:1, :].to_broadcast([P, D])).then_inc(s["n2_in"], 16)
            pool.dma_start(sk_rows, A["sub_keys"][0].rearrange("c k d -> k c d")).then_inc(s["sk_in"], 16)
            pool.wait_ge(s["h2_ready"], 1)
            pool.dma_start(h2_dram, h2_rows[0:TS, 2, :]).then_inc(s["h2_scratch"], 16)

            def gather(table, dst, idx, landed):
                pool.sem_inc(s["gather_turn"], 1)
                nc.gpsimd.indirect_dma_start(dst, None, table, bass.IndirectOffsetOnAxis(ap=idx, axis=0)).then_inc(landed, 16)

            def gather_u(par, g, j):
                pool.wait_ge(s["u_used"], g * TOPK + (j + 1))
                gather(peer_u, u_slots[j % 4], uidx[:, par, j:j + 1], u_landed[j % 4])

            def gather_v(par, g, j):
                pool.wait_ge(s["v_used"], g * TOPK + (j + 1))
                gather(peer_v, e_slots[j % 4], uidx[:, par, j:j + 1], e_landed[j % 4])

            def heads(i, par):
                pool.wait_ge(s["v_used"], i * 32 + (par * 16 + 4))
                st(nc.gpsimd.tensor_copy(uidx[:, 1 - par, :], idx_flat[:, ds(i * 32 + (par * 16 + 16), TOPK)]))
                for j in range(TOPK):
                    gather_u(1 - par, i * 2 + (par + 1), j)
                    gather_v(par, i * 2 + par, j)

            pool.wait_ge(s["idx_ready"], 1)
            st(nc.gpsimd.tensor_copy(uidx[:, 0, :], idx_flat[:, 0:TOPK]))
            for j in range(TOPK):
                gather_u(0, 0, j)
            with st.loop(3, 2) as i:
                for par in range(2):
                    heads(i, par)
            pool.wait_ge(s["idx_ready"], 2)
            with st.loop(4, 2) as i:
                for par in range(2):
                    heads(i + 3, par)
            heads(7, 0)
            pool.wait_ge(s["idx_ready"], 4)
            pool.wait_ge(s["h2_scratch"], 16)
            for j in range(TOPK):
                gather_v(1, 15, j)
                if j % 2:
                    b = j // 2
                    pool.wait_ge(s["hb_used"], b + 1)
                    pool.dma_start(hb[b % 2], h2_dram[b:b + 1, :].to_broadcast([P, D])).then_inc(hb_landed[b % 2], 16)
                    pool.wait_ge(s["u_used"], 2 * P + b + 1)
                    gather(peer_u, u_slots[b % 4], sidx[:, b:b + 1], u_landed[b % 4])
            for b in range(TS):
                pool.wait_ge(s["v_used"], 2 * P + b + 1)
                gather(peer_v, e_slots[b % 4], sidx[:, b:b + 1], e_landed[b % 4])
            pool.wait_ge(s["qk_stored"], 64)

        @block.tensor
        def _(pe):
            mm = nc.tensor.matmul

            pe.wait_ge(s["consts"], 1)
            pe.wait_ge(s["cols_in"], 48)
            nc.tensor.transpose(ps[:, 0, 0:56], colrows, ident[0:56, 0:56]).then_inc(s["cols_full"], 1)
            pe.wait_ge(s["st_in"], 16)
            for j in range(BC):
                last = nc.tensor.transpose(ps[:, 1, j * 16:(j + 1) * 16], ring4[0:16, 0, j * P:(j + 1) * P], ident[0:16, 0:16])
            last.then_inc(s["st_full"], 1)

            def transpose_rows(src, k, bank, tiles):
                for t, (first, n) in enumerate(tiles):
                    last = nc.tensor.transpose(ps[:, bank, first:first + n], src[0:n, t, k * P:(k + 1) * P], ident[0:n, 0:n])
                return last

            pe.wait_ge(s["x_scaled"], 1)
            for k in range(KC):
                if k >= 4:
                    pe.wait_ge(s["xT_taken"], k - 3)
                transpose_rows(x_rows, k, 4 + k % 4, TILES).then_inc(s["xT_full"], 1)
            pe.wait_ge(s["x_scaled"], 2)
            for k in range(KC):
                pe.wait_ge(s["xT_taken"], KC + k - 3)
                transpose_rows(h2_rows, k, 4 + k % 4, TILES[0:2]).then_inc(s["xT_full"], 1)
            pe.wait_ge(s["xT_taken"], 2 * KC)

            def chunk(r, c, n, rhs):
                pe.wait_ge(s["chunk_taken"], n + 1)
                for k in range(KC):
                    last = mm(ps[:, (2 * r + c) % 4, 0:NT], wring[:, r, k, c * P:(c + 1) * P], rhs[:, k, :], start=(k == 0), stop=(k == KC - 1))
                last.then_inc(s["chunk_full"], 1)

            def linear(g0, n_blocks, c0, rhs, turn=None):
                with pe.Fori(0, n_blocks // NR) as i:
                    for r in range(NR):
                        pe.wait_ge(w_landed[r], i * 16 + 16 * (g0 // NR + 1))
                        for c in range(2):
                            q = 2 * r + c
                            chunk(r, c, i * (2 * NR) + (c0 + q), rhs)
                            if turn and q:
                                turn(q - 1, i * (2 * NR) + (q - 1))
                    if turn:
                        turn(2 * NR - 1, i * (2 * NR) + (2 * NR - 1))

            def turner(c0, m0):
                def turn(q, m):
                    pe.wait_ge(s["chunk_taken"], m + (c0 + 4 + 1))
                    pe.wait_ge(s["rows_taken"], m + (m0 + 1))
                    for t, (first, n) in enumerate(TILES):
                        last = nc.tensor.transpose(ps[0:n, 4 + q % 2, t * P:(t + 1) * P], zst[:, q % 2, first:first + n], ident[:, :])
                    last.then_inc(s["tr_full"], 1)
                return turn

            linear(G_QKV, 16, C_QKV, hT, turner(C_QKV, R_QKV))
            linear(G_CONV, 12, C_CONV, hT)
            def conv_state():
                pe.wait_ge(s["conv_ready"], 1)
                pe.wait_ge(s["rows_taken"], 32 + 2)
                for j in range(BC):
                    last = nc.tensor.transpose(ps[0:2 + TS, 4 + j // 4, (j % 4) * P:(j % 4 + 1) * P], conv[:, BC + j, TP - 2:NT], ident[:, :])
                last.then_inc(s["cs_full"], 1)

            def own_scores():
                pe.wait_ge(s["self_in"], 1)
                mm(ps[:, 4, 0:P], ones[0:TS, :], small[0:TS, 0, :], start=True, stop=True).then_inc(s["self_full"], 1)

            def turn_maxima(m, n):
                pe.wait_ge(s["max_full"], m + 1)
                nc.tensor.transpose(ps[0:n, 5, 0:P], small[:, 1, 0:n], ident[:, :]).then_inc(s["max_diag"], 1)

            def spread_maxima(m, n):
                pe.wait_ge(s["mb_full"], m + 1)
                mm(ps[:, 6, 0:n], ones[0:n, :], small[0:n, 2, 0:n], start=True, stop=True).then_inc(s["max_diag"], 1)

            def sum_partitions(m, n):
                pe.wait_ge(s["sum_in"], m + 1)
                mm(ps[:, 7, 0:n], ones[:, :], small[:, 1, 0:n], start=True, stop=True).then_inc(s["sum_full"], 1)

            nk, nm = P, TS * MH
            after = {1: (conv_state,), 2: (own_scores,), 4: (turn_maxima, 0, nk), 5: (spread_maxima, 0, nk), 8: (sum_partitions, 0, nk),
                     10: (turn_maxima, 1, nm), 11: (spread_maxima, 1, nm), 13: (sum_partitions, 1, nm)}
            for g in range(8):
                pe.wait_ge(w_landed[g % NR], 16 * ((G_MEM + g) // NR + 1))
                for t in range(2):
                    n = 2 * g + t
                    pe.wait_ge(s["chunk_taken"], C_MEM + n + 1)
                    for k in range(KC):
                        last = mm(ps[:, n % 4, 0:BLK], memT[:, k, t * P:(t + 1) * P], wring[:, g % NR, k, :], start=(k == 0), stop=(k == KC - 1))
                    last.then_inc(s["chunk_full"], 1)
                    if n in after:
                        after[n][0](*after[n][1:])
            pe.wait_ge(s["chunk_taken"], C_O + 4)
            pe.wait_ge(s["a_ready"], 1)

            def flat(u):
                b = 4 - 4 * u
                return ps[:, b:b + 4, :].rearrange("p a b -> p (a b)")

            def attention(n_heads, base, w):
                halves = w // P
                a0 = 1536
                s0 = 512 * halves
                with pe.Fori(0, n_heads // 2) as i:
                    for u in range(2):
                        pe.wait_ge(s["attn_staged"], i * 2 + (base + u + 1))
                        for o in range(2):
                            for f in range(halves):
                                for t in range(2):
                                    last = nc.tensor.transpose(
                                        flat(u)[:, (o * halves + f) * 256 + t * P:(o * halves + f) * 256 + (t + 1) * P],
                                        temp[u][:, (2 * o + t) * w + f * P:(2 * o + t) * w + (f + 1) * P], ident[:, :])
                        last.then_inc(s["tt_full"], 1)
                    for u in range(2):
                        pe.wait_ge(s["qk_T"], i * 2 + (base + u + 1))
                        T = temp[u][:, 6 * w:6 * w + 1024]
                        for t in range(2):
                            if halves == 1:
                                for c in range(2):
                                    last = mm(flat(u)[:, s0 + (2 * c + t) * 256:s0 + (2 * c + t + 1) * 256],
                                              T[c * DK:(c + 1) * DK, t * P:(t + 1) * P], T[c * DK:(c + 1) * DK, 256:512], start=True, stop=True)
                            else:
                                for f in range(2):
                                    last = mm(flat(u)[:, s0 + t * 256:s0 + (t + 1) * 256], T[:, f * 256 + t * P:f * 256 + (t + 1) * P],
                                              T[:, 512 + f * 256:512 + (f + 1) * 256], start=(f == 0), stop=(f == 1))
                        last.then_inc(s["s_full"], 1)
                    for u in range(2):
                        pe.wait_ge(s["p_ready"], i * 2 + (base + u + 1))
                        p0, step = (6 * w + 512, 512) if halves == 1 else (6 * w + 1024, 256)
                        for k in range(2):
                            for t in range(2):
                                last = nc.tensor.transpose(flat(u)[:, a0 + k * 256 + t * P:a0 + k * 256 + (t + 1) * P],
                                                           temp[u][:, p0 + t * step + k * P:p0 + t * step + (k + 1) * P], ident[:, :])
                        last.then_inc(s["at_full"], 1)
                    for u in range(2):
                        pe.wait_ge(s["at_ready"], i * 2 + (base + u + 1))
                        t0 = 6 * w + 512 + 1024 if halves == 1 else 6 * w + 1024 + 512
                        for f in range(halves):
                            for k in range(2):
                                last = mm(flat(u)[:, a0 + f * 256:a0 + (f + 1) * 256], temp[u][:, 4 * w + k * w + f * P:4 * w + k * w + (f + 1) * P],
                                          temp[u][:, t0 + k * 256:t0 + (k + 1) * 256], start=(k == 0), stop=(k == 1))
                        last.then_inc(s["o_full"], 1)

            attention(HEADS, 0, DV)
            attention(MH, HEADS, MD)
            pe.wait_ge(s["attn_done"], 2)

            pe.wait_ge(s["merge_zero"], 1)
            mm(ps[:, 4, 0:P], mask0, mask0, start=True, stop=False, skip_group_check=True)

            def own_value():
                for h in range(HEADS):
                    mm(ps[:, 4, h:TS * HEADS:HEADS], rows[0:TS, 2, 2 * DC + h * DV:2 * DC + (h + 1) * DV],
                       selfA[0:TS, h, :], start=False, stop=False, skip_group_check=True)
            own_value()

            def value_page(i, par, j, k):
                r = (2 * par + k) % 4
                b = i * 2 + par
                pe.wait_ge(v_landed[r], i * (9 * 16) + j * 16 + 16 * ((18 * par + k) // 4 + 1))
                for h in range(HEADS):
                    last = mm(ps[:, 4, ds(b * HEADS + h, 1)], v_slots[r][:, h * DV:(h + 1) * DV],
                              Ad_f[:, ds(b * (PAGES * HEADS) + j * (4 * HEADS) + (k * HEADS + h), 1)], start=False, stop=False, skip_group_check=True)
                last.then_inc(s["vpage_used"], 1)

            def value_mem(i, par, t):
                r = (2 * par + t) % 4
                b = i * 2 + par
                pe.wait_ge(v_landed[r], i * (9 * 16) + 16 * ((18 * par + 16 + t) // 4 + 1))
                for h in range(MH):
                    for f in range(2):
                        last = mm(ps[:, 4, ds(b * BC + (64 + 2 * h + f), 1)], v_slots[r][:, h * MD + f * P:h * MD + (f + 1) * P],
                                  Sm_f[:, ds(b * (2 * MH) + (t * MH + h), 1)], start=False, stop=False, skip_group_check=True)
                last.then_inc(s["vpage_used"], 1)

            for b, operand in enumerate((conv[:, 0:BC, :], oT_mem, oT_diff)):
                if b:
                    pe.wait_ge(s["vo_ready" if b == 1 else "sub_scaled"], 1)
                with pe.Fori(0, 8 // NR) as i:
                    for r in range(NR):
                        g = G_GATE // NR + b * (8 // NR)
                        pe.wait_ge(w_landed[r], i * 16 + 16 * (g + 1))
                        pe.wait_ge(bw_landed[r], i * 16 + 16 * (b * (8 // NR) + 1))
                        for c in range(2):
                            q = i * (2 * NR) + (16 * b + 2 * r + c)
                            pe.wait_ge(s["gate_done"], q + 1)
                            for k in range(KC):
                                last = mm(ps[:, c, 0:NT], wring[:, r, k, c * P:(c + 1) * P], hT[:, k, :], start=(k == 0), stop=(k == KC - 1))
                            last.then_inc(s["gate_full"], 1)
                            pe.wait_ge(s["y_taken"], q + 1)
                            for k in range(BC):
                                last = mm(ps[:, 2 + c, 0:NT], bwring[:, r, k, c * P:(c + 1) * P], operand[:, k, :], start=(k == 0), stop=(k == BC - 1))
                            last.then_inc(s["y_full"], 1)
                            if b == 0:
                                with pe.Fori(2 * c, 2 * c + 2) as j:
                                    for k in range(4):
                                        value_page(i, r, j, k)
                                if c:
                                    value_mem(i, r, 0)
                                    value_mem(i, r, 1)
                if b == 0:
                    mm(ps[:, 4, 0:P], mask0, mask0, start=False, stop=True, skip_group_check=True).then_inc(s["vo_full"], 1)
                if b == 1:
                    pe.wait_ge(s["sub_in"], 1)
                    for h in range(HEADS):
                        if h >= 4:
                            pe.wait_ge(s["sub_taken"], h - 3)
                        mm(ps[:, 4 + h % 4, 0:NT], ones[:, :], sq_mkv[:, h * NT:(h + 1) * NT], start=True, stop=True).then_inc(s["sub_full"], 1)

            pe.wait_ge(s["merge_ready"], 1)
            linear(G_O, 8, C_O, merged, turner(C_O, R_O))
            pe.wait_ge(s["x1_ready"], 1)
            for k in range(KC):
                if k >= 4:
                    pe.wait_ge(s["h2T_taken"], k - 3)
                transpose_rows(h2_rows, k, 4 + k % 4, TILES).then_inc(s["h2T_full"], 1)
            pe.wait_ge(s["h2T_taken"], KC)
            pe.wait_ge(s["sk_in"], 16)
            for c in range(2):
                last = nc.tensor.transpose(ps[:, 6, c * P:(c + 1) * P], sk_rows[:, c, :], ident[:, :])
            last.then_inc(s["sk_full"], 1)
            pe.wait_ge(s["sk_ready"], 1)

            def score(q, m):
                pe.wait_ge(s["chunk_taken"], m + (C_PQ + 4 + 1))
                pe.wait_ge(s["rows_taken"], m + (R_PQ + 1))
                for t, (first, n) in enumerate(TILES):
                    last = mm(ps[0:n, 4 + q % 2, t * P:(t + 1) * P], zst[:, q % 2, first:first + n], skT[:, q % 2, :], start=True, stop=True)
                last.then_inc(s["tr_full"], 1)

            linear(G_PQ, 8, C_PQ, hT, score)
            pe.wait_ge(s["rows_taken"], 64 + 2)
            pe.wait_ge(s["chunk_taken"], 104 + 4)

            pe.wait_ge(s["zero_ready"], 1)

            def add_zero(t, start, stop):
                n = TILES[t][1]
                for q in range(4):
                    last = mm(ps[0:n, 4 * (t % 2) + q, :], zero512[:, 0:n], zero512, start=start, stop=stop, skip_group_check=True)
                return last

            def add_heads(g0, n):
                bank = 4 * (g0 // PH)
                with pe.Fori(0, n) as g:
                    for j in range(TOPK):
                        pe.wait_ge(s["diag_ready"], g * TOPK + (g0 * TOPK + j + 1))
                        pe.wait_ge(e_landed[j % 4], g * 64 + 16 * (g0 * 4 + j // 4 + 1))
                        for q in range(4):
                            last = mm(ps[:, bank + q, :], diag[:, j % 4, :], e_slots[j % 4][:, q * 512:(q + 1) * 512], start=False, stop=False, skip_group_check=True)
                        last.then_inc(s["v_used"], 1)

            add_zero(0, True, False)
            add_heads(0, 5)
            pe.wait_ge(s["sT_in"], 1)
            nc.tensor.transpose(ps[:, 4, 0:TS], idx_f[0:TS, :], ident[0:TS, 0:TS])
            nc.tensor.transpose(ps[:, 4, TS:2 * TS], gates[0:TS, 2, :], ident[0:TS, 0:TS]).then_inc(s["sT_full"], 1)
            add_heads(5, 3)
            add_zero(0, False, True).then_inc(s["yo_full"], 1)
            pe.wait_ge(s["idx_ready"], 4)
            add_zero(1, True, False)
            add_heads(8, 8)
            add_zero(1, False, True).then_inc(s["yo_full"], 1)
            pe.wait_ge(s["y_ready"], 1)
            add_zero(2, True, False)
            pe.wait_ge(s["w_ready"], 17)
            for b in range(TS):
                pe.wait_ge(e_landed[b % 4], 16 * (64 + b // 4 + 1))
                for q in range(4):
                    last = mm(ps[0:TS, q, :], wz[:, b, :], e_slots[b % 4][:, q * 512:(q + 1) * 512], start=False, stop=False, skip_group_check=True)
                last.then_inc(s["v_used"], 1)
            add_zero(2, False, True).then_inc(s["yo_full"], 1)

        @block.scalar
        def _(act):
            st = Steps(act, s["act_done"])
            A_ = nc.scalar.activation
            act.sem_inc(s["chunk_taken"], 4)
            act.sem_inc(s["gate_done"], 2)
            junk = cflat[:, 0:D]

            def square_sums(tiles):
                for col, src, n in tiles:
                    st(A_(junk[0:n], src, ACT.Square, accum_out=stat[0:n, col:col + 1]))

            def root(n, ap):
                act.wait_ge(s["sqrt_in"], n)
                st(A_(ap, ap, ACT.Sqrt))
                act.sem_inc(s["sqrt_out"], 1)

            act.wait_ge(s["x_clear"], 1)
            act.wait_ge(s["x_in"], 32)
            square_sums([(t, x_rows[0:n, t, :], n) for t, (_, n) in enumerate(TILES)])
            act.wait_ge(s["mem_in"], 16)
            square_sums([(3 + t, h2_rows[:, t, :], P) for t in range(2)])
            act.sem_inc(s["x_ss"], 1)
            root(1, stat[:, 0:5])
            act.wait_ge(s["lam_pre"], 1)
            st(A_(lam[:, 0:2], lam[:, 0:2], ACT.Exp))
            act.sem_inc(s["lam_exp"], 1)
            act.wait_ge(s["cols_ready"], 1)
            for k in range(2 * KC):
                act.wait_ge(s["xT_full"], k + 1)
                if k < KC:
                    st(A_(hT[:, k, :], ps[:, 4 + k % 4, 0:NT], ACT.Copy, scale=cols[:, k:k + 1]))
                else:
                    st(A_(memT[:, k - KC, :], ps[:, 4 + k % 4, 0:NM], ACT.Copy, scale=cols[:, k:k + 1]))
                act.sem_inc(s["xT_taken"], 1)

            def to_stage(n_chunks, c0, m0):
                with st.loop(n_chunks // 4, 4) as i:
                    for q in range(4):
                        act.wait_ge(s["chunk_full"], i * 4 + (c0 + q + 1))
                        act.wait_ge(s["rows_taken"], i * 4 + (m0 + q + 1))
                        st(A_(zst[:, q % 2, :], ps[:, q, 0:NT], ACT.Copy))
                        act.sem_inc(s["chunk_taken"], 1)

            to_stage(8, C_QKV, R_QKV)
            root(2, small[:, 3, 0:48])
            act.wait_ge(s["rows_taken"], 2 + 8)
            with st.loop(6, 12) as i:
                for q in range(4):
                    n = i * 4 + (8 + q)
                    act.wait_ge(s["chunk_full"], n + 1)
                    st(A_(zst[:, q % 2, :], ps[:, q, 0:NT], ACT.Copy))
                    act.sem_inc(s["chunk_taken"], 1)
                    act.wait_ge(s["tr_full"], n + 1)
                    at = ds(i * (4 * P) + (DC + q * P), P)
                    st.run(A_(rows[:, 0:2, at], ps[:, 4 + q % 2, 0:2 * P].rearrange("p (t n) -> p t n", t=2), ACT.Copy))
                    st(A_(rows[0:TS, 2, at], ps[0:TS, 4 + q % 2, 2 * P:3 * P], ACT.Copy))
                    act.sem_inc(s["rows_taken"], 1)

            def conv_chunks(i0, n):
                with st.loop(n, 4) as i:
                    for q in range(4):
                        act.wait_ge(s["chunk_full"], i * 4 + (C_CONV + 4 * i0 + q + 1))
                        st(A_(cflat[:, ds(i * (4 * NT) + (4 * i0 + q) * NT, NT)], ps[:, q, 0:NT], ACT.Copy))
                        act.sem_inc(s["chunk_taken"], 1)

            conv_chunks(0, 4)
            root(3, small[:, 3, 0:60])
            conv_chunks(4, 2)
            act.wait_ge(s["q_ready"], 2)
            for n in range(16):
                act.wait_ge(s["chunk_full"], C_MEM + n + 1)
                st(A_(mkv[:, n % 2, (n // 2) * BLK:(n // 2 + 1) * BLK], ps[:, n % 4, 0:BLK], ACT.Copy))
                act.sem_inc(s["chunk_taken"], 1)
                if n == 6:
                    act.wait_ge(s["exp_in"], 1)
                    st.run(A_(work, work, ACT.Exp, scale=DK ** -0.5))
                    st(A_(small[:, 0, :], small[:, 0, :], ACT.Exp, scale=DK ** -0.5))
                    act.sem_inc(s["exp_out"], 1)
                if n == 11:
                    act.wait_ge(s["exp_in"], 2)
                    st(A_(Sm_f, Sm_f, ACT.Exp, scale=MD ** -0.5))
                    act.sem_inc(s["exp_out"], 1)
            root(4, small[:, 3, 0:8])

            def flat(u):
                b = 4 - 4 * u
                return ps[:, b:b + 4, :].rearrange("p a b -> p (a b)")

            def attention(n_heads, base, w, srcs, out, n_rows, scale):
                T0 = 6 * w
                tt = 512 * (w // P)
                with st.loop(n_heads // 2, 2 * (3 + 1 + n_rows + 1 + 1)) as i:
                    for u in range(2):
                        for o, (src, col) in enumerate(srcs):
                            st.run(A_(temp[u][:, 2 * o * w:(2 * o + 2) * w].rearrange("p (t n) -> p t n", t=2),
                                      src[:, 0:2, ds(i * (2 * w) + (col + u * w), w)], ACT.Copy))
                        st.settle()
                        act.sem_inc(s["attn_staged"], 1)
                    for u in range(2):
                        act.wait_ge(s["tt_full"], i * 2 + (base + u + 1))
                        st(A_(temp[u][:, T0:T0 + tt], flat(u)[:, 0:tt], ACT.Copy))
                        act.sem_inc(s["qk_T"], 1)
                    for u in range(2):
                        act.wait_ge(s["sm_ready"], i * 2 + (base + u + 1))
                        for n in range(n_rows):
                            dst = temp[u][:, T0 + tt + n * 256:T0 + tt + (n + 1) * 256]
                            src = dst if n_rows == 4 else flat(u)[:, tt + n * 256:tt + (n + 1) * 256]
                            st.run(A_(dst, src, ACT.Exp, scale=scale, bias=stat[:, 16 * u + 4 + n:16 * u + 5 + n],
                                      accum_out=stat[:, 16 * u + 8 + n:16 * u + 9 + n]))
                        st.settle()
                        act.sem_inc(s["exp_ready"], 1)
                    for u in range(2):
                        act.wait_ge(s["at_full"], i * 2 + (base + u + 1))
                        st(A_(temp[u][:, T0 + 1536:T0 + 2048], flat(u)[:, 1536:2048], ACT.Copy))
                        act.sem_inc(s["at_ready"], 1)
                    for u in range(2):
                        act.wait_ge(s["o_full"], i * 2 + (base + u + 1))
                        c = w // P
                        st(A_(out[:, ds(i * (2 * c) + u * c, c), 0:TP], flat(u)[:, 1536:1536 + 256 * c].rearrange("p (a b) -> p a b", a=c), ACT.Copy))
                act.sem_inc(s["attn_done"], 1)

            qkv = [(rows, 0), (rows, DC), (rows, 2 * DC)]
            act.wait_ge(s["mk_ready"], 1)
            attention(HEADS, 0, DV, qkv, oT_diff, 4, DK ** -0.5)
            attention(MH, HEADS, MD, [(rows, 3 * DC), (mkv, 0), (mkv, DC)], oT_mem, 2, MD ** -0.5)

            for b in range(3):
                with st.loop(4, 4) as i:
                    for q in range(4):
                        act.wait_ge(s["gate_full"], i * 4 + (16 * b + q + 1))
                        act.wait_ge(s["y_taken"], i * 4 + (16 * b + q + 1))
                        st(A_(sg[:, q % 2, :], ps[:, q % 2, 0:NT], ACT.Sigmoid))
                        act.sem_inc(s["gate_done"], 1)
                if b == 1:
                    root(5, sq_mkv[:, 0:BC * NT])

            to_stage(16, C_O, R_O)
            act.wait_ge(s["x1_rows"], 1)
            square_sums([(t, x_rows[0:n, t, :], n) for t, (_, n) in enumerate(TILES)])
            act.sem_inc(s["n2_ss"], 1)
            root(6, stat[:, 0:3])
            for k in range(KC):
                act.wait_ge(s["h2T_full"], k + 1)
                st(A_(hT[:, k, :], ps[:, 4 + k % 4, 0:NT], ACT.Copy))
                act.sem_inc(s["h2T_taken"], 1)
            to_stage(16, C_PQ, R_PQ)
            act.wait_ge(s["gate_in"], 1)
            st(A_(win_v, shifted.rearrange("p (t n) -> p t n", t=3), ACT.Exp))
            act.sem_inc(s["gate_out"], 1)

            with st.loop(2 * PH, 1 + TOPK) as g:
                act.wait_ge(s["a_in"], g + 1)
                st(A_(act_g[:, 0, :], act_a[:, 0, :], ACT.Gelu))
                act.sem_inc(s["a_out"], 1)
                act.wait_ge(s["w_ready"], g + 1)
                for j in range(TOPK):
                    act.wait_ge(s["v_used"], g * TOPK + (j + 1))
                    st(A_(diag[:, j % 4, :], ident[:, :], ACT.Copy, scale=wexp[:, 0, j:j + 1]))
                    act.sem_inc(s["diag_ready"], 1)
            act.wait_ge(s["a_in"], 2 * PH + 1)
            st(A_(act_g[:, 0, 0:TS], act_a[:, 0, 0:TS], ACT.Gelu))
            act.sem_inc(s["a_out"], 1)

        @block.vector
        def _(dve):
            st = Steps(dve, s["dve_done"])
            V = nc.vector
            TT, TSC, STT, CP, RED, REC = V.tensor_tensor, V.tensor_scalar, V.scalar_tensor_tensor, V.tensor_copy, V.tensor_reduce, V.reciprocal

            def signal(name, n=1):
                dve.sem_inc(s[name], n)

            def root(n):
                signal("sqrt_in")
                dve.wait_ge(s["sqrt_out"], n)

            signal("rows_taken", 2)
            signal("y_taken", 2)
            st(V.memset(stat[:, :], 1.0))
            signal("x_clear")
            dve.wait_ge(s["lam_in"], 64)
            st(TT(lam4[:, 0, :], lam4[:, 0, :], lam4[:, 1, :], ALU.mult))
            st(TT(lam4[:, 2, :], lam4[:, 2, :], lam4[:, 3, :], ALU.mult))
            st(RED(lam[:, 0:1], lam4[:, 0, :], X, ALU.add))
            st(RED(lam[:, 1:2], lam4[:, 2, :], X, ALU.add))
            signal("lam_pre")
            dve.wait_ge(s["cols_full"], 1)
            st.run(CP(cols[:, :], ps[:, 0, 0:56]))
            dve.wait_ge(s["st_full"], 1)
            st(CP(stT[:, :, :], ps[:, 1, 0:P].rearrange("p (a b) -> p a b", a=BC)))
            signal("cols_ready")

            dve.wait_ge(s["x_ss"], 1)
            st(TSC(stat[:, 0:5], stat[:, 0:5], 1.0 / D, EPS, ALU.mult, ALU.add))
            root(1)
            st(REC(stat[:, 0:5], stat[:, 0:5]))
            for t, (_, n) in enumerate(TILES):
                st.run(TSC(x_rows[0:n, t, :], x_rows[0:n, t, :], stat[0:n, t:t + 1], None, ALU.mult))
            st.settle()
            signal("x_scaled")
            for t in range(2):
                st.run(TSC(h2_rows[:, t, :], h2_rows[:, t, :], stat[:, 3 + t:4 + t], None, ALU.mult))
            st.settle()
            signal("x_scaled")
            dve.wait_ge(s["lam_exp"], 1)
            st(TT(lam[:, 2:3], lam[:, 1:2], lam[:, 0:1], ALU.subtract))
            st(TSC(lam[:, 3:4], lam[:, 2:3], LAM_INIT, None, ALU.subtract))

            dve.wait_ge(s["xT_full"], 2 * KC)
            st(V.memset(rows[:, 2, :], 0.0))

            def rows_from(n_chunks, m0, out, add=False):
                with st.loop(n_chunks // 4, 8) as i:
                    for q in range(4):
                        dve.wait_ge(s["tr_full"], i * 4 + (m0 + q + 1))
                        at = ds(i * (4 * P) + q * P, P)
                        src = ps[:, 4 + q % 2, 0:2 * P].rearrange("p (t n) -> p t n", t=2)
                        own = ps[0:TS, 4 + q % 2, 2 * P:3 * P]
                        if add:
                            st.run(TT(out[:, 0:2, at], src, out[:, 0:2, at], ALU.add))
                            st(TT(out[0:TS, 2, at], own, out[0:TS, 2, at], ALU.add))
                        else:
                            st.run(CP(out[:, 0:2, at], src))
                            st(CP(out[0:TS, 2, at], own))
                        signal("rows_taken")

            rows_from(8, R_QKV, rows)

            dve.wait_ge(s["small_in"], 80)
            dve.wait_ge(s["rope_in"], 16)
            r_ = small[:, 3, :]

            def row_norms(groups, area, n_root):
                sq3 = area[:, 0:3 * DC].rearrange("p (t n) -> p t n", t=3)
                at = 0
                spans = []
                for c, g, w, _ in groups:
                    part = rows[:, :, c:c + DC]
                    st(TT(sq3, part, part, ALU.mult))
                    r = r_[:, at:at + 3 * g]
                    st(RED(r, area[:, 0:3 * DC].rearrange("p (g w) -> p g w", w=w), X, ALU.add))
                    st(TSC(r, r, 1.0 / w, EPS, ALU.mult, ALU.add))
                    spans.append(r)
                    at += 3 * g
                root(n_root)
                st(REC(r_[:, 0:at], r_[:, 0:at]))
                for (c, g, w, wt), r in zip(groups, spans):
                    part = rows[:, :, c:c + DC].rearrange("p t (g w) -> p t g w", w=w)
                    rr = r.rearrange("p (t g) -> p t g", t=3).unsqueeze(3).broadcast_to([P, 3, g, w])
                    st(TT(part, part, rr, ALU.mult))
                    for t in range(3):
                        st.run(TT(part[:, t], part[:, t], wt[:, :].unsqueeze(1).broadcast_to([P, g, w]), ALU.mult))
                    st.settle()
                    if w == DK:
                        cos, sin = [rope[:, :, 8 * h:8 * h + 8].unsqueeze(2).broadcast_to([P, 3, g, 8]) for h in range(2)]
                        x1, x2 = part[:, :, :, 0:8], part[:, :, :, 8:16]
                        t4 = [area[:, 384 * n:384 * (n + 1)].rearrange("p (t g w) -> p t g w", t=3, g=g) for n in range(4)]
                        for n, (a, b) in enumerate(((x1, cos), (x2, sin), (x2, cos), (x1, sin))):
                            st.run(TT(t4[n], a, b, ALU.mult))
                        st.settle()
                        st.run(TT(x1, t4[0], t4[1], ALU.subtract))
                        st(TT(x2, t4[2], t4[3], ALU.add))

            row_norms([(0, 16, DK, qn_w)], sq_mkv, 2)
            signal("q_ready")

            def score_group(i, g):
                half, par = g % 2, g // 4
                slots = kpages[4 * half:4 * half + 4]
                landed = i * 64 + 16 * (g // 2 + 1)
                out = lambda r: work[:, ds(i * 512 + (g * 64 + r * 16), 16)]
                by_head = lambda ap: ap.rearrange("p (g w) -> p g w", w=DK)
                k0 = st.k
                dve.wait_ge(k_landed[4 * half], landed)
                st.run(TT(prods[0], slots[0], qb[:, par, :], ALU.mult))
                dve.wait_ge(k_landed[4 * half + 2], landed)
                st.run(TT(prods[1], slots[2], qb[:, par, :], ALU.mult))
                st.reach(k0 + 1)
                signal("kpage_used")
                st.run(RED(out(0), by_head(prods[0]), X, ALU.add))
                dve.wait_ge(s["kprod_ready"], i * 16 + (2 * g + 1))
                st.run(RED(out(1), by_head(slots[1]), X, ALU.add))
                st.reach(k0 + 2)
                st.run(RED(out(2), by_head(prods[1]), X, ALU.add))
                st.reach(k0 + 4)
                signal("kpage_used", 2)
                dve.wait_ge(s["kprod_ready"], i * 16 + (2 * g + 2))
                st(RED(out(3), by_head(slots[3]), X, ALU.add))
                signal("kpage_used")

            with st.loop(TS // 2, 8 * 6) as i:
                for g in range(8):
                    if g % 4 == 0:
                        dve.wait_ge(qb_landed[g // 4], i * 16 + 16)
                        signal("loop_turn")
                    score_group(i, g)
                    if g % 4 == 3:
                        signal("token_done")

            dve.wait_ge(s["rows_taken"], 2 + 32)
            row_norms([(DC, 16, DK, kn_w), (3 * DC, 4, MD, mq_w)], ring_flat, 3)
            signal("q_ready")

            with st.loop(TS // 2, 8) as i:
                for par in range(2):
                    dve.wait_ge(qb_landed[par], i * 16 + (64 + 16))
                    for t in range(2):
                        dve.wait_ge(k_landed[2 * par + t], i * 16 + (16 * 16 + 16))
                        st(TT(prods[t], ring4[:, 2 * par + t, :], qb[:, par, :], ALU.mult))
                        signal("kpage_used")
                        st(RED(Sm_f[:, ds(i * 16 + (par * 8 + t * 4), 4)], prods[t].rearrange("p (g w) -> p g w", w=MD), X, ALU.add))
                    signal("token_done")

            dve.wait_ge(s["chunk_taken"], C_MEM + 4)
            st(TT(conv[:, BC:2 * BC, :], conv[:, BC:2 * BC, :], conv[:, 2 * BC:3 * BC, :], ALU.mult))
            for j in range(BC):
                u, y = conv[:, BC + j, :], conv[:, 2 * BC + j, :]
                w0, w1, w2 = [cols[:, 32 + 8 * n + j:33 + 8 * n + j] for n in range(3)]
                st(TSC(y, u, w2, None, ALU.mult))
                st(STT(y[:, 1:TP], u[:, 0:TP - 1], w1, y[:, 1:TP], ALU.mult, ALU.add))
                st(STT(y[:, 2:TP], u[:, 0:TP - 2], w0, y[:, 2:TP], ALU.mult, ALU.add))
                st(STT(y[:, TP:NT], stT[:, j, 1:2 * TS:2], w1, y[:, TP:NT], ALU.mult, ALU.add))
                st(STT(y[:, TP:NT], stT[:, j, 0:2 * TS:2], w0, y[:, TP:NT], ALU.mult, ALU.add))
            st(TT(conv[:, 0:BC, :], conv[:, 0:BC, :], conv[:, 2 * BC:3 * BC, :], ALU.mult))
            signal("conv_ready")

            b0, b1, b2, b3, b4 = [small[:, n, :] for n in range(5)]
            st(TT(prod[0:TS], rows[0:TS, 2, 0:DC], rows[0:TS, 2, DC:2 * DC], ALU.mult))
            st(RED(b4[0:TS, 0:16], prod[0:TS].rearrange("p (g w) -> p g w", w=DK), X, ALU.add))
            st(TT(b0[0:TS].rearrange("p (b c) -> p b c", b=TS), b4[0:TS, 0:16].unsqueeze(1).broadcast_to([TS, TS, 16]),
                  ident[0:TS, 0:TS].unsqueeze(2).broadcast_to([TS, TS, 16]), ALU.mult))
            dve.wait_ge(s["cs_full"], 1)
            st(CP(cs_rows[0:2 + TS, :].rearrange("p (a b) -> p a b", a=2), ps[0:2 + TS, 4:6, :]))
            signal("cs_rows")
            signal("self_in")
            by_page = S[:, :, :, :].rearrange("p b g c -> p b c g")
            c3 = lambda ap: ap.rearrange("p (b c) -> p b c", b=TS)
            st(RED(c3(b1), by_page, X, ALU.max))
            dve.wait_ge(s["self_full"], 1)
            st(CP(b0, ps[:, 4, 0:P]))
            st(TT(b1, b1, b0, ALU.max))

            def all_max(m, n):
                signal("max_full")
                dve.wait_ge(s["max_diag"], 2 * m + 1)
                st(RED(stat[0:n, 40:41], ps[0:n, 5, 0:P], X, ALU.max))
                st(TSC(b2[0:n, 0:n], ident[0:n, 0:n], stat[0:n, 40:41], None, ALU.mult))
                signal("mb_full")
                dve.wait_ge(s["max_diag"], 2 * m + 2)
                st(CP(b3[:, 0:n], ps[:, 6, 0:n]))

            all_max(0, P)
            over_pages = lambda ap: c3(ap).unsqueeze(2).broadcast_to([P, TS, PAGES, 16])
            st.run(TT(S[:, :, :, :], S[:, :, :, :], over_pages(b3), ALU.subtract))
            st(TT(b0, b0, b3, ALU.subtract))
            signal("exp_in")
            dve.wait_ge(s["exp_out"], 1)
            st(RED(c3(b1), by_page, X, ALU.add))
            signal("sum_in")
            dve.wait_ge(s["sum_full"], 1)
            st(TT(b1, ps[:, 7, 0:P], b0, ALU.add))
            st(REC(b1, b1))
            odd = b1.rearrange("p (a c) -> p a c", c=2)[:, :, 1:2]
            st(TSC(odd, odd, lam[:, 3:4], None, ALU.mult))
            st.run(TT(S[:, :, :, :], S[:, :, :, :], over_pages(b1), ALU.mult))
            st(TT(b0, b0, b1, ALU.mult))
            pairs = work.rearrange("p (a c) -> p a c", c=2)
            ob = b0.rearrange("p (a c) -> p a c", c=2)
            st(TT(b4[:, 0:64].unsqueeze(2), ob[:, :, 0:1], ob[:, :, 1:2], ALU.add))
            st(TT(selfA[0:TS], b4[0:TS, 0:64].rearrange("p (b h) -> p h b", b=TS),
                  ident[0:TS, 0:TS].unsqueeze(1).broadcast_to([TS, HEADS, TS]), ALU.mult))

            mem3 = Sm[:, :, :, :]
            n = TS * MH
            m3 = b1[:, 0:n].rearrange("p (b h) -> p b h", b=TS)
            st(TT(m3, mem3[:, :, 0, :], mem3[:, :, 1, :], ALU.max))
            all_max(1, n)
            over_m = lambda ap: ap[:, 0:n].rearrange("p (b h) -> p b h", b=TS).unsqueeze(2).broadcast_to([P, TS, 2, MH])
            st(TT(mem3, mem3, over_m(b3), ALU.subtract))
            signal("exp_in")
            dve.wait_ge(s["exp_out"], 2)
            st(TT(m3, mem3[:, :, 0, :], mem3[:, :, 1, :], ALU.add))
            signal("sum_in")
            dve.wait_ge(s["sum_full"], 2)
            st(REC(b1[:, 0:n], ps[:, 7, 0:n]))
            st(TT(mem3, mem3, over_m(b1), ALU.mult))
            dve.wait_ge(s["conv_stored"], 48)
            st(TT(cs_rows.unsqueeze(2), pairs[:, :, 0:1], pairs[:, :, 1:2], ALU.add))
            signal("a_ready")

            dve.wait_ge(s["chunk_taken"], C_O + 4)
            sqm = oflat[:, 0:D].rearrange("p (t n) -> p t n", t=2)
            mk = mkv[:, :, 0:DC]
            st(TT(sqm, mk, mk, ALU.mult))
            st(RED(b3[:, 0:8], oflat[:, 0:D].rearrange("p (g w) -> p g w", w=MD), X, ALU.add))
            st(TSC(b3[:, 0:8], b3[:, 0:8], 1.0 / MD, EPS, ALU.mult, ALU.add))
            root(4)
            st(REC(b3[:, 0:8], b3[:, 0:8]))
            mk4 = mk.rearrange("p t (g w) -> p t g w", w=MD)
            st(TT(mk4, mk4, b3[:, 0:8].rearrange("p (t g) -> p t g", t=2).unsqueeze(3).broadcast_to([P, 2, 4, MD]), ALU.mult))
            for t in range(2):
                st.run(TT(mk4[:, t], mk4[:, t], mk_w[:, :].unsqueeze(1).broadcast_to([P, 4, MD]), ALU.mult))
            st.settle()
            signal("mk_ready")

            dve.wait_ge(s["consts"], 2)

            def flat(u):
                b = 4 - 4 * u
                return ps[:, b:b + 4, :].rearrange("p a b -> p (a b)")

            with st.loop(HEADS // 2, 2 * 3 + 2 * 6) as i:
                for u in range(2):
                    sm = temp[u][:, 6 * DV + 512:6 * DV + 1536]
                    v4 = lambda ap: ap.rearrange("p (t c n) -> p t c n", t=2, c=2)
                    dve.wait_ge(s["s_full"], i * 2 + (u + 1))
                    st(TT(v4(sm), flat(u)[:, 512:1536].rearrange("p (c t n) -> p t c n", t=2, c=2), mask[:, :, :].unsqueeze(2).broadcast_to([P, 2, 2, TP]), ALU.add))
                    st(RED(stat[:, 16 * u:16 * u + 4], sm.rearrange("p (a n) -> p a n", a=4), X, ALU.max))
                    st(TSC(stat[:, 16 * u + 4:16 * u + 8], stat[:, 16 * u:16 * u + 4], -DK ** -0.5, None, ALU.mult))
                    signal("sm_ready")
                for u in range(2):
                    sm = temp[u][:, 6 * DV + 512:6 * DV + 1536]
                    r4 = stat[:, 16 * u + 12:16 * u + 16]
                    dve.wait_ge(s["exp_ready"], i * 2 + (u + 1))
                    st(REC(r4, stat[:, 16 * u + 8:16 * u + 12]))
                    st(TSC(r4[:, 1:4:2], r4[:, 1:4:2], lam[:, 3:4], None, ALU.mult))
                    for t in range(2):
                        a, b = sm[:, t * 512:t * 512 + 256], sm[:, t * 512 + 256:t * 512 + 512]
                        st(TSC(a, a, r4[:, 2 * t:2 * t + 1], None, ALU.mult))
                        st(STT(a, b, r4[:, 2 * t + 1:2 * t + 2], a, ALU.mult, ALU.add))
                    signal("p_ready")
            with st.loop(MH // 2, 2 * 2 + 2 * 3) as i:
                for u in range(2):
                    dve.wait_ge(s["s_full"], i * 2 + (HEADS + u + 1))
                    st(RED(stat[:, 16 * u:16 * u + 2], flat(u)[:, 1024:1536].rearrange("p (a n) -> p a n", a=2), X, ALU.max))
                    st(TSC(stat[:, 16 * u + 4:16 * u + 6], stat[:, 16 * u:16 * u + 2], -MD ** -0.5, None, ALU.mult))
                    signal("sm_ready")
                for u in range(2):
                    sm = temp[u][:, 6 * MD + 1024:6 * MD + 1536]
                    dve.wait_ge(s["exp_ready"], i * 2 + (HEADS + u + 1))
                    st(REC(stat[:, 16 * u + 12:16 * u + 14], stat[:, 16 * u + 8:16 * u + 10]))
                    for t in range(2):
                        st.run(TSC(sm[:, t * 256:(t + 1) * 256], sm[:, t * 256:(t + 1) * 256], stat[:, 16 * u + 12 + t:16 * u + 13 + t], None, ALU.mult))
                    st.settle()
                    signal("p_ready")
            dve.wait_ge(s["attn_done"], 2)
            st.run(V.memset(merged, 0.0))
            st(V.memset(zst[:, :, :], 0.0))
            signal("merge_zero")

            for b in range(3):
                with st.loop(4, 8) as i:
                    for q in range(4):
                        dve.wait_ge(s["gate_done"], i * 4 + (16 * b + q + 3))
                        dve.wait_ge(s["y_full"], i * 4 + (16 * b + q + 1))
                        st(TT(tmpm, sg[:, q % 2, :], ps[:, 2 + q % 2, 0:NT], ALU.mult))
                        signal("y_taken")
                        at = ds(i * (4 * NT) + (BC * NT + q * NT), NT)
                        st(TT(cflat[:, at], cflat[:, at], tmpm, ALU.add))
                if b == 0:
                    dve.wait_ge(s["vo_full"], 1)
                    st.run(CP(oT_diff[:, :, TP:NT], ps[:, 4, 0:64].rearrange("p (b h) -> p h b", b=TS)))
                    st(CP(oT_mem[:, :, TP:NT], ps[:, 4, 64:128].rearrange("p (b h) -> p h b", b=TS)))
                    signal("vo_ready")
                    dve.wait_ge(s["mkv_stored"], 32)
                    of = oflat[:, BC * NT:2 * BC * NT]
                    st(TT(sq_mkv[:, 0:BC * NT], of, of, ALU.mult))
                    signal("sub_in")
                if b == 1:
                    for h in range(HEADS):
                        dve.wait_ge(s["sub_full"], h + 1)
                        st(TSC(sq_mkv[:, h * NT:(h + 1) * NT], ps[:, 4 + h % 4, 0:NT], 1.0 / DV, EPS, ALU.mult, ALU.add))
                        signal("sub_taken")
                    root(5)
                    st(REC(sq_mkv[:, 0:BC * NT], sq_mkv[:, 0:BC * NT]))
                    st(TT(of, of, sq_mkv[:, 0:BC * NT], ALU.mult))
                    st(TSC(of, of, sub_w[:, 0:1], 1.0 - LAM_INIT, ALU.mult, ALU.mult))
                    signal("sub_scaled")
            signal("merge_ready")

            dve.wait_ge(s["x_again"], 32)
            rows_from(16, R_O, rows, add=True)
            st(V.memset(stat[:, 0:8], 1.0))
            signal("x1_rows")
            dve.wait_ge(s["n2_ss"], 1)
            st(TSC(stat[:, 0:3], stat[:, 0:3], 1.0 / D, EPS, ALU.mult, ALU.add))
            root(6)
            st(REC(stat[:, 0:3], stat[:, 0:3]))
            dve.wait_ge(s["n2_in"], 16)
            for t, (_, n) in enumerate(TILES):
                st.run(STT(h2_rows[0:n, t, :], x_rows[0:n, t, :], stat[0:n, t:t + 1], n2_w[0:n, :], ALU.mult, ALU.mult))
            st.settle()
            signal("x1_ready")
            signal("h2_ready")
            dve.wait_ge(s["sk_full"], 1)
            st(CP(skT, ps[:, 6, 0:2 * P].rearrange("p (c d) -> p c d", c=2)))
            signal("sk_ready")
            st(V.memset(scores[:, 2, :], 0.0))
            st.run(V.memset(zero512, 0.0))
            st.run(V.memset(wz, 0.0))
            dve.wait_ge(s["consts"], 3)
            st(CP(iota_f, iota_i))
            signal("zero_ready")

            def best16(values, places, src, rest):
                for t in range(3):
                    st.run(V.max(values(t)[:, 0:8], src(t)))
                st.settle()
                for t in range(3):
                    st.run(V.max_index(places(t)[:, 0:8], values(t)[:, 0:8], src(t)))
                    st.run(V.match_replace(rest(t), values(t)[:, 0:8], src(t), -3e38))
                st.settle()
                for t in range(3):
                    st.run(V.max(values(t)[:, 8:16], rest(t)))
                st.settle()
                for t in range(3):
                    st.run(V.max_index(places(t)[:, 8:16], values(t)[:, 8:16], rest(t)))
                st.settle()

            for m in range(2 * PH):
                dve.wait_ge(s["tr_full"], R_PQ + m + 1)
                bank, at = 4 + m % 2, slice(m * NKEY, (m + 1) * NKEY)
                st.run(CP(scores[:, 0:2, at], ps[:, bank, 0:2 * P].rearrange("p (t n) -> p t n", t=2)))
                st(CP(scores[0:TS, 2, at], ps[0:TS, bank, 2 * P:3 * P]))
                signal("rows_taken")
                a = m * TOPK
                best16(lambda t: top_v[:, t, a:a + TOPK], lambda t: top_i[:, t, a:a + TOPK],
                       lambda t: scores[:, t, at], lambda t: score_rest[:, t, :])
                if m % 2:
                    for t in range(3):
                        v1, v2 = top_v[:, t, a - TOPK:a], top_v[:, t, a:a + TOPK]
                        st.run(TT(cand[:, t, :].rearrange("p (a b) -> p a b", a=TOPK), v1.unsqueeze(2).broadcast_to([P, TOPK, TOPK]),
                                  v2.unsqueeze(1).broadcast_to([P, TOPK, TOPK]), ALU.add))
                    st.settle()
                    a = m // 2 * TOPK
                    best16(lambda t: win_v[:, t, a:a + TOPK], lambda t: win_p[:, t, a:a + TOPK],
                           lambda t: cand[:, t, :], lambda t: cand_rest[:, t, :])

            def experts(t):
                four = [P, PH, TOPK, TOPK]
                st(CP(top_f, top_i[:, t, :]))
                hf = top_f.rearrange("p (h c n) -> p h c n", h=PH, c=2)
                f4 = lambda ap: ap.rearrange("p (h a b) -> p h a b", h=PH, a=TOPK)
                for half, (op, arg) in enumerate(((ALU.logical_shift_right, 4), (ALU.bitwise_and, 15))):
                    st(V.tensor_single_scalar(part_i, win_p[:, t, :], arg, op))
                    st(CP(part_f[:, half * P:(half + 1) * P], part_i))
                    pf = part_f[:, half * P:(half + 1) * P].rearrange("p (h n) -> p h n", h=PH).unsqueeze(3).broadcast_to(four)
                    st(TT(f4(hot), pf, iota_f.unsqueeze(1).unsqueeze(1).broadcast_to(four), ALU.is_equal))
                    st(TT(f4(hot), f4(hot), hf[:, :, half, :].unsqueeze(2).broadcast_to(four), ALU.mult))
                    st(RED(pick[:, half * P:(half + 1) * P], hot.rearrange("p (a b) -> p a b", b=TOPK), X, ALU.add))
                st(STT(idx_f, pick[:, 0:P], float(NKEY), pick[:, P:2 * P], ALU.mult, ALU.add))
                st(CP(idx_all[:, t, :], idx_f))
                signal("idx_ready")

            wv = win_v.rearrange("p t (h n) -> p (t h) n", n=TOPK)
            st(TT(shifted.rearrange("p (g n) -> p g n", n=TOPK), wv, wv[:, :, 0:1].broadcast_to([P, 3 * PH, TOPK]), ALU.subtract))
            signal("gate_in")
            experts(0)
            dve.wait_ge(s["gate_out"], 1)
            st(RED(denom, wv, X, ALU.add))
            st(REC(denom, denom))
            st(TT(gates.rearrange("p t (h n) -> p (t h) n", n=TOPK), wv, denom.unsqueeze(2).broadcast_to([P, 3 * PH, TOPK]), ALU.mult))

            def dot(h2, slot, out):
                st(V.tensor_tensor_reduce(out=work, in0=u_slots[slot], in1=h2, scale=1.0, scalar=0.0, op0=ALU.mult, op1=ALU.add, accum_out=out))
                signal("u_used")

            def dot_heads(g0, n):
                t = g0 // PH
                with st.loop(n, TOPK + 1) as g:
                    for j in range(TOPK):
                        dve.wait_ge(u_landed[j % 4], g * 64 + 16 * (g0 * 4 + j // 4 + 1))
                        dot(h2_rows[:, t, :], j % 4, act_a[:, 0, j:j + 1])
                    signal("a_in")
                    dve.wait_ge(s["a_out"], g + (g0 + 1))
                    dve.wait_ge(s["v_used"], g * TOPK + (g0 * TOPK + 4))
                    st(TT(wexp[:, 0, :], act_g[:, 0, :], gates[:, t, ds(g * TOPK + g0 % PH * TOPK, TOPK)], ALU.mult))
                    signal("w_ready")

            def add_output(t):
                n = TILES[t][1]
                y = x_rows[0:n, t, :].rearrange("p (a b) -> p a b", a=4)
                dve.wait_ge(s["yo_full"], t + 1)
                st(TT(y, ps[0:n, 4 * (t % 2):4 * (t % 2) + 4, :], y, ALU.add))
                signal("y_ready")

            dot_heads(0, 3)
            experts(1)
            dot_heads(3, 2)
            experts(2)
            signal("sT_in")
            dot_heads(5, 3)
            dve.wait_ge(s["sT_full"], 1)
            st.run(CP(sidx, ps[:, 4, 0:TS]))
            st(CP(sgate, ps[:, 4, TS:2 * TS]))
            signal("idx_ready")
            dot_heads(8, 1)
            add_output(0)
            dot_heads(9, 7)
            for b in range(TS):
                dve.wait_ge(hb_landed[b % 2], 16 * (b // 2 + 1))
                dve.wait_ge(u_landed[b % 4], 16 * (64 + b // 4 + 1))
                dot(hb[b % 2], b % 4, act_a[:, 0, b:b + 1])
                signal("hb_used")
            signal("a_in")
            add_output(1)
            dve.wait_ge(s["a_out"], 2 * PH + 1)
            st(TT(wz.rearrange("p b c -> p (b c)")[:, 0:TS * TS:TS + 1], act_g[:, 0, 0:TS], sgate, ALU.mult))
            signal("w_ready")
            add_output(2)


_OUTS = [("y_prompt", (1, 256, 2048)), ("y_sample", (8, 1, 2048)), ("k_prompt", (1, 1, 256, 8, 128)),
         ("v_prompt", (1, 1, 256, 8, 128)), ("conv_prompt", (1, 1, 2, 1024)), ("mem_k_prompt", (1, 1, 256, 4, 256)),
         ("mem_v_prompt", (1, 1, 256, 4, 256)), ("k_sample", (1, 8, 1, 8, 128)), ("v_sample", (1, 8, 1, 8, 128)),
         ("conv_sample", (1, 8, 2, 1024))]


def rope_table():
    half = DK // 8
    freq = np.float32(500000.0) ** (-np.arange(half, dtype=np.float32) / np.float32(half))
    pos = np.concatenate([np.arange(TP), np.full(P, PAGES * PAGE)]).astype(np.float32)
    ang = pos[:, None] * freq[None, :]
    tab = np.concatenate([np.cos(ang), np.sin(ang)], axis=1).astype(np.float32)
    return np.ascontiguousarray(tab.reshape(3, P, 2 * half).transpose(1, 0, 2))


def kernel(**inputs):
    import concourse.bacc as bacc
    from concourse.bass_utils import run_bass_kernel_spmd

    nc = bacc.Bacc("TRN2", target_bir_lowering=False, num_devices=1)
    arrays, A, O = {}, {}, {}
    for name, a in list(inputs.items()) + [("rope_tab", rope_table())]:
        a = np.ascontiguousarray(a)
        arrays[f"in_{name}_dram"] = a
        A[name] = nc.dram_tensor(f"in_{name}_dram", a.shape, mybir.dt.from_np(a.dtype), kind="ExternalInput").ap()
    for name, shape in _OUTS:
        O[name] = nc.dram_tensor(f"out_{name}_dram", shape, F32, kind="ExternalOutput").ap()
    build(nc, A, O)
    r = run_bass_kernel_spmd(nc, [arrays], core_ids=[0])
    return tuple(r.results[0][f"out_{name}_dram"] for name, _ in _OUTS)
```

```python
from contextlib import ExitStack, contextmanager

import numpy as np

import concourse.bass as bass
from concourse import mybir

F32 = mybir.dt.float32
I32 = mybir.dt.int32
U32 = mybir.dt.uint32
ALU = mybir.AluOpType
ACT = mybir.ActivationFunctionType
X = mybir.AxisListType.X
ds = bass.ds

P = 128
D = 2048
KC = D // P
TP, TS = 256, 8
NT = TP + TS
DC = D // 2
BC = DC // P
HEADS, DK, DV = 8, 64, 128
MH, MD, NM = 4, 256, 256
PAGES, PAGE = 16, 128
POOL_PAGES = 160
NKEY, PH, TOPK = 128, 8, 16
EPS = 1e-6
NEG = -1e30
LAM_INIT = 0.2
BLK = 256
NR = 2
TILES = [(0, P), (P, P), (TP, TS)]


class Steps:

    def __init__(self, eng, sem):
        self.eng, self.sem, self.base, self.k = eng, sem, 0, 0

    def run(self, ins):
        ins.then_inc(self.sem, 1)
        self.k += 1

    def settle(self):
        self.eng.wait_ge(self.sem, self.base + self.k)

    def reach(self, k):
        self.eng.wait_ge(self.sem, self.base + k)

    def __call__(self, ins):
        self.run(ins)
        self.settle()

    @contextmanager
    def loop(self, n, per):
        base, k = self.base, self.k
        with self.eng.Fori(0, n) as i:
            self.base, self.k = base + (i * per + k), 0
            yield i
            assert self.k == per, f"the body has {self.k} steps, not {per}"
        self.base, self.k = base, k + n * per


def build(nc, A, O):
    rope_tab = A["rope_tab"]
    w_in = A["w_in"][0].rearrange("(k p) n -> p k n", p=P)
    w_mem = A["w_mem_kv"][0].rearrange("(k p) n -> p k n", p=P)
    w_o = A["w_o"][0].rearrange("(k p) n -> p k n", p=P)
    w_pq = A["w_peer_q"][0].rearrange("(k p) n -> p k n", p=P)
    w_br = [A[n][0].rearrange("(k p) n -> p k n", p=P) for n in ("w_conv_out", "w_cross_out", "w_diff_out")]
    gate_col = [7 * 1024, 7 * 1024 + 2 * D, 7 * 1024 + D]
    cache_k = A["cache_k"][0].rearrange("n t h d -> (n t) (h d)")
    cache_v = A["cache_v"][0].rearrange("n t h d -> (n t) (h d)")
    cmem_k = A["cache_mem_k"][0].rearrange("b m h d -> (b m) (h d)")
    cmem_v = A["cache_mem_v"][0].rearrange("b m h d -> (b m) (h d)")
    peer_u, peer_v = A["peer_u"][0], A["peer_v"][0]
    q_dram = nc.dram_tensor("q_rows_scratch", [TS, DC], F32, kind="Internal").ap()
    mq_dram = nc.dram_tensor("mq_rows_scratch", [TS, DC], F32, kind="Internal").ap()
    h2_dram = nc.dram_tensor("h2_rows_scratch", [TS, D], F32, kind="Internal").ap()

    ctx = ExitStack()
    with ctx:
        def sb(name, shape, dt=F32):
            return ctx.enter_context(nc.sbuf_tensor("sb_" + name, shape, dt))

        def sem(name):
            return ctx.enter_context(nc.semaphore(name))

        ps = ctx.enter_context(nc.psum_tensor("ps", [P, 8, 512], F32))

        wring = sb("wring", [P, NR, KC, BLK])
        bregion = sb("bregion", [P, 4096])
        ring4 = sb("ring4", [P, 4, DC])
        hT = sb("hT", [P, KC, NT])
        conv = sb("conv", [P, 3 * BC, NT])
        rows = sb("rows", [P, 3, 4 * DC])
        mkv = sb("mkv", [P, 2, 2 * DC])
        S = sb("S", [P, TS, PAGES, 2 * HEADS])
        Ad = sb("Ad", [P, TS, PAGES, HEADS])
        oreg = sb("oreg", [P, 2 * BC, NT])
        memT = bregion[:, :].rearrange("p (k m) -> p k m", k=KC)
        bwring = bregion[:, :].rearrange("p (s k n) -> p s k n", s=NR, k=BC)
        merged = conv[:, BC:3 * BC, :]
        oT_mem, oT_diff = oreg[:, 0:BC, :], oreg[:, BC:2 * BC, :]
        oflat = oreg[:, :, :].rearrange("p a b -> p (a b)")
        qb = oflat[:, 0:2 * DC].rearrange("p (s n) -> p s n", s=2)
        prods = [oflat[:, n * DC:(n + 1) * DC] for n in (2, 3)]
        prod = prods[0]
        cflat = conv[:, :, :].rearrange("p a b -> p (a b)")
        PART = 8
        temp = [ring4[:, :, :].rearrange("p a b -> p (a b)"), bregion[:, :]]
        x_rows, h2_rows = rows[:, :, 0:D], rows[:, :, D:2 * D]
        cs_rows = Ad[:, :, :, :].rearrange("p a b c -> p (a b c)")
        n2_w, sk_rows = mkv[:, 0, :], mkv[:, 1, 0:2 * P].rearrange("p (c d) -> p c d", c=2)
        skT = mkv[:, 1, 2 * P:4 * P].rearrange("p (c d) -> p c d", c=2)
        sq_mkv = mkv[:, :, :].rearrange("p a b -> p (a b)")
        kpages = [ring4[:, n, :] for n in range(4)] + [sq_mkv[:, n * DC:(n + 1) * DC] for n in range(4)]
        ring_flat = ring4[:, :, :].rearrange("p a b -> p (a b)")
        scores = cflat[:, 0:3 * 2 * PH * NKEY].rearrange("p (t n) -> p t n", t=3)
        work = S[:, :, :, :].rearrange("p a b c -> p (a b c)")
        colrows, lam4 = work[0:72, 0:P], work[:, P:P + 4 * DK].rearrange("p (a n) -> p a n", a=4)
        mask = work[:, 0:2 * TP].rearrange("p (t n) -> p t n", t=2)
        sg = work[:, 1024:1024 + 2 * NT].rearrange("p (s n) -> p s n", s=2)
        rt = ring4[:, :, :].rearrange("p a b -> p (a b)")
        top_v, top_i = [mkv[:, 1, n:n + 3 * 256].rearrange("p (t n) -> p t n", t=3) for n in (4 * P, 4 * P + 3 * 256)]
        top_i = top_i.bitcast(U32)
        top_f = rt[:, 0:256]
        win_v, win_p = [rt[:, n:n + 3 * P].rearrange("p (t n) -> p t n", t=3) for n in (256, 640)]
        win_p = win_p.bitcast(U32)
        part_i, part_f = rt[:, 1024:1152].bitcast(U32), rt[:, 1152:1408]
        pick = rt[:, 1408:1664]
        iota_i, iota_f = rt[:, 1664:1680].bitcast(I32), rt[:, 1680:1696]
        idx_f = rt[:, 1696:1824]
        idx_all = rt[:, 1824:2208].bitcast(I32).rearrange("p (t n) -> p t n", t=3)
        idx_flat = rt[:, 1824:2208].bitcast(I32)
        gates = rt[:, 2208:2592].rearrange("p (t n) -> p t n", t=3)
        uidx = rt[:, 2824:2824 + 3 * TOPK].bitcast(I32).rearrange("p (s n) -> p s n", s=3)
        sidx, sgate = rt[:, 2624:2632].bitcast(I32), rt[:, 2632:2640]
        act_a = rt[:, 2640:2672].rearrange("p (s n) -> p s n", s=2)
        act_g = rt[:, 2672:2704].rearrange("p (s n) -> p s n", s=2)
        wexp = rt[:, 2704:2736].rearrange("p (s n) -> p s n", s=2)
        wz = rt[:, 2736:2800].rearrange("p (b c) -> p b c", b=TS)
        denom = rt[:, 2800:2824]
        diag = rt[:, 3072:3584].rearrange("p (s n) -> p s n", s=4)
        zero512 = rt[:, 3584:4096]
        hot = oflat[:, 2048:4096]
        cand, cand_rest = [oflat[:, n:n + 3 * 256].rearrange("p (t n) -> p t n", t=3) for n in (0, 768)]
        score_rest = work[:, 0:3 * NKEY].rearrange("p (t n) -> p t n", t=3)
        shifted = oflat[:, 1536:1536 + 3 * P]
        u_slots = [wring[:, r].rearrange("p k n -> p (k n)")[:, h * D:(h + 1) * D] for r in range(NR) for h in range(2)]
        hflat = hT[:, :, :].rearrange("p k n -> p (k n)")
        e_slots = [bregion[:, 0:D], bregion[:, D:2 * D], hflat[:, 0:D], hflat[:, D:2 * D]]
        hb = [oflat[:, 0:D], oflat[:, D:2 * D]]
        VR, DR = 4, 2
        v_slots = [rows[:, t, c * DC:(c + 1) * DC] for t in range(2) for c in range(3)]
        DP = 6
        PV = 2 + PAGES - DP
        weighed = work[:, 0:DC]
        own_heads = [sq_mkv[0:n, o:o + DC] for n, o in ((MH, 2 * DC), (HEADS, 3 * DC))]

        ident = sb("ident", [P, P])
        ones = sb("ones", [P, P])
        cols = sb("cols", [P, 72])
        stT = sb("stT", [P, BC, 2 * TS])
        qn_w, kn_w, sub_w = sb("qn_w", [P, DK]), sb("kn_w", [P, DK]), sb("sub_w", [P, 1])
        mq_w, mk_w = sb("mq_w", [P, MD]), sb("mk_w", [P, MD])
        rope = sb("rope", [P, 3, 16])
        lam = sb("lam", [P, 4])
        zst = sb("zst", [P, 2, NT])
        stat = sb("stat", [P, 64])
        pt = sb("pt", [1, TS * PAGES], I32)
        Sm = sb("Sm", [P, TS, 2, MH])
        small = sb("small", [P, 5, P])
        a_now = [zst[:, n, 0:PAGES * HEADS].rearrange("p (t h) -> p t h", t=PAGES) for n in range(2)]
        am_now = [zst[:, n, PAGES * HEADS:PAGES * HEADS + 2 * MH].rearrange("p (t h) -> p t h", t=2) for n in range(2)]
        Ad_f, Sm_f = cs_rows, Sm[:, :, :, :].rearrange("p a b c -> p (a b c)")
        tmpm = small[:, 0:3, :].rearrange("p a b -> p (a b)")[:, 0:NT]

        names = """consts x_in x_clear mem_in cols_in st_in small_in lam_in rope_in pt_in x_ss x_scaled xT_full xT_taken
            cols_full cols_ready st_full chunk_full chunk_taken tr_full rows_taken kprod_ready
            scores_clear q_ready qk_stored q_scratch kpage_used token_done conv_ready cs_full cs_rows
            conv_stored sqrt_in sqrt_out mk_ready mkv_stored self_full self_in max_full max_diag mb_full
            exp_in exp_out sum_in sum_full a_ready attn_staged tt_full qk_T s_full sm_ready exp_ready
            p_ready at_full at_ready o_full attn_done vpage_used vo_ready sub_in sub_full sub_scaled
            gate_full gate_done y_full y_taken merge_ready x_again h2_ready h2T_full h2T_taken h2_scratch
            sk_in sk_full sk_ready gate_in gate_out idx_ready sT_full sT_in u_used a_in a_out w_ready
            diag_ready v_used yo_full y_ready y_stored hb_used zero_ready dve_done act_done pool_done
            n2_in lam_pre lam_exp x1_rows n2_ss sums_free weights_staged dpage_used weighed_ready
            weighed_used sums_masked columns_done sub_taken gather_turn loop_turn""".split()
        s = {n: sem(n) for n in names}
        w_landed = [sem(f"w_landed{i}") for i in range(NR)]
        bw_landed = [sem(f"bw_landed{i}") for i in range(NR)]
        k_landed = [sem(f"k_landed{i}") for i in range(8)]
        v_landed = [sem(f"v_landed{i}") for i in range(VR + DR)]
        qb_landed = [sem(f"qb_landed{i}") for i in range(2)]
        u_landed = [sem(f"u_landed{i}") for i in range(4)]
        e_landed = [sem(f"e_landed{i}") for i in range(4)]
        hb_landed = [sem(f"hb_landed{i}") for i in range(2)]

        G_QKV, G_CONV, G_MEM, G_GATE, G_O, G_PQ = 0, 16, 28, 36, 60, 68
        C_QKV, C_CONV, C_MEM, C_O, C_PQ = 0, 32, 56, 72, 88
        R_QKV, R_O, R_PQ = 0, 32, 48

        def flat(u):
            b = 4 - 4 * u
            return ps[:, b:b + 4, :].rearrange("p a b -> p (a b)")

        selfA = small[:, 4, 64:128].rearrange("p (h b) -> p h b", h=HEADS)

        block = ctx.enter_context(nc.Block())

        @block.sync
        def _(sp):
            sp.dma_start(colrows[0:16, :], A["norm1_w"][0].rearrange("(k p) -> k p", p=P)).then_inc(s["cols_in"], 16)
            sp.dma_start(colrows[16:32, :], A["mem_norm_w"][0].rearrange("(k p) -> k p", p=P)).then_inc(s["cols_in"], 16)
            sp.dma_start(colrows[32:56, :], A["conv_w"][0].rearrange("w (k p) -> (w k) p", p=P)).then_inc(s["cols_in"], 16)
            sp.dma_start(colrows[56:72, :], A["norm2_w"][0].rearrange("(k p) -> k p", p=P)).then_inc(s["cols_in"], 16)
            sp.dma_start(x_rows[:, 0:2, :], A["x_prompt"][0].rearrange("(t p) d -> p t d", p=P)).then_inc(s["x_in"], 16)
            sp.dma_start(x_rows[0:TS, 2, :], A["x_sample"].rearrange("b t d -> (b t) d")).then_inc(s["x_in"], 16)

            def fetch(r, src, col):
                sp.dma_start(wring[:, r], src[:, :, ds(col, BLK)]).then_inc(w_landed[r], 16)

            def stream(n, src, col, c0, before):
                for r in range(NR):
                    if before:
                        sp.wait_ge(s[before[0]], before[1] - 2 * (NR - 1 - r))
                    fetch(r, src, col + r * BLK)
                with sp.Fori(0, n // NR - 1) as i:
                    for r in range(NR):
                        sp.wait_ge(s["chunk_full"], i * (2 * NR) + (c0 + 2 * r + 2))
                        fetch(r, src, i * (NR * BLK) + (col + (NR + r) * BLK))

            stream(16, w_in, 3 * DC, C_QKV, None)
            stream(12, w_in, 0, C_CONV, ("chunk_full", C_CONV))
            stream(8, w_mem, 0, C_MEM, ("chunk_full", C_MEM))
            def gate_weights(b, n, r, i=0):
                sp.wait_ge(s["y_full"], i * (2 * NR) + (16 * b + 2 * n - 2))
                fetch(r, w_in, i * (NR * BLK) + (gate_col[b] + n * BLK))

            def branch_weights(b, n, r, i=0):
                sp.dma_start(bwring[:, r], w_br[b][:, :, ds(i * (NR * BLK) + n * BLK, BLK)]).then_inc(bw_landed[r], 16)

            for b in range(3):
                if b == 0:
                    for r in range(NR):
                        sp.wait_ge(s["chunk_full"], C_O - 2 * (NR - 1 - r))
                        fetch(r, w_in, gate_col[b] + r * BLK)
                    sp.wait_ge(s["chunk_full"], C_O)
                    for r in range(NR):
                        branch_weights(b, r, r)
                    for n in (2, 3):
                        gate_weights(b, n, n % NR)
                        branch_weights(b, n, n % NR)
                    for n in (4, 5):
                        gate_weights(b, n, n % NR)
                    sp.wait_ge(s["attn_done"], 2)
                    for n in (4, 5):
                        branch_weights(b, n, n % NR)
                    for n in (6, 7):
                        gate_weights(b, n, n % NR)
                        branch_weights(b, n, n % NR)
                else:
                    for r in range(NR):
                        gate_weights(b, r, r)
                        branch_weights(b, r, r)
                    with sp.Fori(0, 8 // NR - 1) as i:
                        for r in range(NR):
                            gate_weights(b, NR + r, r, i)
                            branch_weights(b, NR + r, r, i)
            stream(8, w_o, 0, C_O, ("y_full", 48))
            stream(8, w_pq, 0, C_PQ, ("chunk_full", C_PQ))
            for t in range(2):
                sp.wait_ge(s["y_ready"], t + 1)
                sp.dma_start(O["y_prompt"][0, t * P:(t + 1) * P, :], x_rows[:, t, :]).then_inc(s["y_stored"], 16)
            sp.wait_ge(s["y_ready"], 3)
            sp.dma_start(O["y_sample"].rearrange("b t d -> (b t) d"), x_rows[0:TS, 2, :]).then_inc(s["y_stored"], 16)
            sp.wait_ge(s["y_stored"], 48)

        @block.gpsimd
        def _(pool):
            st = Steps(pool, s["pool_done"])
            pool.sem_inc(s["kpage_used"], 8)
            pool.sem_inc(s["vpage_used"], VR)
            pool.sem_inc(s["dpage_used"], DR)
            pool.sem_inc(s["u_used"], 4)
            pool.sem_inc(s["v_used"], 4)
            pool.sem_inc(s["hb_used"], 2)
            pool.sem_inc(s["token_done"], 2)
            pool.dma_start(pt[:, :], A["page_table"].rearrange("(a b) n -> a (b n)", a=1)).then_inc(s["pt_in"], 16)
            st_rows = ring4[0:2 * TS, 0, :]
            pool.dma_start(st_rows, A["state_conv"][0].rearrange("b t c -> (b t) c")).then_inc(s["st_in"], 16)
            for dst, name in ((qn_w, "q_norm_w"), (kn_w, "k_norm_w"), (mq_w, "mq_norm_w"), (mk_w, "mk_norm_w")):
                pool.dma_start(dst[:, :], A[name][0:1, :].to_broadcast([P, dst.shape[1]])).then_inc(s["small_in"], 16)
            pool.dma_start(sub_w[:, :], A["subln_w"].rearrange("a p -> p a")).then_inc(s["small_in"], 16)
            for j, name in enumerate(("lambda_q1", "lambda_k1", "lambda_q2", "lambda_k2")):
                pool.dma_start(lam4[:, j, :], A[name][0:1, :].to_broadcast([P, DK])).then_inc(s["lam_in"], 16)
            pool.dma_start(h2_rows[:, 0:2, :], A["mem_prompt"][0].rearrange("(t p) d -> p t d", p=P)).then_inc(s["mem_in"], 16)
            pool.dma_start(rope[:, :, :], rope_tab).then_inc(s["rope_in"], 16)
            st(nc.gpsimd.memset(ident[:, :], 0.0))
            st(nc.gpsimd.affine_select(out=ident[:, :], in_=ident[:, :], compare_op=ALU.not_equal, fill=1.0, base=0,
                                       pattern=[[-1, P]], channel_multiplier=1))
            st(nc.gpsimd.memset(ones[:, :], 1.0))
            pool.sem_inc(s["consts"], 1)

            pool.wait_ge(s["q_ready"], 1)
            pool.dma_start(q_dram, rows[0:TS, 2, 0:DC]).then_inc(s["q_scratch"], 16)
            pool.wait_ge(s["q_scratch"], 16)
            pool.wait_ge(s["pt_in"], 16)
            pool.wait_ge(s["st_full"], 1)
            pool.wait_ge(s["small_in"], 80)

            def load_pages(i, g):
                par, half = g // 4 % 2, g % 2
                if g % 4 == 0:
                    b = i * 2 + g // 4
                    pool.wait_ge(s["token_done"], i * 2 + (g // 4 + 1))
                    pool.dma_start(qb[:, par, :], q_dram[ds(b, 1), :].to_broadcast([P, DC])).then_inc(qb_landed[par], 16)
                for r in range(4):
                    n = i * 32 + (g * 4 + r)
                    pool.wait_ge(s["kpage_used"], n + 1)
                    page = pool.value_load(pt[0:1, ds(n, 1)], min_val=0, max_val=POOL_PAGES - 1)
                    pool.dma_start(kpages[4 * half + r], cache_k[ds(page * PAGE, PAGE), :]).then_inc(k_landed[4 * half + r], 16)

            def multiply_pages(i, g):
                par, half = g // 4, g % 2
                pool.wait_ge(qb_landed[par], i * 16 + 16)
                for r in (1, 3):
                    pool.wait_ge(k_landed[4 * half + r], i * 64 + 16 * (g // 2 + 1))
                    st(nc.gpsimd.tensor_tensor(kpages[4 * half + r], kpages[4 * half + r], qb[:, par, :], ALU.mult))
                    pool.sem_inc(s["kprod_ready"], 1)

            load_pages(0, 0)
            with st.loop(TS // 2 - 1, 16) as i:
                for g in range(8):
                    load_pages(i, g + 1)
                    multiply_pages(i, g)
            for g in range(8):
                if g < 7:
                    load_pages(TS // 2 - 1, g + 1)
                multiply_pages(TS // 2 - 1, g)

            pool.wait_ge(s["q_ready"], 2)
            pool.dma_start(mq_dram, rows[0:TS, 2, 3 * DC:4 * DC]).then_inc(s["q_scratch"], 16)
            pool.wait_ge(s["q_scratch"], 32)
            with pool.Fori(0, TS // 2) as i:
                for par in range(2):
                    b = i * 2 + par
                    pool.wait_ge(s["token_done"], i * 2 + (TS + par + 1))
                    pool.dma_start(qb[:, par, :], mq_dram[ds(b, 1), :].to_broadcast([P, DC])).then_inc(qb_landed[par], 16)
                    for t in range(2):
                        pool.wait_ge(s["kpage_used"], i * 4 + (TS * PAGES + 4 + 2 * par + t + 1))
                        pool.dma_start(ring4[:, 2 * par + t, :], cmem_k[ds(b * NM + t * P, P), :]).then_inc(k_landed[2 * par + t], 16)

            for c, (po, so) in ((1, ("k_prompt", "k_sample")), (2, ("v_prompt", "v_sample"))):
                pool.dma_start(O[po][0, 0].rearrange("(t p) h d -> p t (h d)", p=P),
                               rows[:, 0:2, c * DC:(c + 1) * DC]).then_inc(s["qk_stored"], 16)
                pool.dma_start(O[so][0].rearrange("b t h d -> (b t) (h d)"),
                               rows[0:TS, 2, c * DC:(c + 1) * DC]).then_inc(s["qk_stored"], 16)
            pool.wait_ge(s["cs_rows"], 1)
            pool.dma_start(O["conv_prompt"][0, 0], cs_rows[0:2, :]).then_inc(s["conv_stored"], 16)
            pool.dma_start(O["conv_sample"][0, :, 1, :], cs_rows[2:2 + TS, :]).then_inc(s["conv_stored"], 16)
            pool.dma_start(O["conv_sample"][0, :, 0, :], A["state_conv"][0, :, 1, :]).then_inc(s["conv_stored"], 16)
            pool.wait_ge(s["a_ready"], 1)
            st(nc.gpsimd.memset(mask[:, :, :], 0.0))
            for t in range(2):
                st(nc.gpsimd.affine_select(out=mask[:, t, :], in_=mask[:, t, :], compare_op=ALU.is_ge, fill=NEG,
                                           base=t * P, pattern=[[-1, TP]], channel_multiplier=1))
            pool.sem_inc(s["consts"], 1)
            pool.wait_ge(s["mk_ready"], 1)
            for c, name in ((0, "mem_k_prompt"), (1, "mem_v_prompt")):
                pool.dma_start(O[name][0, 0].rearrange("(t p) h d -> p t (h d)", p=P),
                               mkv[:, :, c * DC:(c + 1) * DC]).then_inc(s["mkv_stored"], 16)

            pool.wait_ge(s["attn_done"], 2)
            pool.wait_ge(s["qk_stored"], 64)
            with pool.Fori(0, TS) as b:
                for k in range(DP):
                    for n in (2 * k, 2 * k + 1, PV + k):
                        if n < PV:
                            pool.wait_ge(s["vpage_used"], b * PV + (n + 1))
                            r = n % VR
                        else:
                            pool.wait_ge(s["dpage_used"], b * DP + (k + 1))
                            r = VR + k % DR
                        if n < 2:
                            src = cmem_v[ds(b * NM + n * P, P), :]
                        else:
                            page = pool.value_load(pt[0:1, ds(b * PAGES + (n - 2), 1)], min_val=0, max_val=POOL_PAGES - 1)
                            src = cache_v[ds(page * PAGE, PAGE), :]
                        pool.dma_start(v_slots[r], src).then_inc(v_landed[r], 16)

            pool.wait_ge(s["vpage_used"], TS * PV + VR)
            pool.wait_ge(s["dpage_used"], TS * DP + DR)
            pool.dma_start(x_rows[:, 0:2, :], A["x_prompt"][0].rearrange("(t p) d -> p t d", p=P)).then_inc(s["x_again"], 16)
            pool.dma_start(x_rows[0:TS, 2, :], A["x_sample"].rearrange("b t d -> (b t) d")).then_inc(s["x_again"], 16)
            st(nc.gpsimd.iota(iota_i, pattern=[[1, TOPK]], base=0, channel_multiplier=0))
            pool.sem_inc(s["consts"], 1)
            pool.wait_ge(s["mkv_stored"], 32)
            pool.wait_ge(s["conv_stored"], 48)
            pool.wait_ge(s["sub_scaled"], 1)
            pool.dma_start(n2_w, A["norm2_w"][0:1, :].to_broadcast([P, D])).then_inc(s["n2_in"], 16)
            pool.dma_start(sk_rows, A["sub_keys"][0].rearrange("c k d -> k c d")).then_inc(s["sk_in"], 16)
            pool.wait_ge(s["h2_ready"], 1)
            pool.dma_start(h2_dram, h2_rows[0:TS, 2, :]).then_inc(s["h2_scratch"], 16)

            def gather(table, dst, idx, landed):
                pool.sem_inc(s["gather_turn"], 1)
                nc.gpsimd.indirect_dma_start(dst, None, table, bass.IndirectOffsetOnAxis(ap=idx, axis=0)).then_inc(landed, 16)

            def gather_u(k, g, j):
                pool.wait_ge(s["u_used"], g * TOPK + (j + 1))
                gather(peer_u, u_slots[j % 4], uidx[:, k, j:j + 1], u_landed[j % 4])

            def gather_v(k, g, j):
                pool.wait_ge(s["v_used"], g * TOPK + (j + 1))
                gather(peer_v, e_slots[j % 4], uidx[:, k, j:j + 1], e_landed[j % 4])

            def heads(i, k):
                st(nc.gpsimd.tensor_copy(uidx[:, (k + 1) % 3, :], idx_flat[:, ds(i * (3 * TOPK) + (k + 1) * TOPK, TOPK)]))
                for j in range(TOPK):
                    gather_u((k + 1) % 3, i * 3 + (k + 1), j)
                    gather_v(k, i * 3 + k, j)

            pool.wait_ge(s["idx_ready"], 1)
            st(nc.gpsimd.tensor_copy(uidx[:, 0, :], idx_flat[:, 0:TOPK]))
            for j in range(TOPK):
                gather_u(0, 0, j)
            pool.wait_ge(s["idx_ready"], 2)
            with st.loop(2, 3) as i:
                for k in range(3):
                    heads(i, k)
            pool.wait_ge(s["idx_ready"], 3)
            with st.loop(3, 3) as i:
                for k in range(3):
                    heads(i + 2, k)
            pool.wait_ge(s["idx_ready"], 4)
            pool.wait_ge(s["h2_scratch"], 16)
            for j in range(TOPK):
                gather_v(0, 15, j)
                if j % 2:
                    b = j // 2
                    pool.wait_ge(s["hb_used"], b + 1)
                    pool.dma_start(hb[b % 2], h2_dram[b:b + 1, :].to_broadcast([P, D])).then_inc(hb_landed[b % 2], 16)
                    pool.wait_ge(s["u_used"], 2 * P + b + 1)
                    gather(peer_u, u_slots[b % 4], sidx[:, b:b + 1], u_landed[b % 4])
            for b in range(TS):
                pool.wait_ge(s["v_used"], 2 * P + b + 1)
                gather(peer_v, e_slots[b % 4], sidx[:, b:b + 1], e_landed[b % 4])
            pool.wait_ge(s["qk_stored"], 64)

        @block.tensor
        def _(pe):
            mm = nc.tensor.matmul

            pe.wait_ge(s["consts"], 1)
            pe.wait_ge(s["cols_in"], 64)
            nc.tensor.transpose(ps[:, 0, 0:72], colrows, ident[0:72, 0:72]).then_inc(s["cols_full"], 1)
            pe.wait_ge(s["st_in"], 16)
            for j in range(BC):
                last = nc.tensor.transpose(ps[:, 1, j * 16:(j + 1) * 16], ring4[0:16, 0, j * P:(j + 1) * P], ident[0:16, 0:16])
            last.then_inc(s["st_full"], 1)

            def transpose_rows(src, k, bank, tiles):
                for t, (first, n) in enumerate(tiles):
                    last = nc.tensor.transpose(ps[:, bank, first:first + n], src[0:n, t, k * P:(k + 1) * P], ident[0:n, 0:n])
                return last

            pe.wait_ge(s["x_scaled"], 1)
            for k in range(KC):
                if k >= 4:
                    pe.wait_ge(s["xT_taken"], k - 3)
                transpose_rows(x_rows, k, 4 + k % 4, TILES).then_inc(s["xT_full"], 1)
            pe.wait_ge(s["xT_taken"], KC)

            def chunk(r, c, n, rhs):
                pe.wait_ge(s["chunk_taken"], n + 1)
                for k in range(KC):
                    last = mm(ps[:, (2 * r + c) % 4, 0:NT], wring[:, r, k, c * P:(c + 1) * P], rhs[:, k, :], start=(k == 0), stop=(k == KC - 1))
                last.then_inc(s["chunk_full"], 1)

            def linear(g0, n_blocks, c0, rhs, turn=None):
                with pe.Fori(0, n_blocks // NR) as i:
                    for r in range(NR):
                        pe.wait_ge(w_landed[r], i * 16 + 16 * (g0 // NR + 1))
                        for c in range(2):
                            q = 2 * r + c
                            chunk(r, c, i * (2 * NR) + (c0 + q), rhs)
                            if turn and q:
                                turn(q - 1, i * (2 * NR) + (q - 1))
                    if turn:
                        turn(2 * NR - 1, i * (2 * NR) + (2 * NR - 1))

            def turner(c0, m0):
                def turn(q, m):
                    pe.wait_ge(s["chunk_taken"], m + (c0 + 4 + 1))
                    pe.wait_ge(s["rows_taken"], m + (m0 + 1))
                    for t, (first, n) in enumerate(TILES):
                        last = nc.tensor.transpose(ps[0:n, 4 + q % 2, t * P:(t + 1) * P], zst[:, q % 2, first:first + n], ident[:, :])
                    last.then_inc(s["tr_full"], 1)
                return turn

            linear(G_QKV, 4, C_QKV, hT, turner(C_QKV, R_QKV))
            pe.wait_ge(s["x_scaled"], 2)
            pe.wait_ge(s["rows_taken"], 2 + 8)
            for k in range(KC):
                pe.wait_ge(s["xT_taken"], KC + k - 3)
                transpose_rows(h2_rows, k, 4 + k % 4, TILES[0:2]).then_inc(s["xT_full"], 1)
            pe.wait_ge(s["xT_taken"], 2 * KC)
            linear(G_QKV + 4, 12, C_QKV + 8, hT, turner(C_QKV + 8, R_QKV + 8))
            linear(G_CONV, 12, C_CONV, hT)
            def conv_state():
                pe.wait_ge(s["conv_ready"], 1)
                pe.wait_ge(s["rows_taken"], 32 + 2)
                for j in range(BC):
                    last = nc.tensor.transpose(ps[0:2 + TS, 4 + j // 4, (j % 4) * P:(j % 4 + 1) * P], conv[:, BC + j, TP - 2:NT], ident[:, :])
                last.then_inc(s["cs_full"], 1)

            def own_scores():
                pe.wait_ge(s["self_in"], 1)
                mm(ps[:, 7, 0:P], ones[0:TS, :], small[0:TS, 0, :], start=True, stop=True).then_inc(s["self_full"], 1)

            def turn_maxima(m, n):
                pe.wait_ge(s["max_full"], m + 1)
                nc.tensor.transpose(ps[0:n, 5, 0:P], small[:, 1, 0:n], ident[:, :]).then_inc(s["max_diag"], 1)

            def spread_maxima(m, n):
                pe.wait_ge(s["mb_full"], m + 1)
                mm(ps[:, 6, 0:n], ones[0:n, :], small[0:n, 2, 0:n], start=True, stop=True).then_inc(s["max_diag"], 1)

            def sum_partitions(m, n):
                pe.wait_ge(s["sum_in"], m + 1)
                mm(ps[:, 7, 0:n], ones[:, :], small[:, 1, 0:n], start=True, stop=True).then_inc(s["sum_full"], 1)

            with pe.Fori(0, 8 // NR) as i:
                for r in range(NR):
                    pe.wait_ge(w_landed[r], i * 16 + 16 * (G_MEM // NR + 1))
                    for t in range(2):
                        pe.wait_ge(s["chunk_taken"], i * (2 * NR) + (C_MEM + 2 * r + t + 1))
                        for k in range(KC):
                            last = mm(ps[:, 2 * r + t, 0:BLK], memT[:, k, t * P:(t + 1) * P], wring[:, r, k, :], start=(k == 0), stop=(k == KC - 1))
                        last.then_inc(s["chunk_full"], 1)
            conv_state()
            own_scores()
            pe.wait_ge(s["chunk_taken"], C_O + 4)

            def gate_chunk(b, r, c, q, operand, between=None, ready=None):
                pe.wait_ge(s["gate_done"], q + 1)
                for k in range(KC):
                    last = mm(ps[:, c, 0:NT], wring[:, r, k, c * P:(c + 1) * P], hT[:, k, :], start=(k == 0), stop=(k == KC - 1))
                    if k == KC - 1:
                        last.then_inc(s["gate_full"], 1)
                    if between:
                        between(k)
                pe.wait_ge(s["y_taken"], q + 2)
                if ready:
                    pe.wait_ge(s[ready], 1)
                for k in range(BC):
                    last = mm(ps[:, 2, 0:NT], bwring[:, r, k, c * P:(c + 1) * P], operand[:, k, :], start=(k == 0), stop=(k == BC - 1))
                    if k == BC - 1:
                        last.then_inc(s["y_full"], 1)
                    if between:
                        between(KC + k)

            nk, nm = P, TS * MH
            after = {(0, KC - 1): (turn_maxima, 0, nk), (0, KC + BC - 1): (spread_maxima, 0, nk), (1, KC + BC - 1): (sum_partitions, 0, nk),
                     (2, KC + BC - 1): (turn_maxima, 1, nm), (3, KC - 1): (spread_maxima, 1, nm), (4, KC - 1): (sum_partitions, 1, nm)}
            for q in range(PART):
                g, r, c = q // 2, q // 2 % NR, q % 2
                if c == 0:
                    pe.wait_ge(w_landed[r], 16 * ((G_GATE + g) // NR + 1))
                    pe.wait_ge(bw_landed[r], 16 * (g // NR + 1))

                def softmax_step(k):
                    if (q, k) in after:
                        after[q, k][0](*after[q, k][1:])
                gate_chunk(0, r, c, q, conv[:, 0:BC, :], softmax_step)
            pe.wait_ge(s["a_ready"], 1)
            pe.wait_ge(s["gate_done"], PART + 2)
            pe.wait_ge(s["y_taken"], PART + 2)

            def attention(n_heads, base, w):
                halves = w // P
                a0 = 1536
                s0 = 512 * halves
                with pe.Fori(0, n_heads // 2) as i:
                    for u in range(2):
                        pe.wait_ge(s["attn_staged"], i * 2 + (base + u + 1))
                        for o in range(2):
                            for f in range(halves):
                                for t in range(2):
                                    last = nc.tensor.transpose(
                                        flat(u)[:, (o * halves + f) * 256 + t * P:(o * halves + f) * 256 + (t + 1) * P],
                                        temp[u][:, (2 * o + t) * w + f * P:(2 * o + t) * w + (f + 1) * P], ident[:, :])
                        last.then_inc(s["tt_full"], 1)
                    for u in range(2):
                        pe.wait_ge(s["qk_T"], i * 2 + (base + u + 1))
                        T = temp[u][:, 6 * w:6 * w + 1024]
                        for t in range(2):
                            if halves == 1:
                                for c in range(2):
                                    last = mm(flat(u)[:, s0 + (2 * c + t) * 256:s0 + (2 * c + t + 1) * 256],
                                              T[c * DK:(c + 1) * DK, t * P:(t + 1) * P], T[c * DK:(c + 1) * DK, 256:512], start=True, stop=True)
                            else:
                                for f in range(2):
                                    last = mm(flat(u)[:, s0 + t * 256:s0 + (t + 1) * 256], T[:, f * 256 + t * P:f * 256 + (t + 1) * P],
                                              T[:, 512 + f * 256:512 + (f + 1) * 256], start=(f == 0), stop=(f == 1))
                        last.then_inc(s["s_full"], 1)
                    for u in range(2):
                        pe.wait_ge(s["p_ready"], i * 2 + (base + u + 1))
                        p0, step = (6 * w + 512, 512) if halves == 1 else (6 * w + 1024, 256)
                        for k in range(2):
                            for t in range(2):
                                last = nc.tensor.transpose(flat(u)[:, a0 + k * 256 + t * P:a0 + k * 256 + (t + 1) * P],
                                                           temp[u][:, p0 + t * step + k * P:p0 + t * step + (k + 1) * P], ident[:, :])
                        last.then_inc(s["at_full"], 1)
                    for u in range(2):
                        pe.wait_ge(s["at_ready"], i * 2 + (base + u + 1))
                        t0 = 6 * w + 512 + 1024 if halves == 1 else 6 * w + 1024 + 512
                        for f in range(halves):
                            for k in range(2):
                                last = mm(flat(u)[:, a0 + f * 256:a0 + (f + 1) * 256], temp[u][:, 4 * w + k * w + f * P:4 * w + k * w + (f + 1) * P],
                                          temp[u][:, t0 + k * 256:t0 + (k + 1) * 256], start=(k == 0), stop=(k == 1))
                        last.then_inc(s["o_full"], 1)

            attention(HEADS, 0, DV)
            attention(MH, HEADS, MD)
            pe.wait_ge(s["attn_done"], 2)

            pe.wait_ge(s["sums_free"], 1)
            for h in range(HEADS):
                last = mm(ps[:, 3, 128 + h * TS:128 + (h + 1) * TS], rows[0:TS, 2, 2 * DC + h * DV:2 * DC + (h + 1) * DV],
                          selfA[0:TS, h, :], start=True, stop=True)

            def values(i, k, n):
                if n < PV:
                    pe.wait_ge(v_landed[n % VR], i * (4 * (PV // VR) * 16) + 16 * (PV // VR * k + n // VR + 1))
                    block = v_slots[n % VR]
                else:
                    pe.wait_ge(s["weighed_ready"], i * 4 + (k + 1))
                    block = weighed
                if n < 2:
                    bank, w, first, final = 6, am_now[k % 2][:, n, :], n == 0, n == 1
                else:
                    bank, w, first, final = 4, a_now[k % 2][:, n - 2, :] if n < PV else ones[:, 0:HEADS], n == 2, n == PV
                if n == 0:
                    pe.wait_ge(s["sums_masked"], i * 8 + (2 * k + 1))
                for q in range(2):
                    last = mm(ps[0:w.shape[1], bank + q, :], w, block[:, q * 512:(q + 1) * 512], start=first, stop=final)
                last.then_inc(s["vpage_used" if n < PV else "weighed_used"], 1)

            def columns(i, k, kind):
                pe.wait_ge(s["sums_masked"], i * 8 + (2 * k + kind + 2))
                src = own_heads[kind]
                n = src.shape[0]
                for h in range(BC):
                    last = mm(ps[:, 3, ds(i * (4 * BC) + ((1 - kind) * 64 + k * BC + h), 1)], src[:, h * P:(h + 1) * P], ones[0:n, 0:1], start=True, stop=True)
                last.then_inc(s["columns_done"], 1)

            with pe.Fori(0, 2) as i:
                for r in range(NR):
                    pe.wait_ge(w_landed[r], i * 16 + 16 * ((G_GATE + 4) // NR + 1))
                    pe.wait_ge(bw_landed[r], i * 16 + 16 * (4 // NR + 1))
                    for c in range(2):
                        k = 2 * r + c
                        pe.wait_ge(s["weights_staged"], i * 4 + (k + 1))
                        todo = list(range(PV + 1))

                        def sample_values(step):
                            if step % 5 in (0, 2, 4) and todo:
                                values(i, k, todo.pop(0))
                            if step == 5:
                                columns(i, k, 0)
                        gate_chunk(0, r, c, i * 4 + (PART + k), conv[:, 0:BC, :], sample_values)
                        assert not todo
                        columns(i, k, 1)

            def branch(b, g0, n, operand, ready):
                with pe.Fori(0, n // NR) as i:
                    for r in range(NR):
                        g = g0 // NR + b * (8 // NR)
                        pe.wait_ge(w_landed[r], i * 16 + 16 * (G_GATE // NR + g + 1))
                        pe.wait_ge(bw_landed[r], i * 16 + 16 * (g + 1))
                        for c in range(2):
                            gate_chunk(b, r, c, i * (2 * NR) + (16 * b + 2 * g0 + 2 * r + c), operand, ready=ready)

            branch(1, 0, 4, oT_mem, "vo_ready")
            pe.wait_ge(s["sub_in"], 1)
            for h in range(HEADS):
                if h >= 4:
                    pe.wait_ge(s["sub_taken"], h - 3)
                mm(ps[:, 4 + h % 4, 0:NT], ones[:, :], sq_mkv[:, h * NT:(h + 1) * NT], start=True, stop=True).then_inc(s["sub_full"], 1)
            branch(1, 4, 4, oT_mem, "vo_ready")
            branch(2, 0, 8, oT_diff, "sub_scaled")

            pe.wait_ge(s["merge_ready"], 1)
            linear(G_O, 8, C_O, merged, turner(C_O, R_O))
            pe.wait_ge(s["x1_rows"], 1)
            for k in range(KC):
                if k >= 4:
                    pe.wait_ge(s["h2T_taken"], k - 3)
                transpose_rows(x_rows, k, 4 + k % 4, TILES).then_inc(s["h2T_full"], 1)
            pe.wait_ge(s["h2T_taken"], KC)
            pe.wait_ge(s["sk_in"], 16)
            for c in range(2):
                last = nc.tensor.transpose(ps[:, 6, c * P:(c + 1) * P], sk_rows[:, c, :], ident[:, :])
            last.then_inc(s["sk_full"], 1)
            pe.wait_ge(s["sk_ready"], 1)

            def score(q, m):
                pe.wait_ge(s["chunk_taken"], m + (C_PQ + 4 + 1))
                pe.wait_ge(s["rows_taken"], m + (R_PQ + 1))
                for t, (first, n) in enumerate(TILES):
                    last = mm(ps[0:n, 4 + q % 2, t * P:(t + 1) * P], zst[:, q % 2, first:first + n], skT[:, q % 2, :], start=True, stop=True)
                last.then_inc(s["tr_full"], 1)

            linear(G_PQ, 8, C_PQ, hT, score)
            pe.wait_ge(s["rows_taken"], 64 + 2)
            pe.wait_ge(s["chunk_taken"], 104 + 4)

            pe.wait_ge(s["zero_ready"], 1)

            def add_zero(t, start, stop):
                n = TILES[t][1]
                for q in range(4):
                    last = mm(ps[0:n, 4 * (t % 2) + q, :], zero512[:, 0:n], zero512, start=start, stop=stop, skip_group_check=True)
                return last

            def add_heads(g0, n):
                bank = 4 * (g0 // PH)
                with pe.Fori(0, n) as g:
                    for j in range(TOPK):
                        pe.wait_ge(s["diag_ready"], g * TOPK + (g0 * TOPK + j + 1))
                        pe.wait_ge(e_landed[j % 4], g * 64 + 16 * (g0 * 4 + j // 4 + 1))
                        for q in range(4):
                            last = mm(ps[:, bank + q, :], diag[:, j % 4, :], e_slots[j % 4][:, q * 512:(q + 1) * 512], start=False, stop=False, skip_group_check=True)
                        last.then_inc(s["v_used"], 1)

            add_zero(0, True, False)
            add_heads(0, 7)
            pe.wait_ge(s["sT_in"], 1)
            nc.tensor.transpose(ps[:, 4, 0:TS], idx_f[0:TS, :], ident[0:TS, 0:TS])
            nc.tensor.transpose(ps[:, 4, TS:2 * TS], gates[0:TS, 2, :], ident[0:TS, 0:TS]).then_inc(s["sT_full"], 1)
            add_heads(7, 1)
            add_zero(0, False, True).then_inc(s["yo_full"], 1)
            pe.wait_ge(s["idx_ready"], 4)
            add_zero(1, True, False)
            add_heads(8, 8)
            add_zero(1, False, True).then_inc(s["yo_full"], 1)
            pe.wait_ge(s["y_ready"], 1)
            add_zero(2, True, False)
            pe.wait_ge(s["w_ready"], 17)
            for b in range(TS):
                pe.wait_ge(e_landed[b % 4], 16 * (64 + b // 4 + 1))
                for q in range(4):
                    last = mm(ps[0:TS, q, :], wz[:, b, :], e_slots[b % 4][:, q * 512:(q + 1) * 512], start=False, stop=False, skip_group_check=True)
                last.then_inc(s["v_used"], 1)
            add_zero(2, False, True).then_inc(s["yo_full"], 1)

        @block.scalar
        def _(act):
            st = Steps(act, s["act_done"])
            A_ = nc.scalar.activation
            act.sem_inc(s["chunk_taken"], 4)
            act.sem_inc(s["gate_done"], 2)
            junk = cflat[:, 0:D]

            def square_sums(tiles):
                for col, src, n in tiles:
                    st(A_(junk[0:n], src, ACT.Square, accum_out=stat[0:n, col:col + 1]))

            def root(n, ap):
                act.wait_ge(s["sqrt_in"], n)
                st(A_(ap, ap, ACT.Sqrt))
                act.sem_inc(s["sqrt_out"], 1)

            act.wait_ge(s["x_clear"], 1)
            act.wait_ge(s["x_in"], 32)
            square_sums([(t, x_rows[0:n, t, :], n) for t, (_, n) in enumerate(TILES)])
            act.sem_inc(s["x_ss"], 1)
            root(1, stat[:, 0:3])
            act.wait_ge(s["lam_pre"], 1)
            st(A_(lam[:, 0:2], lam[:, 0:2], ACT.Exp))
            act.sem_inc(s["lam_exp"], 1)
            act.wait_ge(s["cols_ready"], 1)
            for k in range(KC):
                act.wait_ge(s["xT_full"], k + 1)
                st(A_(hT[:, k, :], ps[:, 4 + k % 4, 0:NT], ACT.Copy, scale=cols[:, k:k + 1]))
                act.sem_inc(s["xT_taken"], 1)
            act.wait_ge(s["mem_in"], 16)
            square_sums([(3 + t, h2_rows[:, t, :], P) for t in range(2)])
            act.sem_inc(s["x_ss"], 1)
            root(2, stat[:, 3:5])

            def to_stage(n_chunks, c0, m0):
                with st.loop(n_chunks // 4, 4) as i:
                    for q in range(4):
                        act.wait_ge(s["chunk_full"], i * 4 + (c0 + q + 1))
                        act.wait_ge(s["rows_taken"], i * 4 + (m0 + q + 1))
                        st(A_(zst[:, q % 2, :], ps[:, q, 0:NT], ACT.Copy))
                        act.sem_inc(s["chunk_taken"], 1)

            def to_rows(n_chunks, c0, m0, out, col):
                act.wait_ge(s["rows_taken"], m0 + 2)
                with st.loop(n_chunks // 4, 12) as i:
                    for q in range(4):
                        act.wait_ge(s["chunk_full"], i * 4 + (c0 + q + 1))
                        st(A_(zst[:, q % 2, :], ps[:, q, 0:NT], ACT.Copy))
                        act.sem_inc(s["chunk_taken"], 1)
                        act.wait_ge(s["tr_full"], i * 4 + (m0 + q + 1))
                        at = ds(i * (4 * P) + (col + q * P), P)
                        st.run(A_(out[:, 0:2, at], ps[:, 4 + q % 2, 0:2 * P].rearrange("p (t n) -> p t n", t=2), ACT.Copy))
                        st(A_(out[0:TS, 2, at], ps[0:TS, 4 + q % 2, 2 * P:3 * P], ACT.Copy))
                        act.sem_inc(s["rows_taken"], 1)

            to_stage(8, C_QKV, R_QKV)
            root(3, small[:, 3, 0:48])
            for k in range(KC, 2 * KC):
                act.wait_ge(s["xT_full"], k + 1)
                st(A_(memT[:, k - KC, :], ps[:, 4 + k % 4, 0:NM], ACT.Copy, scale=cols[:, k:k + 1]))
                act.sem_inc(s["xT_taken"], 1)
            to_rows(24, C_QKV + 8, R_QKV + 8, rows, DC)

            def conv_chunks(i0, n):
                with st.loop(n, 4) as i:
                    for q in range(4):
                        act.wait_ge(s["chunk_full"], i * 4 + (C_CONV + 4 * i0 + q + 1))
                        st(A_(cflat[:, ds(i * (4 * NT) + (4 * i0 + q) * NT, NT)], ps[:, q, 0:NT], ACT.Copy))
                        act.sem_inc(s["chunk_taken"], 1)

            conv_chunks(0, 6)
            act.wait_ge(s["token_done"], 2 + TS)
            def memory_chunk(i, q):
                act.wait_ge(s["chunk_full"], i * 4 + (C_MEM + q + 1))
                st(A_(mkv[:, q % 2, ds(i * (2 * BLK) + (q // 2) * BLK, BLK)], ps[:, q % 4, 0:BLK], ACT.Copy))
                act.sem_inc(s["chunk_taken"], 1)

            for q in range(4):
                memory_chunk(0, q)
            root(4, small[:, 3, 0:60])
            with st.loop(3, 4) as i:
                for q in range(4):
                    memory_chunk(i, 4 + q)

            for q in range(PART):
                act.wait_ge(s["gate_full"], q + 1)
                act.wait_ge(s["y_taken"], q + 1)
                st(A_(zst[:, q % 2, :], ps[:, q % 2, 0:NT], ACT.Sigmoid))
                act.sem_inc(s["gate_done"], 1)
                if q == 0:
                    act.wait_ge(s["exp_in"], 1)
                    st.run(A_(work, work, ACT.Exp, scale=DK ** -0.5))
                    st(A_(small[:, 0, :], small[:, 0, :], ACT.Exp, scale=DK ** -0.5))
                    act.sem_inc(s["exp_out"], 1)
                if q == 3:
                    act.wait_ge(s["exp_in"], 2)
                    st(A_(Sm_f, Sm_f, ACT.Exp, scale=MD ** -0.5))
                    act.sem_inc(s["exp_out"], 1)
                if q == 4:
                    root(5, small[:, 3, 0:8])

            def attention(n_heads, base, w, srcs, out, n_rows, scale):
                T0 = 6 * w
                tt = 512 * (w // P)
                with st.loop(n_heads // 2, 2 * (3 + 1 + n_rows + 1 + 1)) as i:
                    for u in range(2):
                        for o, (src, col) in enumerate(srcs):
                            st.run(A_(temp[u][:, 2 * o * w:(2 * o + 2) * w].rearrange("p (t n) -> p t n", t=2),
                                      src[:, 0:2, ds(i * (2 * w) + (col + u * w), w)], ACT.Copy))
                        st.settle()
                        act.sem_inc(s["attn_staged"], 1)
                    for u in range(2):
                        act.wait_ge(s["tt_full"], i * 2 + (base + u + 1))
                        st(A_(temp[u][:, T0:T0 + tt], flat(u)[:, 0:tt], ACT.Copy))
                        act.sem_inc(s["qk_T"], 1)
                    for u in range(2):
                        act.wait_ge(s["sm_ready"], i * 2 + (base + u + 1))
                        for n in range(n_rows):
                            dst = temp[u][:, T0 + tt + n * 256:T0 + tt + (n + 1) * 256]
                            src = dst if n_rows == 4 else flat(u)[:, tt + n * 256:tt + (n + 1) * 256]
                            st.run(A_(dst, src, ACT.Exp, scale=scale, bias=stat[:, 16 * u + 4 + n:16 * u + 5 + n],
                                      accum_out=stat[:, 16 * u + 8 + n:16 * u + 9 + n]))
                        st.settle()
                        act.sem_inc(s["exp_ready"], 1)
                    for u in range(2):
                        act.wait_ge(s["at_full"], i * 2 + (base + u + 1))
                        st(A_(temp[u][:, T0 + 1536:T0 + 2048], flat(u)[:, 1536:2048], ACT.Copy))
                        act.sem_inc(s["at_ready"], 1)
                    for u in range(2):
                        act.wait_ge(s["o_full"], i * 2 + (base + u + 1))
                        c = w // P
                        st(A_(out[:, ds(i * (2 * c) + u * c, c), 0:TP], flat(u)[:, 1536:1536 + 256 * c].rearrange("p (a b) -> p a b", a=c), ACT.Copy))
                act.sem_inc(s["attn_done"], 1)

            qkv = [(rows, 0), (rows, DC), (rows, 2 * DC)]
            act.wait_ge(s["mk_ready"], 1)
            act.wait_ge(s["y_full"], PART)
            attention(HEADS, 0, DV, qkv, oT_diff, 4, DK ** -0.5)
            attention(MH, HEADS, MD, [(rows, 3 * DC), (mkv, 0), (mkv, DC)], oT_mem, 2, MD ** -0.5)

            act.wait_ge(s["sums_free"], 1)
            def gates_of(first, n, staged=False):
                with st.loop(n // 4, 12 if staged else 4) as i:
                    for q in range(4):
                        if staged:
                            w = PAGES * HEADS
                            act.wait_ge(s["columns_done"], i * 8 + (2 * q + 2))
                            st.run(A_(zst[:, q % 2, 0:w], Ad_f[:, ds(i * (4 * w) + q * w, w)], ACT.Copy))
                            st(A_(zst[:, q % 2, w:w + 2 * MH], Sm_f[:, ds(i * (8 * MH) + q * 2 * MH, 2 * MH)], ACT.Copy))
                            act.sem_inc(s["weights_staged"], 1)
                        act.wait_ge(s["gate_full"], i * 4 + (first + q + 1))
                        act.wait_ge(s["y_taken"], i * 4 + (first + q + 1))
                        st(A_(sg[:, q % 2, :], ps[:, q % 2, 0:NT], ACT.Sigmoid))
                        act.sem_inc(s["gate_done"], 1)

            gates_of(PART, 16 - PART, staged=True)
            gates_of(16, 8)
            root(6, sq_mkv[:, 0:BC * NT])
            gates_of(24, 24)

            to_stage(16, C_O, R_O)
            for k in range(KC):
                act.wait_ge(s["h2T_full"], k + 1)
                st(A_(hT[:, k, :], ps[:, 4 + k % 4, 0:NT], ACT.Copy, scale=cols[:, 56 + k:57 + k]))
                act.sem_inc(s["h2T_taken"], 1)
            act.wait_ge(s["x1_rows"], 1)
            square_sums([(t, x_rows[0:n, t, :], n) for t, (_, n) in enumerate(TILES)])
            act.sem_inc(s["n2_ss"], 1)
            root(7, stat[:, 0:3])
            act.wait_ge(s["scores_clear"], 1)
            to_rows(16, C_PQ, R_PQ, scores, 0)
            act.wait_ge(s["gate_in"], 1)
            def winners(t):
                st(A_(win_v[:, t, :], shifted[:, t * P:(t + 1) * P], ACT.Exp, scale=stat[:, t:t + 1]))

            def diagonals(g0, n):
                with st.loop(n, 1 + TOPK) as g:
                    act.wait_ge(s["a_in"], g + (g0 + 1))
                    st(A_(act_g[:, 0, :], act_a[:, 0, :], ACT.Gelu))
                    act.sem_inc(s["a_out"], 1)
                    act.wait_ge(s["w_ready"], g + (g0 + 1))
                    for j in range(TOPK):
                        act.wait_ge(s["v_used"], g * TOPK + (g0 * TOPK + j + 1))
                        st(A_(diag[:, j % 4, :], ident[:, :], ACT.Copy, scale=wexp[:, 0, j:j + 1]))
                        act.sem_inc(s["diag_ready"], 1)

            winners(0)
            winners(1)
            act.sem_inc(s["gate_out"], 1)
            diagonals(0, 4)
            act.wait_ge(s["gate_in"], 2)
            winners(2)
            act.sem_inc(s["gate_out"], 1)
            diagonals(4, 12)
            act.wait_ge(s["a_in"], 2 * PH + 1)
            st(A_(act_g[:, 0, 0:TS], act_a[:, 0, 0:TS], ACT.Gelu))
            act.sem_inc(s["a_out"], 1)

        @block.vector
        def _(dve):
            st = Steps(dve, s["dve_done"])
            V = nc.vector
            TT, TSC, STT, CP, RED, REC = V.tensor_tensor, V.tensor_scalar, V.scalar_tensor_tensor, V.tensor_copy, V.tensor_reduce, V.reciprocal

            def signal(name, n=1):
                dve.sem_inc(s[name], n)

            def root(n):
                signal("sqrt_in")
                dve.wait_ge(s["sqrt_out"], n)

            signal("rows_taken", 2)
            signal("y_taken", 2)
            st(V.memset(stat[:, :], 1.0))
            signal("x_clear")
            dve.wait_ge(s["lam_in"], 64)
            st(TT(lam4[:, 0, :], lam4[:, 0, :], lam4[:, 1, :], ALU.mult))
            st(TT(lam4[:, 2, :], lam4[:, 2, :], lam4[:, 3, :], ALU.mult))
            st(RED(lam[:, 0:1], lam4[:, 0, :], X, ALU.add))
            st(RED(lam[:, 1:2], lam4[:, 2, :], X, ALU.add))
            signal("lam_pre")
            dve.wait_ge(s["cols_full"], 1)
            st.run(CP(cols[:, :], ps[:, 0, 0:72]))
            dve.wait_ge(s["st_full"], 1)
            st(CP(stT[:, :, :], ps[:, 1, 0:P].rearrange("p (a b) -> p a b", a=BC)))
            signal("cols_ready")

            def row_factors(n, ap):
                dve.wait_ge(s["x_ss"], n)
                st(TSC(ap, ap, 1.0 / D, EPS, ALU.mult, ALU.add))
                root(n)
                st(REC(ap, ap))

            row_factors(1, stat[:, 0:3])
            for t, (_, n) in enumerate(TILES):
                st.run(TSC(x_rows[0:n, t, :], x_rows[0:n, t, :], stat[0:n, t:t + 1], None, ALU.mult))
            st.settle()
            signal("x_scaled")
            row_factors(2, stat[:, 3:5])
            for t in range(2):
                st.run(TSC(h2_rows[:, t, :], h2_rows[:, t, :], stat[:, 3 + t:4 + t], None, ALU.mult))
            st.settle()
            signal("x_scaled")
            dve.wait_ge(s["lam_exp"], 1)
            st(TT(lam[:, 2:3], lam[:, 1:2], lam[:, 0:1], ALU.subtract))
            st(TSC(lam[:, 3:4], lam[:, 2:3], LAM_INIT, None, ALU.subtract))

            dve.wait_ge(s["xT_full"], KC)
            st(V.memset(rows[:, 2, :], 0.0))

            def rows_from(n_chunks, m0, out, add=False):
                with st.loop(n_chunks // 4, 8) as i:
                    for q in range(4):
                        dve.wait_ge(s["tr_full"], i * 4 + (m0 + q + 1))
                        at = ds(i * (4 * P) + q * P, P)
                        src = ps[:, 4 + q % 2, 0:2 * P].rearrange("p (t n) -> p t n", t=2)
                        own = ps[0:TS, 4 + q % 2, 2 * P:3 * P]
                        if add:
                            st.run(TT(out[:, 0:2, at], src, out[:, 0:2, at], ALU.add))
                            st(TT(out[0:TS, 2, at], own, out[0:TS, 2, at], ALU.add))
                        else:
                            st.run(CP(out[:, 0:2, at], src))
                            st(CP(out[0:TS, 2, at], own))
                        signal("rows_taken")

            rows_from(8, R_QKV, rows)

            dve.wait_ge(s["small_in"], 80)
            dve.wait_ge(s["rope_in"], 16)
            r_ = small[:, 3, :]

            def row_norms(groups, area, n_root):
                sq3 = area[:, 0:3 * DC].rearrange("p (t n) -> p t n", t=3)
                at = 0
                spans = []
                for c, g, w, _ in groups:
                    part = rows[:, :, c:c + DC]
                    st(TT(sq3, part, part, ALU.mult))
                    r = r_[:, at:at + 3 * g]
                    st(RED(r, area[:, 0:3 * DC].rearrange("p (g w) -> p g w", w=w), X, ALU.add))
                    st(TSC(r, r, 1.0 / w, EPS, ALU.mult, ALU.add))
                    spans.append(r)
                    at += 3 * g
                root(n_root)
                st(REC(r_[:, 0:at], r_[:, 0:at]))
                for (c, g, w, wt), r in zip(groups, spans):
                    part = rows[:, :, c:c + DC].rearrange("p t (g w) -> p t g w", w=w)
                    rr = r.rearrange("p (t g) -> p t g", t=3).unsqueeze(3).broadcast_to([P, 3, g, w])
                    st(TT(part, part, rr, ALU.mult))
                    for t in range(3):
                        st.run(TT(part[:, t], part[:, t], wt[:, :].unsqueeze(1).broadcast_to([P, g, w]), ALU.mult))
                    st.settle()
                    if w == DK:
                        cos, sin = [rope[:, :, 8 * h:8 * h + 8].unsqueeze(2).broadcast_to([P, 3, g, 8]) for h in range(2)]
                        x1, x2 = part[:, :, :, 0:8], part[:, :, :, 8:16]
                        t4 = [area[:, 384 * n:384 * (n + 1)].rearrange("p (t g w) -> p t g w", t=3, g=g) for n in range(4)]
                        for n, (a, b) in enumerate(((x1, cos), (x2, sin), (x2, cos), (x1, sin))):
                            st.run(TT(t4[n], a, b, ALU.mult))
                        st.settle()
                        st.run(TT(x1, t4[0], t4[1], ALU.subtract))
                        st(TT(x2, t4[2], t4[3], ALU.add))

            row_norms([(0, 16, DK, qn_w)], sq_mkv, 3)
            signal("q_ready")

            def score_group(i, g):
                half, par = g % 2, g // 4
                slots = kpages[4 * half:4 * half + 4]
                landed = i * 64 + 16 * (g // 2 + 1)
                out = lambda r: work[:, ds(i * 512 + (g * 64 + r * 16), 16)]
                by_head = lambda ap: ap.rearrange("p (g w) -> p g w", w=DK)
                k0 = st.k
                dve.wait_ge(k_landed[4 * half], landed)
                st.run(TT(prods[0], slots[0], qb[:, par, :], ALU.mult))
                dve.wait_ge(k_landed[4 * half + 2], landed)
                st.run(TT(prods[1], slots[2], qb[:, par, :], ALU.mult))
                st.reach(k0 + 1)
                signal("kpage_used")
                st.run(RED(out(0), by_head(prods[0]), X, ALU.add))
                dve.wait_ge(s["kprod_ready"], i * 16 + (2 * g + 1))
                st.run(RED(out(1), by_head(slots[1]), X, ALU.add))
                st.reach(k0 + 2)
                st.run(RED(out(2), by_head(prods[1]), X, ALU.add))
                st.reach(k0 + 4)
                signal("kpage_used", 2)
                dve.wait_ge(s["kprod_ready"], i * 16 + (2 * g + 2))
                st(RED(out(3), by_head(slots[3]), X, ALU.add))
                signal("kpage_used")

            with st.loop(TS // 2, 8 * 6) as i:
                for g in range(8):
                    if g % 4 == 0:
                        dve.wait_ge(qb_landed[g // 4], i * 16 + 16)
                        signal("loop_turn")
                    score_group(i, g)
                    if g % 4 == 3:
                        signal("token_done")

            dve.wait_ge(s["rows_taken"], 2 + 32)
            row_norms([(DC, 16, DK, kn_w), (3 * DC, 4, MD, mq_w)], ring_flat, 4)
            signal("q_ready")

            dve.wait_ge(s["chunk_taken"], C_MEM + 4)
            st(TT(conv[:, BC:2 * BC, :], conv[:, BC:2 * BC, :], conv[:, 2 * BC:3 * BC, :], ALU.mult))
            u, y = [lambda j, a, b, o=o: conv[:, o + j, a:b] for o in (BC, 2 * BC)]
            tap = lambda n, j: cols[:, 32 + 8 * n + j:33 + 8 * n + j]
            steps = [
                lambda j: TSC(y(j, 0, NT), u(j, 0, NT), tap(2, j), None, ALU.mult),
                lambda j: STT(y(j, 1, TP), u(j, 0, TP - 1), tap(1, j), y(j, 1, TP), ALU.mult, ALU.add),
                lambda j: STT(y(j, 2, TP), u(j, 0, TP - 2), tap(0, j), y(j, 2, TP), ALU.mult, ALU.add),
                lambda j: STT(y(j, TP, NT), stT[:, j, 1:2 * TS:2], tap(1, j), y(j, TP, NT), ALU.mult, ALU.add),
                lambda j: STT(y(j, TP, NT), stT[:, j, 0:2 * TS:2], tap(0, j), y(j, TP, NT), ALU.mult, ALU.add)]
            for step in steps:
                for j in range(BC):
                    st.run(step(j))
                st.settle()
            st(TT(conv[:, 0:BC, :], conv[:, 0:BC, :], conv[:, 2 * BC:3 * BC, :], ALU.mult))
            signal("conv_ready")

            b0, b1, b2, b3, b4 = [small[:, n, :] for n in range(5)]
            st(TT(prod[0:TS], rows[0:TS, 2, 0:DC], rows[0:TS, 2, DC:2 * DC], ALU.mult))
            st(RED(b4[0:TS, 0:16], prod[0:TS].rearrange("p (g w) -> p g w", w=DK), X, ALU.add))
            st(TT(b0[0:TS].rearrange("p (b c) -> p b c", b=TS), b4[0:TS, 0:16].unsqueeze(1).broadcast_to([TS, TS, 16]),
                  ident[0:TS, 0:TS].unsqueeze(2).broadcast_to([TS, TS, 16]), ALU.mult))
            signal("self_in")
            by_page = S[:, :, :, :].rearrange("p b g c -> p b c g")
            c3 = lambda ap: ap.rearrange("p (b c) -> p b c", b=TS)
            st(RED(c3(b1), by_page, X, ALU.max))

            with st.loop(TS // 2, 8) as i:
                for par in range(2):
                    dve.wait_ge(qb_landed[par], i * 16 + (64 + 16))
                    for t in range(2):
                        dve.wait_ge(k_landed[2 * par + t], i * 16 + (16 * 16 + 16))
                        st(TT(prods[t], ring4[:, 2 * par + t, :], qb[:, par, :], ALU.mult))
                        signal("kpage_used")
                        st(RED(Sm_f[:, ds(i * 16 + (par * 8 + t * 4), 4)], prods[t].rearrange("p (g w) -> p g w", w=MD), X, ALU.add))
                    signal("token_done")


            dve.wait_ge(s["cs_full"], 1)
            st(CP(cs_rows[0:2 + TS, :].rearrange("p (a b) -> p a b", a=2), ps[0:2 + TS, 4:6, :]))
            signal("cs_rows")
            def turned_maxima(m, n):
                dve.wait_ge(s["max_diag"], 2 * m + 1)
                st(RED(stat[0:n, 40:41], ps[0:n, 5, 0:P], X, ALU.max))
                st(TSC(b2[0:n, 0:n], ident[0:n, 0:n], stat[0:n, 40:41], None, ALU.mult))
                signal("mb_full")

            def spread_maxima(m, n):
                dve.wait_ge(s["max_diag"], 2 * m + 2)
                st(CP(b3[:, 0:n], ps[:, 6, 0:n]))

            over_pages = lambda ap: c3(ap).unsqueeze(2).broadcast_to([P, TS, PAGES, 16])
            mem3, n_m = Sm[:, :, :, :], TS * MH
            m3 = b1[:, 0:n_m].rearrange("p (b h) -> p b h", b=TS)
            over_m = lambda ap: ap[:, 0:n_m].rearrange("p (b h) -> p b h", b=TS).unsqueeze(2).broadcast_to([P, TS, 2, MH])

            def own_maxima():
                dve.wait_ge(s["self_full"], 1)
                st(CP(b0, ps[:, 7, 0:P]))
                st(TT(b1, b1, b0, ALU.max))
                signal("max_full")

            def exponents():
                spread_maxima(0, P)
                st.run(TT(S[:, :, :, :], S[:, :, :, :], over_pages(b3), ALU.subtract))
                st(TT(b0, b0, b3, ALU.subtract))
                signal("exp_in")

            def page_sums():
                dve.wait_ge(s["exp_out"], 1)
                st(RED(c3(b1), by_page, X, ALU.add))
                signal("sum_in")

            def probabilities():
                dve.wait_ge(s["sum_full"], 1)
                st(TT(b1, ps[:, 7, 0:P], b0, ALU.add))
                st(REC(b1, b1))
                odd = b1.rearrange("p (a c) -> p a c", c=2)[:, :, 1:2]
                st(TSC(odd, odd, lam[:, 3:4], None, ALU.mult))
                st.run(TT(S[:, :, :, :], S[:, :, :, :], over_pages(b1), ALU.mult))
                st(TT(b0, b0, b1, ALU.mult))
                ob = b0.rearrange("p (a c) -> p a c", c=2)
                st(TT(b4[:, 0:64].unsqueeze(2), ob[:, :, 0:1], ob[:, :, 1:2], ALU.add))
                st(TT(selfA[0:TS], b4[0:TS, 0:64].rearrange("p (b h) -> p h b", b=TS),
                      ident[0:TS, 0:TS].unsqueeze(1).broadcast_to([TS, HEADS, TS]), ALU.mult))
                st(TT(m3, mem3[:, :, 0, :], mem3[:, :, 1, :], ALU.max))
                signal("max_full")

            def memory_exponents():
                spread_maxima(1, n_m)
                st(TT(mem3, mem3, over_m(b3), ALU.subtract))
                signal("exp_in")

            def memory_sums():
                dve.wait_ge(s["exp_out"], 2)
                st(TT(m3, mem3[:, :, 0, :], mem3[:, :, 1, :], ALU.add))
                signal("sum_in")

            def weights():
                dve.wait_ge(s["sum_full"], 2)
                st(REC(b1[:, 0:n_m], ps[:, 7, 0:n_m]))
                st(TT(mem3, mem3, over_m(b1), ALU.mult))
                dve.wait_ge(s["conv_stored"], 48)
                pairs = work.rearrange("p (a c) -> p a c", c=2)
                st(TT(cs_rows.unsqueeze(2), pairs[:, :, 0:1], pairs[:, :, 1:2], ALU.add))
                signal("a_ready")

            def memory_key_norm():
                dve.wait_ge(s["chunk_taken"], C_O + 4)
                sqm = oflat[:, 0:D].rearrange("p (t n) -> p t n", t=2)
                mk = mkv[:, :, 0:DC]
                st(TT(sqm, mk, mk, ALU.mult))
                st(RED(b3[:, 0:8], oflat[:, 0:D].rearrange("p (g w) -> p g w", w=MD), X, ALU.add))
                st(TSC(b3[:, 0:8], b3[:, 0:8], 1.0 / MD, EPS, ALU.mult, ALU.add))
                root(5)
                st(REC(b3[:, 0:8], b3[:, 0:8]))
                mk4 = mk.rearrange("p t (g w) -> p t g w", w=MD)
                st(TT(mk4, mk4, b3[:, 0:8].rearrange("p (t g) -> p t g", t=2).unsqueeze(3).broadcast_to([P, 2, 4, MD]), ALU.mult))
                for t in range(2):
                    st.run(TT(mk4[:, t], mk4[:, t], mk_w[:, :].unsqueeze(1).broadcast_to([P, 4, MD]), ALU.mult))
                st.settle()
                signal("mk_ready")

            def first_merge(q):
                dve.wait_ge(s["gate_done"], q + 3)
                dve.wait_ge(s["y_full"], q + 1)
                st(TT(merged[:, q, :], zst[:, q % 2, :], ps[:, 2, 0:NT], ALU.mult))
                signal("y_taken")

            own_maxima()
            turned_maxima(0, P)
            first_merge(0)
            exponents()
            page_sums()
            first_merge(1)
            probabilities()
            first_merge(2)
            turned_maxima(1, n_m)
            memory_exponents()
            first_merge(3)
            memory_sums()
            weights()
            first_merge(4)
            memory_key_norm()
            for q in range(5, PART):
                first_merge(q)

            dve.wait_ge(s["consts"], 2)

            with st.loop(HEADS // 2, 2 * 3 + 2 * 6) as i:
                for u in range(2):
                    sm = temp[u][:, 6 * DV + 512:6 * DV + 1536]
                    v4 = lambda ap: ap.rearrange("p (t c n) -> p t c n", t=2, c=2)
                    dve.wait_ge(s["s_full"], i * 2 + (u + 1))
                    st(TT(v4(sm), flat(u)[:, 512:1536].rearrange("p (c t n) -> p t c n", t=2, c=2), mask[:, :, :].unsqueeze(2).broadcast_to([P, 2, 2, TP]), ALU.add))
                    st(RED(stat[:, 16 * u:16 * u + 4], sm.rearrange("p (a n) -> p a n", a=4), X, ALU.max))
                    st(TSC(stat[:, 16 * u + 4:16 * u + 8], stat[:, 16 * u:16 * u + 4], -DK ** -0.5, None, ALU.mult))
                    signal("sm_ready")
                for u in range(2):
                    sm = temp[u][:, 6 * DV + 512:6 * DV + 1536]
                    r4 = stat[:, 16 * u + 12:16 * u + 16]
                    dve.wait_ge(s["exp_ready"], i * 2 + (u + 1))
                    st(REC(r4, stat[:, 16 * u + 8:16 * u + 12]))
                    st(TSC(r4[:, 1:4:2], r4[:, 1:4:2], lam[:, 3:4], None, ALU.mult))
                    for t in range(2):
                        a, b = sm[:, t * 512:t * 512 + 256], sm[:, t * 512 + 256:t * 512 + 512]
                        st(TSC(a, a, r4[:, 2 * t:2 * t + 1], None, ALU.mult))
                        st(STT(a, b, r4[:, 2 * t + 1:2 * t + 2], a, ALU.mult, ALU.add))
                    signal("p_ready")
            with st.loop(MH // 2, 2 * 2 + 2 * 3) as i:
                for u in range(2):
                    dve.wait_ge(s["s_full"], i * 2 + (HEADS + u + 1))
                    st(RED(stat[:, 16 * u:16 * u + 2], flat(u)[:, 1024:1536].rearrange("p (a n) -> p a n", a=2), X, ALU.max))
                    st(TSC(stat[:, 16 * u + 4:16 * u + 6], stat[:, 16 * u:16 * u + 2], -MD ** -0.5, None, ALU.mult))
                    signal("sm_ready")
                for u in range(2):
                    sm = temp[u][:, 6 * MD + 1024:6 * MD + 1536]
                    dve.wait_ge(s["exp_ready"], i * 2 + (HEADS + u + 1))
                    st(REC(stat[:, 16 * u + 12:16 * u + 14], stat[:, 16 * u + 8:16 * u + 10]))
                    for t in range(2):
                        st.run(TSC(sm[:, t * 256:(t + 1) * 256], sm[:, t * 256:(t + 1) * 256], stat[:, 16 * u + 12 + t:16 * u + 13 + t], None, ALU.mult))
                    st.settle()
                    signal("p_ready")
            dve.wait_ge(s["attn_done"], 2)
            signal("sums_masked")
            signal("columns_done", 4)
            dve.wait_ge(s["mkv_stored"], 32)
            signal("sums_free")

            def mask_sums(i, k, kind):
                n = (MH, HEADS)[kind]
                if kind == 0:
                    dve.wait_ge(s["vpage_used"], i * (4 * PV) + (PV * k + 2 + VR))
                else:
                    dve.wait_ge(s["weighed_used"], i * 4 + (k + 1))
                dve.wait_ge(s["columns_done"], i * 8 + (2 * k + kind + 3))
                as_heads = lambda ap: ap.rearrange("p (h c) -> p h c", h=n)
                st(TT(as_heads(own_heads[kind]), as_heads(ps[0:n, 6 - 2 * kind:8 - 2 * kind, :].rearrange("p a b -> p (a b)")),
                      ident[0:n, 0:n].unsqueeze(2).broadcast_to([n, n, DC // n]), ALU.mult))
                signal("sums_masked")

            def weigh_page(i, k, j):
                dve.wait_ge(v_landed[VR + j % DR], i * (4 * (DP // DR) * 16) + 16 * (DP // DR * k + j // DR + 1))
                for h in range(HEADS):
                    at = slice(h * DV, (h + 1) * DV)
                    w = a_now[k % 2][:, PAGES - DP + j, h:h + 1]
                    page = v_slots[VR + j % DR][:, at]
                    if j == 0:
                        st.run(TSC(weighed[:, at], page, w, None, ALU.mult))
                    else:
                        st.reach(st.k - HEADS + 1)
                        st.run(STT(weighed[:, at], page, w, weighed[:, at], ALU.mult, ALU.add))
                st.settle()
                signal("dpage_used")

            with st.loop((16 - PART) // 4, 4 * (3 + DP * HEADS)) as i:
                for q in range(4):
                    dve.wait_ge(s["weights_staged"], i * 4 + (q + 1))
                    for j in range(DP):
                        weigh_page(i, q, j)
                        if j == 1:
                            mask_sums(i, q, 0)
                    signal("weighed_ready")
                    mask_sums(i, q, 1)
                    dve.wait_ge(s["gate_done"], i * 4 + (PART + q + 3))
                    dve.wait_ge(s["y_full"], i * 4 + (PART + q + 1))
                    st(TT(cflat[:, ds(i * (4 * NT) + (BC + PART + q) * NT, NT)], sg[:, q % 2, :], ps[:, 2, 0:NT], ALU.mult))
                    signal("y_taken")
            dve.wait_ge(s["columns_done"], 4 + 2 * TS)
            st.run(CP(oT_diff[:, :, TP:NT], ps[:, 3, 0:64].rearrange("p (b h) -> p h b", b=TS)))
            st(CP(oT_mem[:, :, TP:NT], ps[:, 3, 64:128].rearrange("p (b h) -> p h b", b=TS)))
            signal("vo_ready")
            st(TT(oT_diff[:, :, TP:NT], oT_diff[:, :, TP:NT], ps[:, 3, 128:192].rearrange("p (h b) -> p h b", b=TS), ALU.add))
            of = oflat[:, BC * NT:2 * BC * NT]
            st(TT(sq_mkv[:, 0:BC * NT], of, of, ALU.mult))
            signal("sub_in")

            def merge(b, first, n):
                with st.loop(n // 4, 8) as i:
                    for q in range(4):
                        dve.wait_ge(s["gate_done"], i * 4 + (16 * b + first + q + 3))
                        dve.wait_ge(s["y_full"], i * 4 + (16 * b + first + q + 1))
                        at = ds(i * (4 * NT) + (BC + first + q) * NT, NT)
                        st(TT(tmpm, sg[:, q % 2, :], ps[:, 2, 0:NT], ALU.mult))
                        signal("y_taken")
                        st(TT(cflat[:, at], cflat[:, at], tmpm, ALU.add))

            merge(1, 0, 8)
            for h in range(HEADS):
                dve.wait_ge(s["sub_full"], h + 1)
                st(TSC(sq_mkv[:, h * NT:(h + 1) * NT], ps[:, 4 + h % 4, 0:NT], 1.0 / DV, EPS, ALU.mult, ALU.add))
                signal("sub_taken")
            signal("sqrt_in")
            merge(1, 8, 4)
            dve.wait_ge(s["sqrt_out"], 6)
            st(REC(sq_mkv[:, 0:BC * NT], sq_mkv[:, 0:BC * NT]))
            st(TT(of, of, sq_mkv[:, 0:BC * NT], ALU.mult))
            st(TSC(of, of, sub_w[:, 0:1], 1.0 - LAM_INIT, ALU.mult, ALU.mult))
            signal("sub_scaled")
            merge(1, 12, 4)
            merge(2, 0, 16)
            signal("merge_ready")

            dve.wait_ge(s["x_again"], 32)
            rows_from(16, R_O, rows, add=True)
            st(V.memset(stat[:, 0:8], 1.0))
            signal("x1_rows")
            dve.wait_ge(s["sk_full"], 1)
            st(CP(skT, ps[:, 6, 0:2 * P].rearrange("p (c d) -> p c d", c=2)))
            signal("sk_ready")
            dve.wait_ge(s["n2_ss"], 1)
            st(TSC(stat[:, 0:3], stat[:, 0:3], 1.0 / D, EPS, ALU.mult, ALU.add))
            root(7)
            st(REC(stat[:, 0:3], stat[:, 0:3]))
            dve.wait_ge(s["n2_in"], 16)
            for t, (_, n) in enumerate(TILES):
                st.run(STT(h2_rows[0:n, t, :], x_rows[0:n, t, :], stat[0:n, t:t + 1], n2_w[0:n, :], ALU.mult, ALU.mult))
            st.settle()
            signal("h2_ready")
            st(V.memset(scores[:, 2, :], 0.0))
            signal("scores_clear")
            st.run(V.memset(zero512, 0.0))
            st.run(V.memset(wz, 0.0))
            dve.wait_ge(s["consts"], 3)
            st(CP(iota_f, iota_i))
            signal("zero_ready")

            def best16(rows_of):
                for values, _, src, _ in rows_of:
                    st.run(V.max(values[:, 0:8], src))
                st.settle()
                for values, places, src, rest in rows_of:
                    st.run(V.max_index(places[:, 0:8], values[:, 0:8], src))
                    st.run(V.match_replace(rest, values[:, 0:8], src, -3e38))
                st.settle()
                for values, _, _, rest in rows_of:
                    st.run(V.max(values[:, 8:16], rest))
                st.settle()
                for values, places, _, rest in rows_of:
                    st.run(V.max_index(places[:, 8:16], values[:, 8:16], rest))
                st.settle()

            def half_best(t, m, area):
                at, a = slice(m * NKEY, (m + 1) * NKEY), slice(m * TOPK, (m + 1) * TOPK)
                return top_v[:, t, a], top_i[:, t, a], scores[:, t, at], score_rest[:, area, :]

            def head_best(tiles, h):
                a = 2 * h * TOPK
                for t in tiles:
                    v1, v2 = top_v[:, t, a:a + TOPK], top_v[:, t, a + TOPK:a + 2 * TOPK]
                    st.run(TT(cand[:, t, :].rearrange("p (a b) -> p a b", a=TOPK), v1.unsqueeze(2).broadcast_to([P, TOPK, TOPK]),
                              v2.unsqueeze(1).broadcast_to([P, TOPK, TOPK]), ALU.add))
                st.settle()
                a = slice(h * TOPK, (h + 1) * TOPK)
                best16([(win_v[:, t, a], win_p[:, t, a], cand[:, t, :], cand_rest[:, t, :]) for t in tiles])

            def experts(t, h0=0, nh=PH):
                four, n = [P, nh, TOPK, TOPK], nh * TOPK
                at = slice(h0 * TOPK, h0 * TOPK + n)
                st(CP(top_f[:, 0:2 * n], top_i[:, t, 2 * h0 * TOPK:2 * h0 * TOPK + 2 * n]))
                hf = top_f[:, 0:2 * n].rearrange("p (h c n) -> p h c n", h=nh, c=2)
                hot_n = hot[:, 0:n * TOPK]
                f4 = lambda ap: ap.rearrange("p (h a b) -> p h a b", h=nh, a=TOPK)
                for half, (op, arg) in enumerate(((ALU.logical_shift_right, 4), (ALU.bitwise_and, 15))):
                    part = part_f[:, half * P:half * P + n]
                    st(V.tensor_single_scalar(part_i[:, 0:n], win_p[:, t, at], arg, op))
                    st(CP(part, part_i[:, 0:n]))
                    pf = part.rearrange("p (h n) -> p h n", h=nh).unsqueeze(3).broadcast_to(four)
                    st(TT(f4(hot_n), pf, iota_f.unsqueeze(1).unsqueeze(1).broadcast_to(four), ALU.is_equal))
                    st(TT(f4(hot_n), f4(hot_n), hf[:, :, half, :].unsqueeze(2).broadcast_to(four), ALU.mult))
                    st(RED(pick[:, half * P:half * P + n], hot_n.rearrange("p (a b) -> p a b", b=TOPK), X, ALU.add))
                st(STT(idx_f[:, at], pick[:, 0:n], float(NKEY), pick[:, P:P + n], ALU.mult, ALU.add))
                st(CP(idx_all[:, t, at], idx_f[:, at]))

            for m in range(2 * PH):
                dve.wait_ge(s["rows_taken"], R_PQ + 2 + m + 1)
                if m == 2 * PH - 1:
                    signal("idx_ready")
                best16([half_best(t, m, t) for t in range(2)])
                if m % 2:
                    head_best((0, 1), m // 2)
                if m == PH + 1:
                    experts(0, 0, PH // 2)

            def shift_winners(t0, n):
                wv = win_v[:, t0:t0 + n, :].rearrange("p t (h n) -> p (t h) n", n=TOPK)
                st(TT(shifted[:, t0 * P:(t0 + n) * P].rearrange("p (g n) -> p g n", n=TOPK), wv, wv[:, :, 0:1].broadcast_to([P, n * PH, TOPK]), ALU.subtract))
                signal("gate_in")

            def softmax_gates(t0, n, n_out):
                wv = win_v[:, t0:t0 + n, :].rearrange("p t (h n) -> p (t h) n", n=TOPK)
                sums = denom[:, 0:n * PH]
                dve.wait_ge(s["gate_out"], n_out)
                st(RED(sums, wv, X, ALU.add))
                st(REC(sums, sums))
                st(TT(gates[:, t0:t0 + n, :].rearrange("p t (h n) -> p (t h) n", n=TOPK), wv, sums.unsqueeze(2).broadcast_to([P, n * PH, TOPK]), ALU.mult))

            shift_winners(0, 2)
            experts(0, PH // 2, PH // 2)
            signal("idx_ready")
            softmax_gates(0, 2, 1)

            def dot(h2, slot, out):
                st(V.tensor_tensor_reduce(out=work, in0=u_slots[slot], in1=h2, scale=1.0, scalar=0.0, op0=ALU.mult, op1=ALU.add, accum_out=out))
                signal("u_used")

            def dot_heads(g0, n):
                t = g0 // PH
                with st.loop(n, TOPK + 1) as g:
                    for j in range(TOPK):
                        dve.wait_ge(u_landed[j % 4], g * 64 + 16 * (g0 * 4 + j // 4 + 1))
                        dot(h2_rows[:, t, :], j % 4, act_a[:, 0, j:j + 1])
                    signal("a_in")
                    dve.wait_ge(s["a_out"], g + (g0 + 1))
                    dve.wait_ge(s["v_used"], g * TOPK + (g0 * TOPK + 4))
                    st(TT(wexp[:, 0, :], act_g[:, 0, :], gates[:, t, ds(g * TOPK + g0 % PH * TOPK, TOPK)], ALU.mult))
                    signal("w_ready")

            def add_output(t):
                n = TILES[t][1]
                y = x_rows[0:n, t, :].rearrange("p (a b) -> p a b", a=4)
                dve.wait_ge(s["yo_full"], t + 1)
                st(TT(y, ps[0:n, 4 * (t % 2):4 * (t % 2) + 4, :], y, ALU.add))
                signal("y_ready")

            for g in range(PH // 2):
                dot_heads(g, 1)
                for h in (2 * g, 2 * g + 1):
                    best16([half_best(2, 2 * h + c, c) for c in range(2)])
                    head_best((2,), h)
            shift_winners(2, 1)
            dot_heads(4, 1)
            experts(1)
            signal("idx_ready")
            dot_heads(5, 1)
            experts(2)
            softmax_gates(2, 1, 2)
            signal("sT_in")
            dot_heads(6, 2)
            dve.wait_ge(s["sT_full"], 1)
            st.run(CP(sidx, ps[:, 4, 0:TS]))
            st(CP(sgate, ps[:, 4, TS:2 * TS]))
            signal("idx_ready")
            dot_heads(8, 1)
            add_output(0)
            dot_heads(9, 7)
            for b in range(TS):
                dve.wait_ge(hb_landed[b % 2], 16 * (b // 2 + 1))
                dve.wait_ge(u_landed[b % 4], 16 * (64 + b // 4 + 1))
                dot(hb[b % 2], b % 4, act_a[:, 0, b:b + 1])
                signal("hb_used")
            signal("a_in")
            add_output(1)
            dve.wait_ge(s["a_out"], 2 * PH + 1)
            st(TT(wz.rearrange("p b c -> p (b c)")[:, 0:TS * TS:TS + 1], act_g[:, 0, 0:TS], sgate, ALU.mult))
            signal("w_ready")
            add_output(2)


_OUTS = [("y_prompt", (1, 256, 2048)), ("y_sample", (8, 1, 2048)), ("k_prompt", (1, 1, 256, 8, 128)),
         ("v_prompt", (1, 1, 256, 8, 128)), ("conv_prompt", (1, 1, 2, 1024)), ("mem_k_prompt", (1, 1, 256, 4, 256)),
         ("mem_v_prompt", (1, 1, 256, 4, 256)), ("k_sample", (1, 8, 1, 8, 128)), ("v_sample", (1, 8, 1, 8, 128)),
         ("conv_sample", (1, 8, 2, 1024))]


def rope_table():
    half = DK // 8
    freq = np.float32(500000.0) ** (-np.arange(half, dtype=np.float32) / np.float32(half))
    pos = np.concatenate([np.arange(TP), np.full(P, PAGES * PAGE)]).astype(np.float32)
    ang = pos[:, None] * freq[None, :]
    tab = np.concatenate([np.cos(ang), np.sin(ang)], axis=1).astype(np.float32)
    return np.ascontiguousarray(tab.reshape(3, P, 2 * half).transpose(1, 0, 2))


def kernel(**inputs):
    import concourse.bacc as bacc
    from concourse.bass_utils import run_bass_kernel_spmd

    nc = bacc.Bacc("TRN2", target_bir_lowering=False, num_devices=1)
    arrays, A, O = {}, {}, {}
    for name, a in list(inputs.items()) + [("rope_tab", rope_table())]:
        a = np.ascontiguousarray(a)
        arrays[f"in_{name}_dram"] = a
        A[name] = nc.dram_tensor(f"in_{name}_dram", a.shape, mybir.dt.from_np(a.dtype), kind="ExternalInput").ap()
    for name, shape in _OUTS:
        O[name] = nc.dram_tensor(f"out_{name}_dram", shape, F32, kind="ExternalOutput").ap()
    build(nc, A, O)
    r = run_bass_kernel_spmd(nc, [arrays], core_ids=[0])
    return tuple(r.results[0][f"out_{name}_dram"] for name, _ in _OUTS)
```
